# Optimizing a Trainium2 kernel written in Bass

```python
import jax, jax.numpy as jnp
from jax import lax
import numpy as np

D_MODEL = 1024
BATCH = 1
SEQ = 512
DEPTH = 2

GRID_W = 64
CTX_LEN = 256

NA_HEADS = 8
NA_HEAD_DIM = 64
NA_DIM = NA_HEADS * NA_HEAD_DIM
NA_WIN_H = 8
NA_WIN_W = 16

HG_HEADS = 4
HG_HEAD_DIM = 128
HG_DIM = HG_HEADS * HG_HEAD_DIM
HG_CHUNK = 64

EVEN_IN = 3 * NA_DIM + 5 * HG_DIM

CONV_WIDTH = 31

D_FF = -(-8 * D_MODEL // (3 * 256)) * 256

N_EVEN = (DEPTH + 1) // 2
N_ODD = DEPTH // 2
ALPHA = (2 * DEPTH) ** 0.25
BETA = (8 * DEPTH) ** -0.25
LN_EPS = 1e-5
RMS_EPS = 1e-6

kernel_name = 'hybrid_natten_hgrn2_conformer_dit'

def layer_norm(x, g, b):
    xf = x.astype(jnp.float32)
    mu = jnp.mean(xf, axis=-1, keepdims=True)
    var = jnp.mean(jnp.square(xf - mu), axis=-1, keepdims=True)
    y = (xf - mu) * lax.rsqrt(var + LN_EPS) * g.astype(jnp.float32) + b.astype(jnp.float32)
    return y.astype(x.dtype)

def modulate(x, shift, scale):
    return x * (1.0 + scale) + shift

def swiglu(h, w1, w3, w2):
    return (jax.nn.silu(h @ w1) * (h @ w3)) @ w2

def split_heads(a, heads):
    return a.reshape(a.shape[0], a.shape[1], heads, -1)

def context_attention(q, k, v):
    s = jnp.einsum('bqhd,bkhd->bhqk', q, k).astype(jnp.float32) * (q.shape[-1] ** -0.5)
    p = jax.nn.softmax(s, axis=-1).astype(v.dtype)
    o = jnp.einsum('bhqk,bkhd->bqhd', p, v)
    return o.reshape(o.shape[0], o.shape[1], -1)

def neighbourhood_attention(q, k, v, k_ctx, v_ctx, rpb):
    bsz, t, heads, hd = q.shape
    rows = t // GRID_W
    kr = min(NA_WIN_H, rows)
    scale = hd ** -0.5
    qg = q.reshape(bsz, rows, GRID_W, heads, hd)
    kg = k.reshape(bsz, rows, GRID_W, heads, hd)
    vg = v.reshape(bsz, rows, GRID_W, heads, hd)
    col = jnp.arange(GRID_W)
    col_start = jnp.clip(col - NA_WIN_W // 2, 0, GRID_W - NA_WIN_W)
    col_in = (col[None, :] >= col_start[:, None]) & (col[None, :] < col_start[:, None] + NA_WIN_W)
    dc_idx = jnp.clip(col[None, :] - col[:, None] + NA_WIN_W - 1, 0, 2 * NA_WIN_W - 2)
    row_start = jnp.clip(jnp.arange(rows) - kr // 2, 0, rows - kr)

    def row_block(r):
        rs = row_start[r]
        q_r = lax.dynamic_index_in_dim(qg, r, axis=1, keepdims=False)
        k_r = lax.dynamic_slice_in_dim(kg, rs, kr, axis=1)
        v_r = lax.dynamic_slice_in_dim(vg, rs, kr, axis=1)
        dr_idx = rs + jnp.arange(kr) - r + NA_WIN_H - 1
        bias = rpb[:, dr_idx[:, None, None], dc_idx[None, :, :]]
        bias = jnp.transpose(bias, (0, 2, 1, 3)).astype(jnp.float32)
        s_loc = jnp.einsum('bqhd,bikhd->bhqik', q_r, k_r).astype(jnp.float32) * scale + bias[None]
        s_loc = jnp.where(col_in[:, None, :], s_loc, -jnp.inf)
        s_ctx = jnp.einsum('bqhd,bchd->bhqc', q_r, k_ctx).astype(jnp.float32) * scale
        s = jnp.concatenate([s_loc.reshape(bsz, heads, GRID_W, kr * GRID_W), s_ctx], axis=-1)
        p = jax.nn.softmax(s, axis=-1).astype(v.dtype)
        p_loc = p[..., :kr * GRID_W].reshape(bsz, heads, GRID_W, kr, GRID_W)
        return (jnp.einsum('bhqik,bikhd->bqhd', p_loc, v_r)
                + jnp.einsum('bhqc,bchd->bqhd', p[..., kr * GRID_W:], v_ctx))

    o = lax.map(row_block, jnp.arange(rows))
    return jnp.transpose(o, (1, 0, 2, 3, 4)).reshape(bsz, t, heads * hd)

def hgrn2_gates(z, lb):
    z = z.astype(jnp.float32)
    key = (1.0 - lb) * jax.nn.sigmoid(-z)
    log_f = jnp.logaddexp(jnp.log(lb), jnp.log1p(-lb) + jax.nn.log_sigmoid(z))
    return key, log_f

def hgrn2_chunk_scan(q, k, v, log_f, s0):
    bsz, t, heads, dk = q.shape
    dv = v.shape[-1]
    n = t // HG_CHUNK

    def chunks(a):
        return jnp.transpose(a.reshape(bsz, n, HG_CHUNK, heads, a.shape[-1]), (1, 0, 3, 2, 4))

    causal = jnp.tril(jnp.ones((HG_CHUNK, HG_CHUNK), dtype=bool))

    def step(S, xs):
        qc, kc, vc, gc = xs
        b = jnp.cumsum(gc, axis=-2)
        diff = b[..., :, None, :] - b[..., None, :, :]
        decay = jnp.exp(jnp.where(causal[:, :, None], diff, -jnp.inf))
        a = jnp.einsum('bhtd,bhsd,bhtsd->bhts', qc, kc, decay)
        o = jnp.einsum('bhts,bhse->bhte', a, vc) + jnp.einsum('bhtd,bhde->bhte', qc * jnp.exp(b), S)
        b_last = b[..., -1:, :]
        S_new = (jnp.exp(b_last[..., 0, :])[..., None] * S
                 + jnp.einsum('bhsd,bhse->bhde', kc * jnp.exp(b_last - b), vc))
        return S_new, o

    s_final, o = lax.scan(step, s0, (chunks(q), chunks(k), chunks(v), chunks(log_f)))
    o = jnp.transpose(o, (1, 0, 3, 2, 4)).reshape(bsz, t, heads, dv)
    return o, s_final

def hgrn2_final_state(k, v, log_f):
    b = jnp.cumsum(log_f, axis=1)
    return jnp.einsum('bthd,bthe->bhde', k * jnp.exp(b[:, -1:] - b), v)

def hgrn2_direction(q, v, z, q_c, v_c, z_c, lb, reverse, need_ctx_out):
    flip = (lambda a: jnp.flip(a, axis=1)) if reverse else (lambda a: a)
    k_c, g_c = hgrn2_gates(z_c, lb)
    k, g = hgrn2_gates(z, lb)
    if need_ctx_out:
        s0 = jnp.zeros((q.shape[0], HG_HEADS, HG_HEAD_DIM, HG_HEAD_DIM), jnp.float32)
        o_c, s_c = hgrn2_chunk_scan(flip(q_c), flip(k_c), flip(v_c), flip(g_c), s0)
        o_c = flip(o_c)
    else:
        o_c = None
        s_c = hgrn2_final_state(flip(k_c), flip(v_c), flip(g_c))
    o, _ = hgrn2_chunk_scan(flip(q), flip(k), flip(v), flip(g), s_c)
    return flip(o), o_c

def hgrn2_readout(o, g, norm_g):
    o = o * lax.rsqrt(jnp.mean(jnp.square(o), axis=-1, keepdims=True) + RMS_EPS) * norm_g.astype(jnp.float32)
    o = o.reshape(g.shape) * jax.nn.silu(g.astype(jnp.float32))
    return o.astype(g.dtype)

def even_mixer(h, h_c, w_in, w_out, rpb, lb, norm_g, need_ctx_out):
    cuts = [NA_DIM, 2 * NA_DIM, 3 * NA_DIM, 3 * NA_DIM + HG_DIM, 3 * NA_DIM + 2 * HG_DIM,
            3 * NA_DIM + 3 * HG_DIM, 3 * NA_DIM + 4 * HG_DIM]
    qa, ka, va, qb, ib, zf, zb, gb = jnp.split(h @ w_in, cuts, axis=-1)
    qa_c, ka_c, va_c, qb_c, ib_c, zf_c, zb_c, gb_c = jnp.split(h_c @ w_in, cuts, axis=-1)
    na = lambda a: split_heads(a, NA_HEADS)
    hg = lambda a: split_heads(a, HG_HEADS).astype(jnp.float32)
    o_na = neighbourhood_attention(na(qa), na(ka), na(va), na(ka_c), na(va_c), rpb)
    o_f, oc_f = hgrn2_direction(hg(qb), hg(ib), hg(zf), hg(qb_c), hg(ib_c), hg(zf_c), lb[0], False, need_ctx_out)
    o_b, oc_b = hgrn2_direction(hg(qb), hg(ib), hg(zb), hg(qb_c), hg(ib_c), hg(zb_c), lb[1], True, need_ctx_out)
    o_hg = hgrn2_readout(o_f + o_b, gb, norm_g)
    y = jnp.concatenate([o_na, o_hg], axis=-1) @ w_out
    if not need_ctx_out:
        return y, None
    o_na_c = context_attention(na(qa_c), na(ka_c), na(va_c))
    o_hg_c = hgrn2_readout(oc_f + oc_b, gb_c, norm_g)
    y_c = jnp.concatenate([o_na_c, o_hg_c], axis=-1) @ w_out
    return y, y_c

def conv_module(h, w1, b1, w_dw, b_dw, ln_g, ln_b, w2, b2):
    u = h @ w1 + b1
    u = u[..., :D_MODEL] * jax.nn.sigmoid(u[..., D_MODEL:])
    u = lax.conv_general_dilated(u, w_dw[:, None, :], window_strides=(1,),
                                 padding=[(CONV_WIDTH // 2, CONV_WIDTH // 2)],
                                 dimension_numbers=('NWC', 'WIO', 'NWC'),
                                 feature_group_count=D_MODEL) + b_dw
    u = jax.nn.silu(layer_norm(u, ln_g, ln_b))
    return u @ w2 + b2

def setup_inputs(seed: int = 0) -> dict:
    key = jax.random.key(seed)
    ks = jax.random.split(key, 32)
    D = D_MODEL

    def nrm(k, shape, s):
        return jax.random.normal(k, shape, jnp.float32) * s

    return {
        'x': nrm(ks[0], (BATCH, SEQ, D), 1.0),
        'c': nrm(ks[1], (BATCH, D), 1.0),
        'ctx': nrm(ks[2], (BATCH, CTX_LEN, D), 1.0),
        'c_ctx': nrm(ks[3], (D,), 1.0),
        'w_mod': nrm(ks[4], (DEPTH, D, 6 * D), 0.5 * D ** -0.5),
        'b_mod': nrm(ks[5], (DEPTH, 6 * D), 0.01),
        'ln1_g': 1.0 + nrm(ks[6], (DEPTH, D), 0.1),
        'ln1_b': nrm(ks[7], (DEPTH, D), 0.01),
        'ln2_g': 1.0 + nrm(ks[8], (DEPTH, D), 0.1),
        'ln2_b': nrm(ks[9], (DEPTH, D), 0.01),
        'w_in_even': nrm(ks[10], (N_EVEN, D, EVEN_IN), D ** -0.5),
        'w_out_even': nrm(ks[11], (N_EVEN, NA_DIM + HG_DIM, D), BETA * (NA_DIM + HG_DIM) ** -0.5),
        'na_rpb': nrm(ks[12], (N_EVEN, NA_HEADS, 2 * NA_WIN_H - 1, 2 * NA_WIN_W - 1), 0.3),
        'hg_lb': nrm(ks[13], (2, N_EVEN, HG_HEADS, HG_HEAD_DIM), 1.0),
        'hg_norm_g': 1.0 + nrm(ks[14], (N_EVEN, HG_HEADS, HG_HEAD_DIM), 0.1),
        'cv_w1': nrm(ks[15], (N_ODD, D, 2 * D), D ** -0.5),
        'cv_b1': nrm(ks[16], (N_ODD, 2 * D), 0.01),
        'cv_wdw': nrm(ks[17], (N_ODD, CONV_WIDTH, D), CONV_WIDTH ** -0.5),
        'cv_bdw': nrm(ks[18], (N_ODD, D), 0.01),
        'cv_ln_g': 1.0 + nrm(ks[19], (N_ODD, D), 0.1),
        'cv_ln_b': nrm(ks[20], (N_ODD, D), 0.01),
        'cv_w2': nrm(ks[21], (N_ODD, D, D), BETA * D ** -0.5),
        'cv_b2': nrm(ks[22], (N_ODD, D), 0.01),
        'ffn_w1': nrm(ks[23], (DEPTH, D, D_FF), D ** -0.5),
        'ffn_w3': nrm(ks[24], (DEPTH, D, D_FF), D ** -0.5),
        'ffn_w2': nrm(ks[25], (DEPTH, D_FF, D), BETA * D_FF ** -0.5),
    }

def reference(x, c, ctx, c_ctx, w_mod, b_mod, ln1_g, ln1_b, ln2_g, ln2_b, w_in_even, w_out_even,
              na_rpb, hg_lb, hg_norm_g, cv_w1, cv_b1, cv_wdw, cv_bdw, cv_ln_g, cv_ln_b, cv_w2, cv_b2,
              ffn_w1, ffn_w3, ffn_w2):
    last_even = DEPTH - 1 if (DEPTH - 1) % 2 == 0 else DEPTH - 2
    p_lb = jax.nn.softmax(hg_lb.astype(jnp.float32), axis=1)
    hg_lower = jnp.maximum(jnp.cumsum(p_lb, axis=1) - p_lb[:, :1], 0.0)
    xc = ctx
    for l in range(DEPTH):
        ctx_used = l <= last_even
        ctx_out = l < last_even
        mod = jax.nn.silu(c) @ w_mod[l] + b_mod[l]
        sh1, sc1, g1, sh2, sc2, g2 = jnp.split(mod[:, None, :], 6, axis=-1)
        h = modulate(x, sh1, sc1)
        if ctx_used:
            mod_c = jax.nn.silu(c_ctx) @ w_mod[l] + b_mod[l]
            sh1c, sc1c, g1c, sh2c, sc2c, g2c = jnp.split(mod_c, 6, axis=-1)
            h_c = modulate(xc, sh1c, sc1c)
        j = l // 2
        if l % 2 == 0:
            y, y_c = even_mixer(h, h_c, w_in_even[j], w_out_even[j], na_rpb[j], hg_lower[:, j],
                                hg_norm_g[j], ctx_out)
        else:
            y = conv_module(h, cv_w1[j], cv_b1[j], cv_wdw[j], cv_bdw[j], cv_ln_g[j], cv_ln_b[j], cv_w2[j], cv_b2[j])
            if ctx_out:
                y_c = conv_module(h_c, cv_w1[j], cv_b1[j], cv_wdw[j], cv_bdw[j], cv_ln_g[j], cv_ln_b[j],
                                  cv_w2[j], cv_b2[j])
        x = layer_norm(ALPHA * x + g1 * y, ln1_g[l], ln1_b[l])
        x = layer_norm(ALPHA * x + g2 * swiglu(modulate(x, sh2, sc2), ffn_w1[l], ffn_w3[l], ffn_w2[l]),
                       ln2_g[l], ln2_b[l])
        if ctx_out:
            xc = layer_norm(ALPHA * xc + g1c * y_c, ln1_g[l], ln1_b[l])
            xc = layer_norm(ALPHA * xc + g2c * swiglu(modulate(xc, sh2c, sc2c), ffn_w1[l], ffn_w3[l], ffn_w2[l]),
                            ln2_g[l], ln2_b[l])
    return x


_drawn_inputs = setup_inputs


def setup_inputs(seed=0):
    import zlib

    import numpy as np

    out = dict(_drawn_inputs(seed))
    spreads = {}
    factors = {'ctx': 8.0,
     'c_ctx': 3.86,
     'b_mod': 8.0,
     'ln1_b': 4.181,
     'ln2_b': 3.841,
     'na_rpb': 64.0,
     'hg_norm_g': 8.0,
     'cv_b1': 8.0,
     'cv_bdw': 8.0,
     'cv_ln_g': 7.587,
     'cv_ln_b': 64.0,
     'cv_b2': 28.622}
    for name, (base, spread) in spreads.items():
        noise = np.random.default_rng([zlib.crc32(name.encode()), seed]).standard_normal(out[name].shape)
        drawn = base * np.exp(spread * noise) if base else spread * noise
        out[name] = __import__('jax').numpy.asarray(drawn.astype(out[name].dtype))
    for name, factor in factors.items():
        out[name] = (out[name] * factor).astype(out[name].dtype)
    return out
```

```python
import concourse.bass as bass
from concourse import mybir
from contextlib import ExitStack

P = 128
D = 1024
KC = D // P
T = 512
TC = 256
ROWS, COLS = 8, 64
NH, HD = 8, 64
HH = 4
CH = 128
NCH = T // CH
TILE_W = 16
NT = COLS // TILE_W
WIN = 3 * TILE_W
DFF = 2816
FC = DFF // P
TAPS = 31
PAD = TAPS // 2
ALPHA = (2 * 2) ** 0.25
LN_EPS, RMS_EPS = 1e-5, 1e-6
LEVELS = [64, 32, 16, 8, 4, 2, 1]

N_IN, N_OUT, N_UP0, N_DN0, N_CV1, N_CV2, N_UP1, N_DN1 = 0, 32, 40, 84, 108, 124, 132, 176
N_END = 200
DN_KC = (8, 7, 7)
IB, ZF, ZB, KA, VA, QB, QA, GB = range(8)
IN_ORDER = (4, 5, 6, 1, 2, 3, 0, 7)

VEC = {}
_at = 0
for _name, _n in (("b_mod", 96), ("ln1_g", 16), ("ln1_b", 16), ("ln2_g", 16), ("ln2_b", 16), ("hg_norm_g", 4),
                  ("cv_b1", 16), ("cv_bdw", 8), ("cv_ln_g", 8), ("cv_ln_b", 8), ("cv_b2", 8), ("cv_wdw", 8 * TAPS)):
    VEC[_name] = _at
    _at += _n
NVEC = _at

SH1, SC1, G1, SH2, SC2, G2 = range(6)


def build(nc, xT, ctxT, cvec, vecs, ident_d, lvl_d, bias_d, mask_d, wmod, w_in, w_out, w_up, w_dn, cv1, cv2, out):
    fp32, f32r, u8 = mybir.dt.float32, mybir.dt.float32r, mybir.dt.uint8
    ACT, ALU, AX = mybir.ActivationFunctionType, mybir.AluOpType, mybir.AxisListType

    stack = ExitStack()
    with stack:
        BASE = 16512
        CONST, RING = BASE, BASE + 8192
        H0 = RING + 32768
        REST = H0 + 49152
        TMP = REST + 94336

        def at(name, shape, offset, dt=fp32):
            return nc.alloc_sbuf_tensor_at(name, [P] + shape, dt, offset=offset)

        const_at = [CONST]

        def const(name, shape, dt=fp32):
            size = 1
            for s in shape:
                size *= s
            t = at(name, shape, const_at[0], dt)
            const_at[0] += -(-size * (1 if dt == u8 else 4) // 32) * 32
            assert const_at[0] <= RING
            return t

        vec = const("vec", [NVEC])
        ident = const("ident", [P])
        ones = const("ones", [P])
        lvl = const("lvl", [2, 7, P], u8)
        cin = const("cin", [KC, 2])
        cact = const("cact", [KC, 2])
        mod = const("mod", [2, 48, 2])
        modp = const("modp", [2, 48, 2])
        norm = const("norm", [5, 5, 8])
        neg_half = const("neg_half", [4])
        mxc = const("mxc", [2, 4])
        sml = const("sml", [2, 2])
        rsum = const("rsum", [2, 8])
        rinv = const("rinv", [2, 8])
        gam = const("gam", [2, 4])
        msq = const("msq", [3, 4])

        raw = at("raw", [4, KC * P], RING)
        whi = at("whi", [2, KC * P], RING + 16384, f32r)
        wlo = at("wlo", [2, KC * P], RING + 24576, f32r)
        h_hi = at("h_hi", [KC, T], H0, f32r)
        h_lo = at("h_lo", [KC, T], H0 + 16384, f32r)
        hc_hi = at("hc_hi", [KC, TC], H0 + 32768, f32r)
        hc_lo = at("hc_lo", [KC, TC], H0 + 40960, f32r)
        modraw0 = at("modraw0", [4, KC * P], REST)
        KEY = at("KEY", [8, T], REST + 16384)
        PRE = at("PRE", [8, NCH, CH + 1], REST + 32768)
        QBt = at("QBt", [HH, T], REST + 49280)
        VI = at("VI", [NCH, 512], REST + 57472)
        VIC = at("VIC", [2, 512], REST + 65664)
        VAt = at("VAt", [NT, 512], REST + 69760)
        VAC = at("VAC", [2, 512], REST + 77952)
        KT_ = at("KT_", [4, T], REST + 82048)
        KTC = at("KTC", [4, TC], REST + 90240)
        xin = at("xin", [KC, T], REST + 69760)
        cxin = at("cxin", [KC, TC], REST + 86144)
        Qt = at("Qt", [4, T], H0 + 32768)
        GBt = at("GBt", [4, T], H0 + 40960)
        S0 = at("S0", [8, P], TMP)
        t1_ = TMP + 4096
        lvl_f = at("lvl_f", [2, 7, P], t1_)
        VT = at("VT", [T + TC], t1_)
        ab = at("ab", [T + TC], t1_ + 3072)
        lb_ = at("lb_", [T + TC], t1_ + 6144)
        ls = at("ls", [T + TC], t1_ + 9216)
        keyc = at("keyc", [TC], t1_ + 12288)
        prec = at("prec", [TC + 1], t1_ + 13312)
        Ec = at("Ec", [TC], t1_ + 14368)
        Kdc = at("Kdc", [TC], t1_ + 15392)
        KcT = at("KcT", [2, P], t1_ + 16416)
        bias = at("bias", [NH, ROWS, WIN], REST)
        mask0 = at("mask0", [ROWS, 2 * TILE_W], REST + 12288)
        mask1 = at("mask1", [ROWS, WIN], REST + 13312)
        mask3 = at("mask3", [ROWS, 2 * TILE_W], REST + 14848)
        EX = at("EX", [4, NCH, CH], H0)
        QD = at("QD", [2, NCH, CH], H0 + 8192)
        AT = at("AT", [2, NCH, CH], H0 + 12288)
        OT = at("OT", [8, T], H0 + 16384)
        St = at("St", [2, 3, P], REST + 65664)
        comb = at("comb", [2, ROWS * WIN], t1_)
        Ssb = at("Ssb", [2, ROWS * WIN], t1_ + 3072)
        Pb = at("Pb", [2, 5 * P], t1_ + 6144)
        PTb = at("PTb", [2, 5 * P], t1_ + 11264)
        Osb = at("Osb", [NH, HD], t1_ + 16384)
        KD = at("KD", [NCH, CH], t1_ + 18432)
        KDT = at("KDT", [3, P], t1_ + 20480)
        ON = at("ON", [NCH, CH], t1_ + 22016)
        XA = at("XA", [8, T], REST)
        modraw1 = at("modraw1", [4, KC * P], H0 + 32768)
        A_hi = at("A_hi", [FC, T], REST + 16384, f32r)
        A_lo = at("A_lo", [FC, T], REST + 16384 + 45056, f32r)
        U = at("U", [2, T + 2 * PAD], REST + 16384)
        RC = at("RC", [8, T], REST + 16384 + 8192)
        tb = at("tb", [4, T], REST + 106496)
        acc = at("acc", [2, T], REST + 114688)

        bank = [stack.enter_context(nc.psum_tensor(f"bank{i}", [P, 512], fp32)) for i in range(8)]

        def sem(name):
            return stack.enter_context(nc.semaphore(name))

        table_in, lvl_done = sem("table_in"), sem("lvl_done")
        raw_in = [sem(f"raw_in{i}") for i in range(4)]
        mod_in = [sem(f"mod_in{i}") for i in range(4)]
        (hi_done, lo_done, gemm_done, mod_done, const_in, x_in, bias_in, xa_in, out_done, ones_set, cact_done,
         modv_done, mchain, hx_done, hhi_done, hlo_done) = [sem(n) for n in (
             "hi_done", "lo_done", "gemm_done", "mod_done", "const_in", "x_in", "bias_in", "xa_in", "out_done",
             "ones_set", "cact_done", "modv_done", "mchain", "hx_done", "hhi_done", "hlo_done")]
        (evac_act, evac_dve, vt_tr, vx_done, vc_done, z_abs, z_exp, z_ln, z_ls, z_d, z_key, z_pre, z_ec, z_kd,
         z_tr, z_kt, z_mm, z_s0) = [sem(n) for n in (
             "evac_act", "evac_dve", "vt_tr", "vx_done", "vc_done", "z_abs", "z_exp", "z_ln", "z_ls", "z_d",
             "z_key", "z_pre", "z_ec", "z_kd", "z_tr", "z_kt", "z_mm", "z_s0")]
        (n_comb, n_s, n_mc, n_mx, n_neg, n_exp, n_sum, n_tr, n_ptl, n_ptc, n_pv, n_inv, n_osb, n_otr, n_ot) = [
            sem(n) for n in ("n_comb", "n_s", "n_mc", "n_mx", "n_neg", "n_exp", "n_sum", "n_tr", "n_ptl", "n_ptc",
                             "n_pv", "n_inv", "n_osb", "n_otr", "n_ot")]
        (g_sub, g_exp, g_x, g_mm, g_at, g_e2, g_kd, g_ktr, g_kdt, g_ds, g_st, g_o, g_qd, g_gam, g_sq, g_ms, g_mse, g_pow, g_on,
         g_onr, g_ot) = [sem(n) for n in ("g_sub", "g_exp", "g_x", "g_mm", "g_at", "g_e2", "g_kd", "g_ktr",
                                          "g_kdt", "g_ds", "g_st", "g_o", "g_qd", "g_gam", "g_sq", "g_ms", "g_mse", "g_pow", "g_on",
                                          "g_onr", "g_ot")]
        (xa_done, oh_hi, oh_lo) = [sem(n) for n in ("xa_done", "oh_hi", "oh_lo")]
        (r_done, sq_done, rs_done, qs_done, acc_zero, st_mm, ln_vec, ln_mu, ln_m2, ln_var, ln_v, ln_l, ln_rstd,
         ln_nmr, ln_t1, ln_t2, ln_h, ln_hi, ln_lo, ln_x) = [sem(n) for n in (
             "r_done", "sq_done", "rs_done", "qs_done", "acc_zero", "st_mm", "ln_vec", "ln_mu", "ln_m2", "ln_var",
             "ln_v", "ln_l", "ln_rstd", "ln_nmr", "ln_t1", "ln_t2", "ln_h", "ln_hi", "ln_lo", "ln_x")]
        (up_s, up_a, up_hi, up_lo, cv_s, cv_u, cv_tap, cv_pad) = [sem(n) for n in (
            "up_s", "up_a", "up_hi", "up_lo", "cv_s", "cv_u", "cv_tap", "cv_pad")]

        block = stack.enter_context(nc.Block())

        def load_piece(eng, g, j, src, cols, first=False):
            if not first:
                eng.wait_ge(lo_done, 4 * g + j - 3)
            eng.dma_start(raw[:, j, 0:cols], src).then_inc(raw_in[j], 16)

        def split_hi(eng, g, j, first=False):
            if j >= 4:
                g, j = g + 1, j - 4
            eng.wait_ge(raw_in[j], 16 * (g + 1))
            if not first:
                eng.wait_ge(gemm_done, 4 * g + j - 1)
            nc.scalar.activation(whi[:, j % 2], raw[:, j], ACT.Copy).then_inc(hi_done, 1)

        def split_lo(eng, g, j):
            if j >= 4:
                g, j = g + 1, j - 4
            eng.wait_ge(hi_done, 4 * g + j + 1)
            nc.gpsimd.tensor_tensor(wlo[:, j % 2], raw[:, j], whi[:, j % 2].bitcast(fp32),
                                    ALU.subtract).then_inc(lo_done, 1)

        def gemm(dst, j, rhs_hi, rhs_lo, cols, kcs, first=True, last=True):
            n = len(kcs)
            for i, kc in enumerate(kcs):
                w_h, w_l = (w[:, j % 2, i * P:(i + 1) * P] for w in (whi, wlo))
                nc.tensor.matmul(dst, w_h, rhs_hi[:, kc, 0:cols], start=(first and i == 0), stop=False)
                nc.tensor.matmul(dst, w_h, rhs_lo[:, kc, 0:cols], start=False, stop=False)
                mm = nc.tensor.matmul(dst, w_l, rhs_hi[:, kc, 0:cols], start=False, stop=(last and i == n - 1))
            return mm

        def mod_tile(pe, layer, q, g, j, col):
            ring = modraw1 if layer else modraw0
            pe.wait_ge(mod_in[j], 16 * (g + 1))
            for kc in range(KC):
                mm = nc.tensor.matmul(bank[7][:, bass.ds(col, 2)] if not isinstance(col, int) else bank[7][:, col:col + 2],
                                      ring[:, j, kc * P:(kc + 1) * P], cact[:, kc, :],
                                      start=(kc == 0), stop=(kc == KC - 1))
            mm.then_inc(mod_done, 1)

        def load_mod(sp, g, j, layer, first=False):
            if not first:
                sp.wait_ge(mod_done, 4 * g + j - 3)
            sp.dma_start((modraw1 if layer else modraw0)[:, j], wmod[4 * g + j]).then_inc(mod_in[j], 16)

        N_CTX = 20
        v_tile = [0, 1, 2, 3, 16, 17, 18, 19]

        def dve_read(eng, n):
            if 4 <= n < 12:
                eng.wait_ge(z_d, n - 3)
            elif n < N_CTX:
                eng.wait_ge(evac_dve, n + 1 if n < 4 else n - 7)

        UNITS = [(t, h) for t in range(NT) for h in range(NH)]
        KIND_MASK = [mask0, mask1, mask1, mask3]

        def window(t):
            lo = max(t - 1, 0)
            return lo, min(t + 2, NT) - lo

        NITEM = 8 * 8
        NSLOT = NITEM + 16

        def hg(s):
            u, e = divmod(s, 8)
            head, d = divmod(u, 2)
            return u, e, d, head, d * HH + head

        def halves(e):
            H = LEVELS[e - 1]
            return CH // (2 * H), H

        def prefix(i, d):
            return PRE[:, i, :, 1:CH + 1] if d == 0 else PRE[:, i, :, 0:CH]

        @block.sync
        def _(sp):
            sp.dma_start(cin[:], cvec).then_inc(const_in, 16)
            sp.dma_start(vec[:], vecs).then_inc(const_in, 16)
            for q in range(4):
                load_mod(sp, q // 4, q % 4, 0, first=True)
            sp.dma_start(ident[:], ident_d).then_inc(table_in, 16)
            sp.dma_start(lvl_f[:], lvl_d).then_inc(table_in, 16)
            for q in range(4, 16):
                load_mod(sp, q // 4, q % 4, 0)
            sp.dma_start(xin[:], xT).then_inc(x_in, 16)
            sp.dma_start(cxin[:], ctxT).then_inc(x_in, 16)
            for n in range(32):
                load_mod(sp, (16 + n) // 4, (16 + n) % 4, 0)
                load_piece(sp, n // 4, n % 4, w_in[n], KC * P, first=n < 4)
            for n in range(4):
                load_piece(sp, N_OUT // 4, n, w_out[n], KC * P)
            sp.wait_ge(mod_done, 48)
            sp.dma_start(bias[:], bias_d).then_inc(bias_in, 16)
            sp.dma_start(mask0[:], mask_d[:, :, 0, 0:2 * TILE_W]).then_inc(bias_in, 16)
            sp.dma_start(mask1[:], mask_d[:, :, 1, :]).then_inc(bias_in, 16)
            sp.dma_start(mask3[:], mask_d[:, :, 2, 0:2 * TILE_W]).then_inc(bias_in, 16)
            sp.wait_ge(n_comb, len(UNITS))
            sp.dma_start(XA[:], xT).then_inc(xa_in, 16)
            for n in range(4, 8):
                load_piece(sp, N_OUT // 4 + 1, n % 4, w_out[n], KC * P)
            sp.wait_ge(oh_lo, 8)
            for q in range(48, 52):
                load_mod(sp, q // 4, q % 4, 1)

            def up(layer):
                with sp.Fori(0, 11) as it:
                    for j in range(4):
                        if layer == 0:
                            load_mod(sp, it + 13, j, 1)
                        load_piece(sp, it + (N_UP1 if layer else N_UP0) // 4, j, w_up[layer, 4 * it + j], KC * P)

            def down(layer):
                with sp.Fori(0, 2) as it:
                    for j in range(12):
                        k0 = sum(DN_KC[:j % 3]) * P
                        cols = DN_KC[j % 3] * P
                        load_piece(sp, 3 * it + (N_DN1 if layer else N_DN0) // 4 + j // 4, j % 4,
                                   w_dn[layer, 4 * it + j // 3, :, k0:k0 + cols], cols)

            up(0)
            down(0)
            with sp.Fori(0, 4) as it:
                for j in range(4):
                    load_piece(sp, it + N_CV1 // 4, j, cv1[4 * it + j], KC * P)
            with sp.Fori(0, 2) as it:
                for j in range(4):
                    load_piece(sp, it + N_CV2 // 4, j, cv2[4 * it + j], KC * P)
            up(1)
            down(1)
            for j in range(8):
                sp.wait_ge(ln_x, 24 + j + 1)
                sp.dma_start(out[j], XA[:, j]).then_inc(out_done, 16)
            sp.wait_ge(out_done, 16 * 8)

        @block.gpsimd
        def _(pool):
            nc.gpsimd.memset(ones[:], 1.0).then_inc(ones_set, 1)
            pool.wait_ge(table_in, 32)
            nc.gpsimd.tensor_copy(lvl[:], lvl_f[:]).then_inc(lvl_done, 1)
            for n in range(2):
                split_lo(pool, 0, n)
            for n in range(32):
                split_lo(pool, (n + 2) // 4, (n + 2) % 4)
            pool.wait_ge(gemm_done, 32)
            pool.wait_ge(bias_in, 64)
            for s in range(NSLOT):
                if s % 2 == 0 and s // 2 < len(UNITS):
                    w = s // 2
                    t, h = UNITS[w]
                    _, nl = window(t)
                    off = TILE_W if t == 0 else 0
                    if w >= 2:
                        pool.wait_ge(n_mx, w - 1)
                    dst = comb[:, w % 2, 0:ROWS * nl * TILE_W].rearrange("p (r c) -> p r c", r=ROWS)
                    nc.gpsimd.tensor_tensor(dst, bias[:, h, :, off:off + nl * TILE_W], KIND_MASK[t][:],
                                            ALU.add).then_inc(n_comb, 1)
                k = s - 2
                if 0 <= k < NITEM:
                    u, e, d, head, i = hg(k)
                    pool.wait_ge(g_exp, k + 1)
                    if e == 0:
                        b = EX[:, k % 4]
                        q_ = QBt[:, head].rearrange("p (c t) -> p c t", c=NCH)
                        k_ = KEY[:, i].rearrange("p (c t) -> p c t", c=NCH)
                        if u >= 1:
                            pool.wait_ge(g_ktr, u)
                        if d == 0:
                            nc.gpsimd.tensor_tensor(KD[:], b, k_, ALU.mult).then_inc(g_kd, 1)
                        else:
                            if head >= 1:
                                pool.wait_ge(g_o, head)
                            pool.wait_ge(g_e2, u + 1)
                            nc.gpsimd.tensor_tensor(QD[:, 1], b, q_, ALU.mult).then_inc(g_qd, 1)
                            nc.gpsimd.tensor_tensor(KD[:], KD[:], k_, ALU.mult).then_inc(g_kd, 1)
                    else:
                        nb, H = halves(e)
                        b = EX[:, k % 4].rearrange("p c t -> p (c t)").rearrange("p (b two h) -> p b two h", two=2, h=H)
                        q_ = QBt[:, head].rearrange("p (b two h) -> p b two h", two=2, h=H)
                        k_ = KEY[:, i].rearrange("p (b two h) -> p b two h", two=2, h=H)
                        first, second = (k_, q_) if d == 0 else (q_, k_)
                        nc.gpsimd.tensor_tensor(b[:, :, 0], b[:, :, 0], first[:, :, 0], ALU.mult)
                        nc.gpsimd.tensor_tensor(b[:, :, 1], b[:, :, 1], second[:, :, 1], ALU.mult).then_inc(g_x, 1)
                k = s - 6
                if 0 <= k < NITEM and k % 16 == 0:
                    u, e, d, head, i = hg(k)
                    pool.wait_ge(g_e2, u + 1)
                    q_ = QBt[:, head].rearrange("p (c t) -> p c t", c=NCH)
                    nc.gpsimd.tensor_tensor(QD[:, 0], QD[:, 0], q_, ALU.mult).then_inc(g_qd, 1)
                k = s - 8
                if k >= 0 and k % 16 == 15 and k < NITEM:
                    hd_ = k // 16
                    pool.wait_ge(g_mse, hd_ + 1)
                    nc.gpsimd.tensor_tensor(msq[:, 2], msq[:, 1], neg_half[:], ALU.pow).then_inc(g_pow, 1)

            pool.wait_ge(xa_in, 16)
            nc.gpsimd.tensor_scalar(XA[:], XA[:], ALPHA, None, ALU.mult).then_inc(xa_done, 1)

            def ln_shift(k, src):
                for j in range(8):
                    pool.wait_ge(ln_t1, 8 * k + j + 1)
                    nc.gpsimd.tensor_tensor(src[:, j], src[:, j], acc[:, 0], ALU.add).then_inc(ln_t2, 1)

            def sum_sq(k, count):
                pool.wait_ge(sq_done, count + 1)
                pool.wait_ge(qs_done, count)
                pool.wait_ge(acc_zero, k + 1)
                nc.gpsimd.tensor_tensor(acc[:, 1], acc[:, 1], tb[:, 0], ALU.add).then_inc(qs_done, 1)

            for n in range(8):
                split_lo(pool, N_OUT // 4 + n // 4, n % 4 + 2)
                sum_sq(0, n)
            ln_shift(0, XA)

            def up(layer):
                with pool.Fori(0, 11) as it:
                    for j in range(4):
                        split_lo(pool, it + (N_UP1 if layer else N_UP0) // 4, j + 2)

            def down_body(layer, it, last=False):
                for j in range(12):
                    if not (last and j >= 10):
                        split_lo(pool, 3 * it + (N_DN1 if layer else N_DN0) // 4 + j // 4, j % 4 + 2)
                    if j % 3 == 2:
                        sum_sq(4 if layer else 1, 4 * it + j // 3 + (32 if layer else 8))

            up(0)
            with pool.Fori(0, 2) as it:
                down_body(0, it)
            ln_shift(1, XA)

            def cv1_body(it):
                for j in range(4):
                    split_lo(pool, it + N_CV1 // 4, j + 2)
                    if j % 2 and not (isinstance(it, int) and j == 1):
                        sum_sq(2, 2 * it + j // 2 + 15)

            cv1_body(0)
            with pool.Fori(1, 4) as it:
                cv1_body(it)
            sum_sq(2, 23)
            ln_shift(2, RC)
            with pool.Fori(0, 2) as it:
                for j in range(4):
                    split_lo(pool, it + N_CV2 // 4, j + 2)
                    sum_sq(3, 4 * it + j + 24)
            ln_shift(3, XA)
            up(1)
            down_body(1, 0)
            down_body(1, 1, last=True)
            ln_shift(4, XA)

        @block.tensor
        def _(pe):
            pe.wait_ge(cact_done, 1)
            for q in range(16):
                mod_tile(pe, 0, q, q // 4, q % 4, 2 * q)
            pe.wait_ge(table_in, 32)
            pe.wait_ge(hlo_done, 16)

            def v_transposes(v):
                pe.wait_ge(evac_act, v_tile[v] + 1)
                dve_read(pe, v_tile[v])
                if v >= 1:
                    pe.wait_ge(vx_done, v)
                    pe.wait_ge(vc_done, v)
                for c in range(4):
                    nc.tensor.transpose(bank[4][:, c * P:(c + 1) * P], VT[:, c * P:(c + 1) * P], ident[:])
                for c in range(2):
                    mm = nc.tensor.transpose(bank[5][:, c * P:(c + 1) * P], VT[:, T + c * P:T + (c + 1) * P], ident[:])
                mm.then_inc(vt_tr, 1)

            def z_tail(i):
                pe.wait_ge(z_kd, i + 1)
                if i >= 1:
                    pe.wait_ge(z_s0, i)
                for c in range(2):
                    mm = nc.tensor.transpose(bank[6][:, c * P:(c + 1) * P], Kdc[:, c * P:(c + 1) * P], ident[:])
                mm.then_inc(z_tr, 1)
                pe.wait_ge(z_kt, i + 1)
                pe.wait_ge(vc_done, 4)
                head = i % HH
                for c in range(2):
                    mm = nc.tensor.matmul(bank[6][:, 256:384], KcT[:, c], VIC[:, c, head * P:(head + 1) * P],
                                          start=(c == 0), stop=(c == 1))
                mm.then_inc(z_mm, 1)

            for n in range(32):
                kind = n // 4
                mod_tile(pe, 0, 16 + n, (16 + n) // 4, n % 4, 2 * (16 + n))
                pe.wait_ge(lo_done, n + 1)
                if n >= 2:
                    pe.wait_ge(evac_act, n - 1)
                    dve_read(pe, n - 2)
                mm = gemm(bank[n % 2][:], n, h_hi, h_lo, T, range(KC))
                if kind <= VA:
                    mm = gemm(bank[2 + n % 2][:, 0:TC], n, hc_hi, hc_lo, TC, range(KC))
                mm.then_inc(gemm_done, 1)
                if n - 1 in v_tile:
                    v_transposes(v_tile.index(n - 1))
                if 5 <= n <= 12:
                    z_tail(n - 5)

            pe.wait_ge(evac_act, 32)
            pe.wait_ge(vx_done, 8)
            pe.wait_ge(vc_done, 8)
            pe.wait_ge(z_s0, 8)
            pe.wait_ge(modv_done, 2)
            B_SL, B_SC, B_PL, B_PC, B_O, B_HA, B_HO, B_HT = bank
            for s in range(NSLOT):
                if s >= 21 and (s - 21) % 16 == 0 and (s - 21) // 16 < NT:
                    t = (s - 21) // 16
                    pe.wait_ge(n_osb, t + 1)
                    pe.wait_ge(n_ptl, min(8 * t + 9, len(UNITS)))
                    for g in range(4):
                        mm = nc.tensor.transpose(B_PL[:, g * P:(g + 1) * P],
                                                 Osb[:, 2 * g:2 * g + 2].rearrange("p a b -> p (a b)"), ident[:])
                    mm.then_inc(n_otr, 1)
                k = s - 5
                if 0 <= k < NITEM and k % 16 == 15:
                    hd_ = k // 16
                    pe.wait_ge(g_at, k + 1)
                    pe.wait_ge(g_st, 3 * 2 * (hd_ + 1))
                    pe.wait_ge(g_qd, 2 * (hd_ + 1))
                    if hd_ >= 1:
                        pe.wait_ge(g_on, hd_)
                    for c in range(NCH):
                        v_ = VI[:, c, hd_ * P:(hd_ + 1) * P]
                        dst = B_HO[:, c * P:(c + 1) * P]
                        nc.tensor.matmul(dst, AT[:, 0, c], v_, start=True, stop=False)
                        nc.tensor.matmul(dst, AT[:, 1, c], v_, start=False, stop=False)
                        sf = S0[:, hd_] if c == 0 else St[:, 0, c - 1]
                        sb_ = S0[:, HH + hd_] if c == 3 else St[:, 1, 2 - c]
                        nc.tensor.matmul(dst, QD[:, 0, c], sf, start=False, stop=False)
                        mm = nc.tensor.matmul(dst, QD[:, 1, c], sb_, start=False, stop=True)
                    mm.then_inc(g_o, 1)
                if s % 2 == 0 and s // 2 < len(UNITS):
                    w = s // 2
                    t, h = UNITS[w]
                    lo, nl = window(t)
                    part = slice(HD * (h % 2), HD * (h % 2) + HD)
                    if w >= 1:
                        pe.wait_ge(n_mx, w)
                        pe.wait_ge(n_exp, w)
                    q_ = Qt[part, h // 2, t * P:(t + 1) * P]
                    k_ = KT_[part, h // 2].rearrange("p (r c) -> p r c", r=ROWS)[:, :, lo * TILE_W:(lo + nl) * TILE_W]
                    nc.tensor.matmul(B_SL[:, 0:ROWS * nl * TILE_W].rearrange("p (r c) -> p r c", r=ROWS), q_, k_,
                                     start=True, stop=True)
                    nc.tensor.matmul(B_SC[:, 0:TC], q_, KTC[part, h // 2], start=True, stop=True).then_inc(n_s, 1)
                if (s - 3) % 2 == 0 and 0 <= (s - 3) // 2 < len(UNITS):
                    w = (s - 3) // 2
                    _, nl = window(UNITS[w][0])
                    pe.wait_ge(n_exp, w + 1)
                    if w >= 1:
                        pe.wait_ge(n_ptl, w)
                        pe.wait_ge(n_ptc, w)
                    if w >= 9:
                        pe.wait_ge(n_ot, (w - 1) // 8)
                    for c in range(nl):
                        nc.tensor.transpose(B_PL[:, c * P:(c + 1) * P], Pb[:, w % 2, c * P:(c + 1) * P], ident[:])
                    for c in range(2):
                        mm = nc.tensor.transpose(B_PC[:, c * P:(c + 1) * P],
                                                 Pb[:, w % 2, (3 + c) * P:(4 + c) * P], ident[:])
                    mm.then_inc(n_tr, 1)
                if (s - 5) % 2 == 0 and 0 <= (s - 5) // 2 < len(UNITS):
                    w = (s - 5) // 2
                    t, h = UNITS[w]
                    lo, nl = window(t)
                    pe.wait_ge(n_ptl, w + 1)
                    pe.wait_ge(n_ptc, w + 1)
                    if h == 0 and t >= 1:
                        pe.wait_ge(n_osb, t)
                    dst = B_O[:, h * HD:(h + 1) * HD]
                    for c in range(nl):
                        nc.tensor.matmul(dst, PTb[:, w % 2, c * P:(c + 1) * P], VAt[:, lo + c, h * HD:(h + 1) * HD],
                                         start=(c == 0), stop=False)
                    for c in range(2):
                        mm = nc.tensor.matmul(dst, PTb[:, w % 2, (3 + c) * P:(4 + c) * P],
                                              VAC[:, c, h * HD:(h + 1) * HD], start=False, stop=(c == 1))
                    mm.then_inc(n_pv, 1)
                k = s - 3
                if 0 <= k < NITEM:
                    u, e, d, head, i = hg(k)
                    if k >= 1:
                        pe.wait_ge(g_at, k)
                    if e == 0:
                        for c in range(NCH):
                            mm = nc.tensor.matmul(B_HA[:, c * P:(c + 1) * P], KEY[:, i, c * P:(c + 1) * P],
                                                  QBt[:, head, c * P:(c + 1) * P], start=True, stop=True)
                        mm.then_inc(g_mm, 1)
                        pe.wait_ge(g_kd, u + 1)
                        if u >= 1:
                            pe.wait_ge(g_st, 3 * u)
                        if u >= 3:
                            pe.wait_ge(g_ot, (u - 1) // 2)
                        for c in range(3):
                            cc = c if d == 0 else 3 - c
                            mm = nc.tensor.transpose(B_HT[:, c * P:(c + 1) * P], KD[:, cc], ident[:])
                        mm.then_inc(g_ktr, 1)
                    else:
                        pe.wait_ge(g_x, k - u)
                        for c in range(NCH):
                            x_ = EX[:, k % 4, c]
                            mm = nc.tensor.matmul(B_HA[:, c * P:(c + 1) * P], x_, x_, start=True, stop=True)
                        mm.then_inc(g_mm, 1)
                k = s - 5
                if 0 <= k < NITEM and k % 8 == 0:
                    u, e, d, head, i = hg(k)
                    pe.wait_ge(g_kdt, u + 1)
                    for c in range(3):
                        cc = c if d == 0 else 3 - c
                        mm = nc.tensor.matmul(B_HT[:, c * P:(c + 1) * P], KDT[:, c], VI[:, cc, head * P:(head + 1) * P],
                                              start=True, stop=True)
                    mm.then_inc(g_ds, 1)
                k = s - 10
                if 0 <= k < NITEM and k % 16 == 15:
                    hd_ = k // 16
                    pe.wait_ge(g_on, hd_ + 1)
                    u_now = min(2 * (hd_ + 1) + 1, 8)
                    pe.wait_ge(g_st, 3 * u_now)
                    for c in range(NCH):
                        mm = nc.tensor.transpose(B_HT[:, c * P:(c + 1) * P], ON[:, c], ident[:])
                    mm.then_inc(g_onr, 1)

            def res_bank(m):
                return bank[m % 2]

            pe.wait_ge(oh_lo, 8)
            for m in range(8):
                pe.wait_ge(lo_done, N_OUT + m + 1)
                if m >= 2:
                    pe.wait_ge(r_done, m - 1)
                gemm(res_bank(m)[:], m, h_hi, h_lo, T, range(KC)).then_inc(gemm_done, 1)

            def stats(k, extra=None):
                if extra:
                    extra()
                pe.wait_ge(rs_done, 8 * (k + 1))
                pe.wait_ge(qs_done, 8 * (k + 1))
                nc.tensor.matmul(bank[5][:], ones[:], acc[:, 0], start=True, stop=True)
                nc.tensor.matmul(bank[6][:], ones[:], acc[:, 1], start=True, stop=True).then_inc(st_mm, 1)

            def mods():
                for q in range(48, 52):
                    mod_tile(pe, 1, q, q // 4, q % 4, 2 * q)

            stats(0, mods)

            def up(layer):
                pe.wait_ge(ln_lo, 32 if layer else 8)
                up_body(layer, 0)
                with pe.Fori(1, 11) as it:
                    up_body(layer, it)

            def up_body(layer, it):
                for j in range(4):
                    if layer == 0:
                        mod_tile(pe, 1, None, it + 13, j, 8 * it + (52 + j) * 2)
                    pe.wait_ge(lo_done, 4 * it + j + (N_UP1 if layer else N_UP0) + 1)
                    if not isinstance(it, int):
                        pe.wait_ge(up_a, 2 * it + j // 2 - 1 + 22 * layer)
                    gemm(bank[j][:], j, h_hi, h_lo, T, range(KC)).then_inc(gemm_done, 1)

            def down_body(layer, it):
                kc0 = (0, 8, 15)
                for j in range(12):
                    m = j // 3
                    if j % 3 == 0:
                        pe.wait_ge(r_done, 4 * it + m - 1 + (32 if layer else 8))
                    pe.wait_ge(lo_done, 12 * it + j + (N_DN1 if layer else N_DN0) + 1)
                    kcs = range(kc0[j % 3], kc0[j % 3] + DN_KC[j % 3])
                    gemm(res_bank(m)[:], j, A_hi, A_lo, T, kcs, first=j % 3 == 0, last=j % 3 == 2)\
                        .then_inc(gemm_done, 1)

            def down(layer):
                pe.wait_ge(up_lo, 22 * (layer + 1))
                with pe.Fori(0, 2) as it:
                    down_body(layer, it)

            up(0)
            down(0)
            stats(1)
            pe.wait_ge(ln_lo, 16)

            def cv1_body(it):
                for j in range(4):
                    pe.wait_ge(lo_done, 4 * it + j + N_CV1 + 1)
                    if not isinstance(it, int):
                        pe.wait_ge(cv_u, 2 * it + j // 2 - 1)
                    gemm(bank[j][:], j, h_hi, h_lo, T, range(KC)).then_inc(gemm_done, 1)

            cv1_body(0)
            with pe.Fori(1, 4) as it:
                cv1_body(it)
            stats(2)
            pe.wait_ge(ln_lo, 24)
            with pe.Fori(0, 2) as it:
                for j in range(4):
                    pe.wait_ge(lo_done, 4 * it + j + N_CV2 + 1)
                    pe.wait_ge(r_done, 4 * it + j - 1 + 24)
                    gemm(res_bank(j)[:], j, h_hi, h_lo, T, range(KC)).then_inc(gemm_done, 1)
            stats(3)
            up(1)
            down(1)
            stats(4)

        @block.scalar
        def _(act):
            act.wait_ge(const_in, 32)
            nc.scalar.activation(cact[:], cin[:], ACT.Silu).then_inc(cact_done, 1)
            for n in range(2):
                split_hi(act, 0, n, first=True)
            act.wait_ge(modv_done, 1)
            act.wait_ge(ones_set, 1)
            act.wait_ge(x_in, 32)
            for j in range(16):
                v, hi, c = (xin, h_hi, 0) if j < 8 else (cxin, hc_hi, 1)
                nc.scalar.activation(v[:, j % 8], v[:, j % 8], ACT.Identity,
                                     bias=mod[:, 0, SH1 * 8 + j % 8, c:c + 1],
                                     scale=modp[:, 0, SC1 * 8 + j % 8, c:c + 1]).then_inc(hx_done, 1)
                act.wait_ge(hx_done, j + 1)
                nc.scalar.activation(hi[:, j % 8], v[:, j % 8], ACT.Copy).then_inc(hhi_done, 1)

            def to_tiles(v):
                return v.rearrange("p (r t c) -> p t r c", r=ROWS, t=NT)

            def tiles(v):
                return v.rearrange("p (t r c) -> p t r c", r=ROWS, t=NT)

            for n in range(32):
                kind, f = divmod(n, 4)
                i, v = n - 4, -1
                if n in v_tile:
                    v = v_tile.index(n)
                if 5 <= n <= 12:
                    u = n - 5
                    act.wait_ge(z_pre, u + 1)
                    if u >= 1:
                        act.wait_ge(z_kd, u)
                    if u < HH:
                        nc.scalar.activation(Ec[:], prec[:, 1:TC + 1], ACT.Exp, bias=prec[:, TC:TC + 1],
                                             scale=-1.0).then_inc(z_ec, 1)
                    else:
                        nc.scalar.activation(Ec[:], prec[:, 0:TC], ACT.Exp).then_inc(z_ec, 1)
                split_hi(act, n // 4, n % 4 + 2)
                px, pc = bank[n % 2], bank[2 + n % 2][:, 0:TC]
                if kind == IB or kind == VA:
                    if v >= 1:
                        act.wait_ge(vt_tr, v)
                    if kind == IB:
                        nc.scalar.activation(VT[:, 0:T], px[:], ACT.Copy).then_inc(evac_act, 1)
                    else:
                        nc.scalar.activation(tiles(VT[:, 0:T]), to_tiles(px[:]), ACT.Copy).then_inc(evac_act, 1)
                elif kind == ZF or kind == ZB:
                    if i >= 1:
                        act.wait_ge(z_key, i)
                    nc.scalar.activation(ab[:, 0:T], px[:], ACT.Abs)
                    nc.scalar.activation(ab[:, T:T + TC], pc, ACT.Abs).then_inc(evac_act, 1)
                    act.wait_ge(evac_act, n + 1)
                    nc.scalar.activation(ab[:], ab[:], ACT.Exp, scale=-1.0).then_inc(z_exp, 1)
                    act.wait_ge(z_exp, i + 1)
                    nc.scalar.activation(lb_[:], ab[:], ACT.Ln, bias=ones[:, 0:1]).then_inc(z_ln, 1)
                elif kind == KA:
                    nc.scalar.activation(KT_[:, f], px[:], ACT.Copy).then_inc(evac_act, 1)
                elif kind == QB:
                    nc.scalar.activation(QBt[:, f], px[:], ACT.Copy).then_inc(evac_act, 1)
                elif kind == QA:
                    nc.scalar.activation(tiles(Qt[:, f]), to_tiles(px[:]), ACT.Copy,
                                         scale=HD ** -0.5).then_inc(evac_act, 1)
                else:
                    nc.scalar.activation(GBt[:, f], px[:], ACT.Silu).then_inc(evac_act, 1)
                if n - 1 in v_tile:
                    w = v_tile.index(n - 1)
                    act.wait_ge(vt_tr, w + 1)
                    dst = (VIC if w < 4 else VAC)[:, :, (w % 4) * P:(w % 4 + 1) * P]
                    nc.scalar.activation(dst, bank[5][:, 0:TC].rearrange("p (c d) -> p c d", c=2),
                                         ACT.Copy).then_inc(vc_done, 1)
                if 5 <= n <= 12:
                    u = n - 5
                    act.wait_ge(z_tr, u + 1)
                    if u >= 1:
                        act.wait_ge(z_mm, u)
                    nc.scalar.activation(KcT[:].rearrange("p c d -> p (c d)"), bank[6][:, 0:TC], ACT.Copy).then_inc(z_kt, 1)
                if kind == ZF or kind == ZB:
                    act.wait_ge(z_d, i + 1)
                    if i >= 1:
                        act.wait_ge(z_kd, i)
                    nc.scalar.activation(KEY[:, i], ab[:, 0:T], ACT.Exp)
                    nc.scalar.activation(keyc[:], ab[:, T:T + TC], ACT.Exp).then_inc(z_key, 1)

            act.wait_ge(gemm_done, 32)
            B_SL, B_SC, B_PL, B_PC, B_O, B_HA, B_HO, B_HT = bank
            for s in range(NSLOT):
                k = s - 1
                if 0 <= k < NITEM:
                    u, e, d, head, i = hg(k)
                    act.wait_ge(g_sub, k + 1)
                    b = EX[:, k % 4].rearrange("p c t -> p (c t)")
                    nc.scalar.activation(b, b, ACT.Exp).then_inc(g_exp, 1)
                    if e == 0:
                        if u >= 1:
                            act.wait_ge(g_st, 3 * u)
                        nc.scalar.activation(gam[:, d], PRE[:, i, :, CH], ACT.Exp).then_inc(g_gam, 1)
                        if d == 1:
                            act.wait_ge(g_ktr, u)
                            nc.scalar.activation(KD[:], prefix(i, d), ACT.Exp).then_inc(g_e2, 1)
                k = s - 5
                if 0 <= k < NITEM and k % 16 == 0:
                    u, e, d, head, i = hg(k)
                    if head >= 1:
                        act.wait_ge(g_o, head)
                    nc.scalar.activation(QD[:, 0], prefix(i, 0), ACT.Exp).then_inc(g_e2, 1)
                if s >= 2 and (s - 2) % 2 == 0 and (s - 2) // 2 < len(UNITS):
                    w = (s - 2) // 2
                    _, nl = window(UNITS[w][0])
                    act.wait_ge(n_neg, w + 1)
                    if w >= 2:
                        act.wait_ge(n_tr, w - 1)
                        act.wait_ge(n_sum, w - 1)
                    src = Ssb[:, w % 2, 0:nl * P].rearrange("p (r t c) -> p t r c", r=ROWS, t=nl)
                    dst = Pb[:, w % 2, 0:nl * P].rearrange("p (t r c) -> p t r c", r=ROWS, t=nl)
                    nc.scalar.activation(dst, src, ACT.Exp, bias=mxc[:, w % 2, 2:3], accum_out=sml[:, w % 2, 0:1])
                    nc.scalar.activation(Pb[:, w % 2, 3 * P:5 * P], B_SC[:, 0:TC], ACT.Exp, bias=mxc[:, w % 2, 2:3],
                                         accum_out=sml[:, w % 2, 1:2]).then_inc(n_exp, 1)
                if s >= 4 and (s - 4) % 2 == 0 and (s - 4) // 2 < len(UNITS):
                    w = (s - 4) // 2
                    act.wait_ge(n_tr, w + 1)
                    if w >= 2:
                        act.wait_ge(n_pv, w - 1)
                    nc.scalar.activation(PTb[:, w % 2, 3 * P:5 * P], B_PC[:, 0:TC], ACT.Copy).then_inc(n_ptc, 1)
                k = s - 4
                if 0 <= k < NITEM and k % 8 == 0:
                    u = k // 8
                    act.wait_ge(g_ktr, u + 1)
                    if u >= 1:
                        act.wait_ge(g_ds, u)
                    nc.scalar.activation(KDT[:].rearrange("p c d -> p (c d)"), B_HT[:, 0:3 * P], ACT.Copy).then_inc(g_kdt, 1)
                k = s - 6
                if 0 <= k < NITEM and k % 16 == 15:
                    hd_ = k // 16
                    act.wait_ge(g_o, hd_ + 1)
                    if hd_ >= 1:
                        act.wait_ge(g_onr, hd_)
                    nc.scalar.activation(ON[:].rearrange("p c d -> p (c d)"), B_HO[:], ACT.Square).then_inc(g_sq, 1)

            act.wait_ge(n_ot, NT)
            act.wait_ge(g_ot, HH)
            for j in range(8):
                nc.scalar.activation(h_hi[:, j], OT[:, j], ACT.Copy).then_inc(oh_hi, 1)

            def square(count, k, src):
                act.wait_ge(r_done, count + 1)
                if not (isinstance(count, int) and count == 0):
                    act.wait_ge(qs_done, count)
                nc.scalar.activation(tb[:, 0], src, ACT.Square).then_inc(sq_done, 1)

            def ln(k, src):
                act.wait_ge(ln_v, k + 1)
                nc.scalar.activation(tb[:, 3], tb[:, 3], ACT.Ln).then_inc(ln_l, 1)
                act.wait_ge(ln_l, k + 1)
                nc.scalar.activation(tb[:, 3], tb[:, 3], ACT.Exp, scale=-0.5).then_inc(ln_rstd, 1)
                nx = {0: 0, 1: 8, 3: 16, 4: 24}
                f = ACT.Silu if k == 2 else ACT.Identity
                for j in range(8):
                    act.wait_ge(ln_t2, 8 * k + j + 1)
                    if k == 4:
                        nc.scalar.activation(src[:, j], src[:, j], f, bias=norm[:, k, 3, j:j + 1],
                                             scale=norm[:, k, 2, j:j + 1]).then_inc(ln_x, 1)
                        continue
                    if j >= 2:
                        act.wait_ge(ln_lo, 8 * k + j - 1)
                    nc.scalar.activation(tb[:, j % 2], src[:, j], f, bias=norm[:, k, 1, j:j + 1],
                                         scale=norm[:, k, 0, j:j + 1]).then_inc(ln_h, 1)
                    act.wait_ge(ln_h, 8 * k + j + 1)
                    nc.scalar.activation(h_hi[:, j], tb[:, j % 2], ACT.Copy).then_inc(ln_hi, 1)
                if k in (0, 1, 3):
                    act.wait_ge(ln_hi, 24 + 8 if k == 3 else 8 * k + 8)
                    for j in range(8):
                        nc.scalar.activation(src[:, j], src[:, j], ACT.Identity, bias=norm[:, k, 3, j:j + 1],
                                             scale=norm[:, k, 2, j:j + 1]).then_inc(ln_x, 1)

            for n in range(8):
                split_hi(act, N_OUT // 4 + n // 4, n % 4 + 2)
                square(n, 0, XA[:, n])
            act.wait_ge(ln_vec, 1)
            ln(0, XA)

            def up(layer):
                n0 = (N_UP1 if layer else N_UP0) // 4
                with act.Fori(0, 11) as it:
                    for b in range(2):
                        k = 2 * it + b
                        split_hi(act, it + n0, 2 * b + 2)
                        nc.scalar.activation(tb[:, b], bank[2 * b][:], ACT.Silu).then_inc(up_s, 1)
                        split_hi(act, it + n0, 2 * b + 3)
                        act.wait_ge(up_a, k + 22 * layer + 1)
                        nc.scalar.activation(A_hi[:, k], tb[:, 2 + b], ACT.Copy).then_inc(up_hi, 1)

            def down_body(layer, it, last=False):
                for j in range(12):
                    if not (last and j >= 10):
                        split_hi(act, 3 * it + (N_DN1 if layer else N_DN0) // 4 + j // 4, j % 4 + 2)
                    if j % 3 == 2:
                        square(4 * it + j // 3 + (32 if layer else 8), 0, XA[:, 4 * it + j // 3])

            up(0)
            with act.Fori(0, 2) as it:
                down_body(0, it)
            act.wait_ge(ln_vec, 5)
            ln(1, XA)

            def cv1_body(it):
                for b in range(2):
                    k = 2 * it + b
                    split_hi(act, it + N_CV1 // 4, 2 * b + 2)
                    split_hi(act, it + N_CV1 // 4, 2 * b + 3)
                    nc.scalar.activation(tb[:, 2 + b], bank[2 * b + 1][:], ACT.Sigmoid,
                                         bias=vec[:, bass.ds(k + VEC["cv_b1"] + 8, 1)]).then_inc(cv_s, 1)
                    if not (isinstance(k, int) and k == 0):
                        square(k + 15, 2, RC[:, k - 1])

            cv1_body(0)
            with act.Fori(1, 4) as it:
                cv1_body(it)
            square(23, 2, RC[:, 7])
            ln(2, RC)
            with act.Fori(0, 2) as it:
                for j in range(4):
                    split_hi(act, it + N_CV2 // 4, j + 2)
                    square(4 * it + j + 24, 3, XA[:, 4 * it + j])
            ln(3, XA)
            up(1)
            down_body(1, 0)
            down_body(1, 1, last=True)
            ln(4, XA)

        @block.vector
        def _(dve):
            V = nc.vector
            steps = [0]

            def small(ins):
                steps[0] += 1
                ins.then_inc(mchain, 1)
                dve.wait_ge(mchain, steps[0])

            V.memset(PRE[:, :, :, 0:1], 0.0)
            small(V.memset(prec[:, 0:1], 0.0))
            small(V.memset(neg_half[:], -0.5))

            def mod_values(layer, lo, hi, count):
                dve.wait_ge(mod_done, count)
                c0 = (48 * layer + lo) * 2
                src = bank[7][:, c0:c0 + 2 * (hi - lo)].rearrange("p (f c) -> p f c", c=2)
                b0 = VEC["b_mod"] + 48 * layer
                b = vec[:, b0 + lo:b0 + hi].unsqueeze(2).broadcast_to([P, hi - lo, 2])
                small(V.tensor_tensor(mod[:, layer, lo:hi], src, b, ALU.add))
                V.tensor_scalar(modp[:, layer, lo:hi], mod[:, layer, lo:hi], 1.0, None, ALU.add).then_inc(modv_done, 1)

            def norm_vectors(k, g, b, sc=None, sh=None, layer=0, extra=None):
                dve.wait_ge(modv_done, 3 if k else 2)
                G, B, AG, AB = (norm[:, k, r] for r in range(4))
                if sc is not None:
                    small(V.tensor_tensor(G, g, modp[:, layer, sc * 8:sc * 8 + 8, 0], ALU.mult))
                    small(V.tensor_tensor(B, b, modp[:, layer, sc * 8:sc * 8 + 8, 0], ALU.mult))
                    small(V.tensor_tensor(B, B, mod[:, layer, sh * 8:sh * 8 + 8, 0], ALU.add))
                elif k == 2:
                    small(V.tensor_copy(G, g))
                    V.tensor_copy(B, b).then_inc(ln_vec, 1)
                    return
                a = 1.0 if k == 4 else ALPHA
                small(V.tensor_scalar(AG, g, a, None, ALU.mult))
                if extra is None:
                    V.tensor_scalar(AB, b, a, None, ALU.mult).then_inc(ln_vec, 1)
                else:
                    small(V.tensor_scalar(AB, b, a, None, ALU.mult))
                    small(V.tensor_tensor(norm[:, k, 4], extra, mod[:, 1, G1 * 8:G1 * 8 + 8, 0], ALU.mult))
                    V.tensor_tensor(AB, AB, norm[:, k, 4], ALU.add).then_inc(ln_vec, 1)

            def vcol(name, i=0):
                return vec[:, VEC[name] + 8 * i:VEC[name] + 8 * i + 8]

            dve.wait_ge(const_in, 32)
            mod_values(0, 0, 16, 16)
            for j in range(16):
                v, hi, lo = (xin, h_hi, h_lo) if j < 8 else (cxin, hc_hi, hc_lo)
                dve.wait_ge(hhi_done, j + 1)
                V.tensor_tensor(lo[:, j % 8], v[:, j % 8], hi[:, j % 8].bitcast(fp32), ALU.subtract).then_inc(hlo_done, 1)

            dve.wait_ge(ones_set, 1)
            for n in range(32):
                kind, f = divmod(n, 4)
                i, v = n - 4, -1
                if n in v_tile:
                    v = v_tile.index(n)
                if 5 <= n <= 12:
                    u = n - 5
                    dve.wait_ge(z_ec, u + 1)
                    if u >= 1:
                        dve.wait_ge(z_tr, u)
                    V.tensor_tensor(Kdc[:], keyc[:], Ec[:], ALU.mult).then_inc(z_kd, 1)
                px, pc = bank[n % 2], bank[2 + n % 2][:, 0:TC]
                dve.wait_ge(gemm_done, n + 1)
                if kind == IB or kind == VA:
                    if v >= 1:
                        dve.wait_ge(vt_tr, v)
                    V.tensor_copy(VT[:, T:T + TC], pc).then_inc(evac_dve, 1)
                elif kind == ZF or kind == ZB:
                    dve.wait_ge(z_ln, i + 1)
                    if i >= 1:
                        dve.wait_ge(z_pre, i)
                    V.scalar_tensor_tensor(out=ls[:, 0:T], in0=px[:], scalar=0.0, in1=lb_[:, 0:T], op0=ALU.min,
                                           op1=ALU.subtract)
                    V.scalar_tensor_tensor(out=ls[:, T:T + TC], in0=pc, scalar=0.0, in1=lb_[:, T:T + TC], op0=ALU.min,
                                           op1=ALU.subtract).then_inc(z_ls, 1)
                    dve.wait_ge(z_ls, i + 1)
                    V.tensor_tensor(ab[:, 0:T], ls[:, 0:T], px[:], ALU.subtract)
                    V.tensor_tensor(ab[:, T:T + TC], ls[:, T:T + TC], pc, ALU.subtract).then_inc(z_d, 1)
                    if i >= 1:
                        dve.wait_ge(z_ec, i)
                    one = ones[:, 0:1].broadcast_to([P, TC])
                    for c in range(NCH):
                        V.tensor_tensor_scan(out=PRE[:, i, c, 1:CH + 1], data0=ones[:], data1=ls[:, c * CH:(c + 1) * CH],
                                             initial=0.0, op0=ALU.mult, op1=ALU.add)
                    V.tensor_tensor_scan(out=prec[:, 1:TC + 1], data0=one, data1=ls[:, T:T + TC],
                                         initial=0.0, op0=ALU.mult, op1=ALU.add).then_inc(z_pre, 1)
                elif kind == KA:
                    V.tensor_copy(KTC[:, f], pc).then_inc(evac_dve, 1)
                if n - 1 in v_tile:
                    w = v_tile.index(n - 1)
                    dve.wait_ge(vt_tr, w + 1)
                    dst = (VI if w < 4 else VAt)[:, :, (w % 4) * P:(w % 4 + 1) * P]
                    V.tensor_copy(dst, bank[4][:].rearrange("p (c d) -> p c d", c=4)).then_inc(vx_done, 1)
                if 5 <= n <= 12:
                    u = n - 5
                    dve.wait_ge(z_mm, u + 1)
                    V.tensor_copy(S0[:, u], bank[6][:, 256:384]).then_inc(z_s0, 1)

            mod_values(0, 16, 48, 48)
            norm_vectors(0, vcol("ln1_g"), vcol("ln1_b"), SC2, SH2)

            B_SL, B_SC, B_PL, B_PC, B_O, B_HA, B_HO, B_HT = bank
            dve.wait_ge(z_key, 8)
            dve.wait_ge(evac_act, 32)
            dve.wait_ge(table_in, 32)
            dve.wait_ge(lvl_done, 1)
            for s in range(NSLOT):
                k = s - 4
                if 0 <= k < NITEM:
                    u, e, d, head, i = hg(k)
                    dve.wait_ge(g_mm, k + 1)
                    a_ = AT[:, d]
                    p_ = B_HA[:].rearrange("p (c t) -> p c t", c=NCH)
                    if e == 0:
                        if head >= 1:
                            dve.wait_ge(g_o, head)
                        V.tensor_tensor(a_, p_, ident[:].unsqueeze(1).broadcast_to([P, NCH, CH]),
                                        ALU.mult).then_inc(g_at, 1)
                    else:
                        dve.wait_ge(g_at, k)
                        m_ = lvl[:, d, e - 1].unsqueeze(1).broadcast_to([P, NCH, CH])
                        V.copy_predicated(a_, m_, p_).then_inc(g_at, 1)
                if s >= 21 and (s - 21) % 16 == 0 and (s - 21) // 16 < NT:
                    t = (s - 21) // 16
                    dve.wait_ge(n_otr, t + 1)
                    for g in range(4):
                        dst = OT[:, g].rearrange("p (r c) -> p r c", r=ROWS)[:, :, t * TILE_W:(t + 1) * TILE_W]
                        ins = V.tensor_copy(dst, B_PL[:, g * P:(g + 1) * P].rearrange("p (r c) -> p r c", r=ROWS))
                    ins.then_inc(n_ot, 1)
                if s >= 1 and (s - 1) % 2 == 0 and (s - 1) // 2 < len(UNITS):
                    w = (s - 1) // 2
                    _, nl = window(UNITS[w][0])
                    dve.wait_ge(n_s, w + 1)
                    dve.wait_ge(n_comb, w + 1)
                    if w >= 2:
                        dve.wait_ge(n_exp, w - 1)
                    V.reduce_max(mxc[:, w % 2, 0:1], B_SC[:, 0:TC], AX.X).then_inc(n_mc, 1)
                    dve.wait_ge(n_mc, w + 1)
                    V.tensor_tensor_reduce(out=Ssb[:, w % 2, 0:nl * P], in0=B_SL[:, 0:nl * P],
                                           in1=comb[:, w % 2, 0:nl * P], scale=1.0, scalar=mxc[:, w % 2, 0:1],
                                           op0=ALU.add, op1=ALU.max, accum_out=mxc[:, w % 2, 1:2]).then_inc(n_mx, 1)
                    dve.wait_ge(n_mx, w + 1)
                    V.tensor_scalar(mxc[:, w % 2, 2:3], mxc[:, w % 2, 1:2], -1.0, None, ALU.mult).then_inc(n_neg, 1)
                if s >= 3 and (s - 3) % 2 == 0 and (s - 3) // 2 < len(UNITS):
                    w = (s - 3) // 2
                    t, h = UNITS[w]
                    dve.wait_ge(n_exp, w + 1)
                    V.tensor_tensor(rsum[:, t % 2, h:h + 1], sml[:, w % 2, 0:1], sml[:, w % 2, 1:2],
                                    ALU.add).then_inc(n_sum, 1)
                if s >= 4 and (s - 4) % 2 == 0 and (s - 4) // 2 < len(UNITS):
                    w = (s - 4) // 2
                    _, nl = window(UNITS[w][0])
                    dve.wait_ge(n_tr, w + 1)
                    if w >= 2:
                        dve.wait_ge(n_pv, w - 1)
                    V.tensor_copy(PTb[:, w % 2, 0:nl * P], B_PL[:, 0:nl * P]).then_inc(n_ptl, 1)
                if s >= 20 and (s - 20) % 16 == 0 and (s - 20) // 16 < NT:
                    t = (s - 20) // 16
                    dve.wait_ge(n_sum, 8 * (t + 1))
                    V.reciprocal(rinv[:, t % 2], rsum[:, t % 2]).then_inc(n_inv, 1)
                    dve.wait_ge(n_inv, t + 1)
                    dve.wait_ge(n_pv, 8 * (t + 1))
                    if t >= 1:
                        dve.wait_ge(n_otr, t)
                    V.tensor_tensor(Osb[:], B_O[:].rearrange("p (h d) -> p h d", h=NH),
                                    rinv[:, t % 2].unsqueeze(2).broadcast_to([P, NH, HD]), ALU.mult).then_inc(n_osb, 1)
                k = s - 6
                if 0 <= k < NITEM and k % 8 == 0:
                    u, e, d, head, i = hg(k)
                    dve.wait_ge(g_ds, u + 1)
                    dve.wait_ge(g_gam, u + 1)
                    if head >= 1:
                        dve.wait_ge(g_o, head)
                    for c in range(3):
                        cc = c if d == 0 else 3 - c
                        prev = S0[:, i] if c == 0 else St[:, d, c - 1]
                        if c:
                            dve.wait_ge(g_st, 3 * u + c)
                        V.scalar_tensor_tensor(out=St[:, d, c], in0=prev, scalar=gam[:, d, cc:cc + 1],
                                               in1=B_HT[:, c * P:(c + 1) * P], op0=ALU.mult,
                                               op1=ALU.add).then_inc(g_st, 1)
                k = s - 7
                if 0 <= k < NITEM and k % 16 == 15:
                    hd_ = k // 16
                    dve.wait_ge(g_sq, hd_ + 1)
                    V.reduce_sum(msq[:, 0], ON[:], AX.X).then_inc(g_ms, 1)
                    dve.wait_ge(g_ms, hd_ + 1)
                    V.tensor_scalar(msq[:, 1], msq[:, 0], 1.0 / P, RMS_EPS, ALU.mult, ALU.add).then_inc(g_mse, 1)
                k = s - 9
                if 0 <= k < NITEM and k % 16 == 15:
                    hd_ = k // 16
                    dve.wait_ge(g_pow, hd_ + 1)
                    V.tensor_tensor(ON[:], B_HO[:].rearrange("p (c d) -> p c d", c=NCH),
                                    msq[:, 2].unsqueeze(2).broadcast_to([P, NCH, P]), ALU.mult).then_inc(g_on, 1)
                k = s - 11
                if 0 <= k < NITEM and k % 16 == 15:
                    hd_ = k // 16
                    dve.wait_ge(g_onr, hd_ + 1)
                    g0 = VEC["hg_norm_g"] + hd_
                    V.scalar_tensor_tensor(out=OT[:, 4 + hd_], in0=B_HT[:], scalar=vec[:, g0:g0 + 1], in1=GBt[:, hd_],
                                           op0=ALU.mult, op1=ALU.mult).then_inc(g_ot, 1)
                k = s
                if k < NITEM:
                    u, e, d, head, i = hg(k)
                    if k >= 4:
                        dve.wait_ge(g_mm, k - 3)
                        if (k - 4) % 8 == 0:
                            dve.wait_ge(g_kd, (k - 4) // 8 + 1)
                    b = EX[:, k % 4]
                    if e == 0:
                        tot = PRE[:, i, :, CH:CH + 1].broadcast_to([P, NCH, CH])
                        V.tensor_tensor(b, tot, prefix(i, d), ALU.subtract).then_inc(g_sub, 1)
                    else:
                        nb, H = halves(e)
                        b = b.rearrange("p c (b t) -> p c b t", b=nb)
                        v_ = prefix(i, d).rearrange("p c (b t) -> p c b t", b=nb)
                        r_ = PRE[:, i, :, 1:CH + 1].rearrange("p c (b t) -> p c b t", b=nb)[:, :, :, H - 1:H]
                        r_ = r_.broadcast_to([P, NCH, nb, H])
                        V.tensor_tensor(b[:, :, :, 0:H], r_, v_[:, :, :, 0:H], ALU.subtract)
                        V.tensor_tensor(b[:, :, :, H:2 * H], v_[:, :, :, H:2 * H], r_, ALU.subtract).then_inc(g_sub, 1)

            for j in range(8):
                dve.wait_ge(oh_hi, j + 1)
                V.tensor_tensor(h_lo[:, j], OT[:, j], h_hi[:, j].bitcast(fp32), ALU.subtract).then_inc(oh_lo, 1)

            def zero_acc():
                V.memset(acc[:], 0.0).then_inc(acc_zero, 1)

            def residual(count, k, ps, gain, xa):
                V.scalar_tensor_tensor(out=xa, in0=ps, scalar=gain, in1=xa, op0=ALU.mult, op1=ALU.add).then_inc(r_done, 1)
                add_up(count, k, xa)

            def add_up(count, k, src):
                dve.wait_ge(r_done, count + 1)
                dve.wait_ge(rs_done, count)
                dve.wait_ge(acc_zero, k + 1)
                V.tensor_tensor(acc[:, 0], acc[:, 0], src, ALU.add).then_inc(rs_done, 1)

            def ln(k, src):
                dve.wait_ge(st_mm, k + 1)
                V.tensor_scalar(tb[:, 2], bank[5][:], 1.0 / D, None, ALU.mult).then_inc(ln_mu, 1)
                dve.wait_ge(ln_mu, k + 1)
                V.tensor_tensor(acc[:, 1], tb[:, 2], tb[:, 2], ALU.mult).then_inc(ln_m2, 1)
                dve.wait_ge(ln_m2, k + 1)
                V.scalar_tensor_tensor(out=tb[:, 3], in0=bank[6][:], scalar=1.0 / D, in1=acc[:, 1], op0=ALU.mult,
                                       op1=ALU.subtract).then_inc(ln_var, 1)
                dve.wait_ge(ln_var, k + 1)
                V.tensor_scalar(tb[:, 3], tb[:, 3], 0.0, LN_EPS, ALU.max, ALU.add).then_inc(ln_v, 1)
                dve.wait_ge(ln_rstd, k + 1)
                V.scalar_tensor_tensor(out=acc[:, 0], in0=tb[:, 2], scalar=-1.0, in1=tb[:, 3], op0=ALU.mult,
                                       op1=ALU.mult).then_inc(ln_nmr, 1)
                dve.wait_ge(ln_nmr, k + 1)

                def lo(j):
                    dve.wait_ge(ln_hi, 8 * k + j + 1)
                    V.tensor_tensor(h_lo[:, j], tb[:, j % 2], h_hi[:, j].bitcast(fp32), ALU.subtract).then_inc(ln_lo, 1)

                for j in range(8):
                    V.tensor_tensor(src[:, j], src[:, j], tb[:, 3], ALU.mult).then_inc(ln_t1, 1)
                    if j >= 2 and k < 4:
                        lo(j - 2)
                if k < 4:
                    lo(6)
                    lo(7)
                    dve.wait_ge(ln_t2, 8 * k + 8)
                    zero_acc()

            zero_acc()
            dve.wait_ge(xa_done, 1)
            for m in range(8):
                dve.wait_ge(gemm_done, N_OUT + m + 1)
                residual(m, 0, bank[m % 2][:], mod[:, 0, G1 * 8 + m, 0:1], XA[:, m])
            ln(0, XA)

            def up(layer):
                n0 = N_UP1 if layer else N_UP0

                def body(it):
                    for b in range(2):
                        k = 2 * it + b
                        dve.wait_ge(gemm_done, 4 * it + 2 * b + n0 + 2)
                        dve.wait_ge(up_s, k + 22 * layer + 1)
                        if not isinstance(it, int):
                            dve.wait_ge(up_lo, k + 22 * layer - 1)
                        V.tensor_tensor(tb[:, 2 + b], tb[:, b], bank[2 * b + 1][:], ALU.mult).then_inc(up_a, 1)
                        dve.wait_ge(up_hi, k + 22 * layer + 1)
                        V.tensor_tensor(A_lo[:, k], tb[:, 2 + b], A_hi[:, k].bitcast(fp32),
                                        ALU.subtract).then_inc(up_lo, 1)

                body(0)
                with dve.Fori(1, 11) as it:
                    body(it)

            def down(layer):
                with dve.Fori(0, 2) as it:
                    for m in range(4):
                        dve.wait_ge(gemm_done, 12 * it + 3 * m + (N_DN1 if layer else N_DN0) + 3)
                        if layer == 0:
                            dve.wait_ge(ln_x, 4 * it + m + 1)
                        residual(4 * it + m + (32 if layer else 8), 4 if layer else 1, bank[m % 2][:],
                                 mod[:, layer, bass.ds(4 * it + m + G2 * 8, 1), 0], XA[:, 4 * it + m])

            up(0)
            mod_values(1, 0, 48, 96)
            norm_vectors(1, vcol("ln2_g"), vcol("ln2_b"), SC1, SH1, 1, extra=vcol("cv_b2"))
            norm_vectors(2, vcol("cv_ln_g"), vcol("cv_ln_b"))
            norm_vectors(3, vcol("ln1_g", 1), vcol("ln1_b", 1), SC2, SH2, 1)
            norm_vectors(4, vcol("ln2_g", 1), vcol("ln2_b", 1))
            down(0)
            V.memset(U[:, :, 0:PAD], 0.0)
            V.memset(U[:, :, PAD + T:], 0.0).then_inc(cv_pad, 1)
            ln(1, XA)
            with dve.Fori(0, 4) as it:
                for b in range(2):
                    k = 2 * it + b
                    dve.wait_ge(cv_pad, 1)
                    dve.wait_ge(cv_s, k + 1)
                    dve.wait_ge(gemm_done, 4 * it + 2 * b + N_CV1 + 2)
                    V.scalar_tensor_tensor(out=U[:, b, PAD:PAD + T], in0=bank[2 * b][:],
                                           scalar=vec[:, bass.ds(k + VEC["cv_b1"], 1)], in1=tb[:, 2 + b], op0=ALU.add,
                                           op1=ALU.mult).then_inc(cv_u, 1)
                    dve.wait_ge(cv_u, k + 1)
                    rc = RC[:, k]
                    for tap in range(TAPS):
                        w_ = vec[:, bass.ds(TAPS * k + VEC["cv_wdw"] + tap, 1)]
                        u_ = U[:, b, tap:tap + T]
                        if tap == 0:
                            ins = V.tensor_scalar(rc, u_, w_, vec[:, bass.ds(k + VEC["cv_bdw"], 1)], ALU.mult, ALU.add)
                        else:
                            dve.wait_ge(cv_tap, (TAPS - 1) * k + tap)
                            ins = V.scalar_tensor_tensor(out=rc, in0=u_, scalar=w_, in1=rc, op0=ALU.mult, op1=ALU.add)
                        ins.then_inc(cv_tap if tap < TAPS - 1 else r_done, 1)
                    add_up(k + 16, 2, rc)
            ln(2, RC)
            with dve.Fori(0, 2) as it:
                for m in range(4):
                    dve.wait_ge(gemm_done, 4 * it + m + N_CV2 + 1)
                    dve.wait_ge(ln_x, 4 * it + m + 9)
                    residual(4 * it + m + 24, 3, bank[m % 2][:], mod[:, 1, bass.ds(4 * it + m + G1 * 8, 1), 0],
                             XA[:, 4 * it + m])
            ln(3, XA)
            up(1)
            dve.wait_ge(ln_x, 24)
            down(1)
            ln(4, XA)


def kernel(x, c, ctx, c_ctx, w_mod, b_mod, ln1_g, ln1_b, ln2_g, ln2_b, w_in_even, w_out_even, na_rpb, hg_lb,
           hg_norm_g, cv_w1, cv_b1, cv_wdw, cv_bdw, cv_ln_g, cv_ln_b, cv_w2, cv_b2, ffn_w1, ffn_w3, ffn_w2):
    import numpy as np
    import concourse.bacc as bacc
    from concourse.bass_utils import run_bass_kernel_spmd

    def features(a, n):
        return np.ascontiguousarray(np.asarray(a).T.reshape(-1, P, n).transpose(1, 0, 2))

    def columns(a):
        return np.asarray(a).reshape(-1, P).T

    def pieces(w):
        w = np.asarray(w)
        k, n = w.shape
        return np.ascontiguousarray(w.reshape(k // P, P, n // P, P).transpose(2, 1, 0, 3)).reshape(n // P, P, k)

    def interleave(a, b):
        return np.ascontiguousarray(np.stack([a, b], 1)).reshape((-1,) + a.shape[1:])

    w_in_t = pieces(w_in_even[0]).reshape(8, 4, P, D)[list(IN_ORDER)].reshape(32, P, D)
    cv1 = pieces(cv_w1[0])
    up_ = np.stack([interleave(pieces(ffn_w1[l]), pieces(ffn_w3[l])) for l in range(2)])
    vectors = np.concatenate([columns(a) for a in (b_mod, ln1_g, ln1_b, ln2_g, ln2_b, hg_norm_g, cv_b1, cv_bdw,
                                                   cv_ln_g, cv_ln_b, cv_b2)]
                             + [np.asarray(cv_wdw[0]).reshape(TAPS, 8, P).transpose(2, 1, 0).reshape(P, 8 * TAPS)], 1)

    qr, qc = np.divmod(np.arange(P), TILE_W)
    dr = np.arange(ROWS)[None, :] - qr[:, None] + ROWS - 1
    dc = np.clip(np.arange(WIN)[None, :] - TILE_W - qc[:, None] + TILE_W - 1, 0, 2 * TILE_W - 2)
    bias_t = np.ascontiguousarray(np.asarray(na_rpb)[0][:, dr[:, :, None], dc[:, None, :]].transpose(1, 0, 2, 3))
    mask = np.zeros((P, ROWS, 3, WIN), np.float32)
    for kind, (t, lo) in enumerate(((0, 0), (1, 0), (3, 2))):
        col = t * TILE_W + qc
        start = np.clip(col - TILE_W // 2, 0, COLS - TILE_W)
        kcol = lo * TILE_W + np.arange(WIN)
        seen = (kcol[None, :] >= start[:, None]) & (kcol[None, :] < start[:, None] + TILE_W)
        mask[:, :, kind, :] = np.where(seen, 0.0, -1e30)[:, None, :]
    lvl_t = np.zeros((P, 2, 7, P), np.float32)
    a = np.arange(P)
    for e, H in enumerate(LEVELS):
        same = a[:, None] // (2 * H) == a[None, :] // (2 * H)
        first = a // H % 2 == 0
        lvl_t[:, 0, e] = same & first[:, None] & ~first[None, :]
        lvl_t[:, 1, e] = same & ~first[:, None] & first[None, :]

    arrays = {
        "xT": features(x[0], T), "ctxT": features(ctx[0], TC),
        "cvec": np.ascontiguousarray(np.stack([columns(c[0]), columns(c_ctx)], 2)),
        "vecs": np.ascontiguousarray(vectors), "ident_d": np.eye(P, dtype=np.float32), "lvl_d": lvl_t,
        "bias_d": bias_t, "mask_d": mask,
        "wmod": np.concatenate([pieces(w_mod[0]), pieces(w_mod[1])]),
        "w_in": w_in_t, "w_out": pieces(w_out_even[0]), "w_up": up_,
        "w_dn": np.stack([pieces(ffn_w2[0]), pieces(ffn_w2[1])]),
        "cv1": interleave(cv1[:8], cv1[8:]), "cv2": pieces(cv_w2[0]),
    }
    nc = bacc.Bacc("TRN2", target_bir_lowering=False, num_devices=1)
    args = [nc.dram_tensor(f"in_{k}", v.shape, mybir.dt.from_np(v.dtype), kind="ExternalInput").ap()
            for k, v in arrays.items()]
    args.append(nc.dram_tensor("out_y", (8, P, T), mybir.dt.float32, kind="ExternalOutput").ap())
    build(nc, *args)
    r = run_bass_kernel_spmd(nc, [{f"in_{k}": v for k, v in arrays.items()}], core_ids=[0])
    y = r.results[0]["out_y"]
    return np.ascontiguousarray(np.asarray(y).reshape(D, T).T)[None]
```

```python
import concourse.bass as bass
from concourse import mybir
from contextlib import ExitStack

P = 128
D = 1024
KC = D // P
T = 512
TC = 256
ROWS, COLS = 8, 64
NH, HD = 8, 64
HH = 4
CH = 128
NCH = T // CH
TILE_W = 16
NT = COLS // TILE_W
WIN = 3 * TILE_W
DFF = 2816
FC = DFF // P
TAPS = 31
PAD = TAPS // 2
TA, TB, TM, TP = 10, 9, 6, 6
assert TA + TB + TM + TP == TAPS
ALPHA = (2 * 2) ** 0.25
LN_EPS, RMS_EPS = 1e-5, 1e-6
LEVELS = [64, 32, 16, 8, 4, 2, 1]

N_IN, N_OUT, N_UP0, N_DN0, N_CV1, N_CV2, N_UP1, N_DN1 = 0, 32, 40, 84, 108, 124, 132, 176
N_END = 200
DN_KC = (8, 7, 7)
IB, ZF, ZB, KA, VA, QB, QA, GB = range(8)
IN_ORDER = (4, 5, 6, 1, 2, 3, 0, 7)

VEC = {}
_at = 0
for _name, _n in (("b_mod", 96), ("ln1_g", 16), ("ln1_b", 16), ("ln2_g", 16), ("ln2_b", 16), ("hg_norm_g", 4),
                  ("cv_b1", 16), ("cv_bdw", 8), ("cv_ln_g", 8), ("cv_ln_b", 8), ("cv_b2", 8), ("cv_wdw", 8 * TAPS)):
    VEC[_name] = _at
    _at += _n
NVEC = _at

SH1, SC1, G1, SH2, SC2, G2 = range(6)


def build(nc, xT, ctxT, cvec, vecs, ident_d, lvl_d, bias_d, mask_d, wmod0, wmod, w_in, w_out, w_up, w_dn, cv1, cv2, out):
    fp32, f32r, u8 = mybir.dt.float32, mybir.dt.float32r, mybir.dt.uint8
    ACT, ALU, AX = mybir.ActivationFunctionType, mybir.AluOpType, mybir.AxisListType

    stack = ExitStack()
    with stack:
        BASE = 16512
        CONST, RING = BASE, BASE + 8192
        H0 = RING + 32768
        REST = H0 + 49152
        TMP = REST + 94336

        def at(name, shape, offset, dt=fp32):
            return nc.alloc_sbuf_tensor_at(name, [P] + shape, dt, offset=offset)

        const_at = [CONST]

        def const(name, shape, dt=fp32):
            size = 1
            for s in shape:
                size *= s
            t = at(name, shape, const_at[0], dt)
            const_at[0] += -(-size * (1 if dt == u8 else 4) // 32) * 32
            assert const_at[0] <= RING
            return t

        vec = const("vec", [NVEC])
        ident = const("ident", [P])
        ones = const("ones", [P])
        lvl = const("lvl", [2, 7, P], u8)
        cin = const("cin", [KC, 2])
        cact = const("cact", [KC, 2])
        mod0 = const("mod0", [KC, 2, 2])
        mod0p = const("mod0p", [KC, 2])
        mod = const("mod", [2, 48])
        modp = const("modp", [2, 48])
        norm = const("norm", [5, 5, 8])
        neg_half = const("neg_half", [4])
        mxc = const("mxc", [2, 4])
        sml = const("sml", [2, 2])
        rsum = const("rsum", [2, 8])
        rinv = const("rinv", [2, 8])
        gam = const("gam", [2, 4])
        msq = const("msq", [3, 4])

        raw = at("raw", [4, KC * P], RING)
        whi = at("whi", [2, KC * P], RING + 16384, f32r)
        wlo = at("wlo", [2, KC * P], RING + 24576, f32r)
        h_hi = at("h_hi", [KC, T], H0, f32r)
        h_lo = at("h_lo", [KC, T], H0 + 16384, f32r)
        hc_hi = at("hc_hi", [KC, TC], H0 + 32768, f32r)
        hc_lo = at("hc_lo", [KC, TC], H0 + 40960, f32r)
        mod_w0 = at("mod_w0", [16, KC * P], REST)
        mod_blk0 = at("mod_blk0", [2, D], REST)
        mod_acc0 = at("mod_acc0", [D], REST + 8192)
        KEY = at("KEY", [8, T], REST + 16384)
        PRE = at("PRE", [8, NCH, CH + 1], REST + 32768)
        QBt = at("QBt", [HH, T], REST + 49280)
        VI = at("VI", [NCH, 512], REST + 57472)
        VIC = at("VIC", [2, 512], REST + 65664)
        VAt = at("VAt", [NT, 512], REST + 69760)
        VAC = at("VAC", [2, 512], REST + 77952)
        KT_ = at("KT_", [4, T], REST + 82048)
        KTC = at("KTC", [4, TC], REST + 90240)
        xin = at("xin", [KC, T], REST + 69760)
        cxin = at("cxin", [KC, TC], REST + 86144)
        Qt = at("Qt", [4, T], H0 + 32768)
        GBt = at("GBt", [4, T], H0 + 40960)
        S0 = at("S0", [8, P], TMP)
        t1_ = TMP + 4096
        lvl_f = at("lvl_f", [2, 7, P], t1_ + 3072)
        VT = at("VT", [T + TC], t1_)
        ab = at("ab", [T + TC], t1_ + 3072)
        lb_ = at("lb_", [T + TC], t1_ + 6144)
        ls = at("ls", [T + TC], t1_ + 9216)
        keyc = at("keyc", [TC], t1_ + 12288)
        prec = at("prec", [TC + 1], t1_ + 13312)
        Ec = at("Ec", [TC], t1_ + 14368)
        Kdc = at("Kdc", [TC], t1_ + 15392)
        KcT = at("KcT", [2, P], t1_ + 16416)
        bias = at("bias", [NH, ROWS, WIN], REST)
        mask0 = at("mask0", [ROWS, 2 * TILE_W], REST + 12288)
        mask1 = at("mask1", [ROWS, WIN], REST + 13312)
        mask3 = at("mask3", [ROWS, 2 * TILE_W], REST + 14848)
        EX = at("EX", [4, NCH, CH], H0)
        QD = at("QD", [2, NCH, CH], H0 + 8192)
        AT = at("AT", [2, NCH, CH], H0 + 12288)
        OT = at("OT", [8, T], H0 + 16384)
        St = at("St", [2, 3, P], REST + 65664)
        comb = at("comb", [2, ROWS * WIN], t1_)
        Ssb = at("Ssb", [2, ROWS * WIN], t1_ + 3072)
        Pb = at("Pb", [2, 5 * P], t1_ + 6144)
        PTb = at("PTb", [2, 5 * P], t1_ + 11264)
        Osb = at("Osb", [NH, HD], t1_ + 16384)
        KD = at("KD", [NCH, CH], t1_ + 18432)
        KDT = at("KDT", [3, P], t1_ + 20480)
        ON = at("ON", [NCH, CH], t1_ + 22016)
        XA = at("XA", [8, T], REST)
        mod_blk1 = at("mod_blk1", [2, D], H0 + 32768)
        mod_acc1 = at("mod_acc1", [D], H0 + 40960)
        A_hi = at("A_hi", [FC, T], REST + 16384, f32r)
        A_lo = at("A_lo", [FC, T], REST + 16384 + 45056, f32r)
        U = at("U", [2, T + 2 * PAD], REST + 16384)
        RC = at("RC", [8, T], REST + 16384 + 8192)
        chain_b = at("chain_b", [2, T], REST + 40960)
        pool_sum = at("pool_sum", [2, T], REST + 45056)
        prod = at("prod", [3, T], REST + 49152)
        diag = at("diag", [2, TM, P], REST + 55296)
        tb = at("tb", [4, T], REST + 106496)
        acc = at("acc", [2, T], REST + 114688)

        bank = [stack.enter_context(nc.psum_tensor(f"bank{i}", [P, 512], fp32)) for i in range(8)]

        def sem(name):
            return stack.enter_context(nc.semaphore(name))

        table_in, lvl_done = sem("table_in"), sem("lvl_done")
        raw_in = [sem(f"raw_in{i}") for i in range(4)]
        mod0_in = [sem(f"mod0_in{i}") for i in range(16)]
        mod_in = [sem(f"mod_in{i}") for i in range(2)]
        mod0_done, blk_done, part_done = sem("mod0_done"), sem("blk_done"), sem("part_done")
        (hi_done, lo_done, gemm_done, mod_done, const_in, x_in, bias_in, xa_in, out_done, ones_set, cact_done,
         modv_done, mchain, hx_done, hhi_done, hlo_done) = [sem(n) for n in (
             "hi_done", "lo_done", "gemm_done", "mod_done", "const_in", "x_in", "bias_in", "xa_in", "out_done",
             "ones_set", "cact_done", "modv_done", "mchain", "hx_done", "hhi_done", "hlo_done")]
        (evac_act, evac_dve, vt_tr, vx_done, vc_done, z_abs, z_exp, z_ln, z_ls, z_d, z_key, z_pre, z_ec, z_kd,
         z_tr, z_kt, z_mm, z_s0) = [sem(n) for n in (
             "evac_act", "evac_dve", "vt_tr", "vx_done", "vc_done", "z_abs", "z_exp", "z_ln", "z_ls", "z_d",
             "z_key", "z_pre", "z_ec", "z_kd", "z_tr", "z_kt", "z_mm", "z_s0")]
        (n_comb, n_s, n_mc, n_mx, n_neg, n_exp, n_sum, n_tr, n_ptl, n_ptc, n_pv, n_inv, n_osb, n_otr, n_ot) = [
            sem(n) for n in ("n_comb", "n_s", "n_mc", "n_mx", "n_neg", "n_exp", "n_sum", "n_tr", "n_ptl", "n_ptc",
                             "n_pv", "n_inv", "n_osb", "n_otr", "n_ot")]
        (g_sub, g_exp, g_x, g_mm, g_at, g_e2, g_kd, g_ktr, g_kdt, g_ds, g_st, g_o, g_qd, g_gam, g_sq, g_ms, g_mse, g_pow, g_on,
         g_onr, g_ot) = [sem(n) for n in ("g_sub", "g_exp", "g_x", "g_mm", "g_at", "g_e2", "g_kd", "g_ktr",
                                          "g_kdt", "g_ds", "g_st", "g_o", "g_qd", "g_gam", "g_sq", "g_ms", "g_mse", "g_pow", "g_on",
                                          "g_onr", "g_ot")]
        (xa_done, oh_hi, oh_lo) = [sem(n) for n in ("xa_done", "oh_hi", "oh_lo")]
        (r_done, sq_done, rs_done, qs_done, acc_zero, st_mm, ln_vec, ln_mu, ln_m2, ln_var, ln_v, ln_l, ln_rstd,
         ln_nmr, ln_t1, ln_t2, ln_h, ln_hi, ln_lo, ln_x) = [sem(n) for n in (
             "r_done", "sq_done", "rs_done", "qs_done", "acc_zero", "st_mm", "ln_vec", "ln_mu", "ln_m2", "ln_var",
             "ln_v", "ln_l", "ln_rstd", "ln_nmr", "ln_t1", "ln_t2", "ln_h", "ln_hi", "ln_lo", "ln_x")]
        (up_s, up_a, up_hi, up_lo, cv_s, cv_u, cv_pad, cv_a, cv_b, cv_diag, cv_mm, cv_prod, cv_sum, cv_join) = [
            sem(n) for n in ("up_s", "up_a", "up_hi", "up_lo", "cv_s", "cv_u", "cv_pad", "cv_a", "cv_b", "cv_diag",
                             "cv_mm", "cv_prod", "cv_sum", "cv_join")]

        block = stack.enter_context(nc.Block())

        def load_piece(eng, g, j, src, cols, first=False):
            if not first:
                eng.wait_ge(lo_done, 4 * g + j - 3)
            eng.dma_start(raw[:, j, 0:cols], src).then_inc(raw_in[j], 16)

        def split_hi(eng, g, j, first=False):
            if j >= 4:
                g, j = g + 1, j - 4
            eng.wait_ge(raw_in[j], 16 * (g + 1))
            if not first:
                eng.wait_ge(gemm_done, 4 * g + j - 1)
            nc.scalar.activation(whi[:, j % 2], raw[:, j], ACT.Copy).then_inc(hi_done, 1)

        def split_lo(eng, g, j):
            if j >= 4:
                g, j = g + 1, j - 4
            eng.wait_ge(hi_done, 4 * g + j + 1)
            nc.gpsimd.tensor_tensor(wlo[:, j % 2], raw[:, j], whi[:, j % 2].bitcast(fp32),
                                    ALU.subtract).then_inc(lo_done, 1)

        def gemm(dst, j, rhs_hi, rhs_lo, cols, kcs, first=True, last=True):
            n = len(kcs)
            for i, kc in enumerate(kcs):
                w_h, w_l = (w[:, j % 2, i * P:(i + 1) * P] for w in (whi, wlo))
                nc.tensor.matmul(dst, w_h, rhs_hi[:, kc, 0:cols], start=(first and i == 0), stop=False)
                nc.tensor.matmul(dst, w_h, rhs_lo[:, kc, 0:cols], start=False, stop=False)
                mm = nc.tensor.matmul(dst, w_l, rhs_hi[:, kc, 0:cols], start=False, stop=(last and i == n - 1))
            return mm

        def load_block(sp, half, j, layer, part, kc, first=False):
            if not first:
                sp.wait_ge(blk_done, 2 * half + j - 1)
            sp.dma_start((mod_blk1 if layer else mod_blk0)[:, j], wmod[6 * layer + part, kc]).then_inc(mod_in[j], 16)

        def add_block(eng, half, j, layer, kc, part_no=None, start=True):
            blk, dst = (mod_blk1, mod_acc1) if layer else (mod_blk0, mod_acc0)
            eng.wait_ge(mod_in[j], 16 * (half + 1))
            if start and isinstance(kc, int) and kc == 0:
                if part_no is not None:
                    eng.wait_ge(part_done, part_no)
                nc.vector.tensor_scalar(dst[:], blk[:, j], cact[:, 0, 0:1], None, ALU.mult).then_inc(blk_done, 1)
            else:
                eng.wait_ge(blk_done, 2 * half + j)
                c_ = cact[:, kc, 0:1] if isinstance(kc, int) else cact[:, bass.ds(kc, 1), 0]
                nc.vector.scalar_tensor_tensor(out=dst[:], in0=blk[:, j], scalar=c_, in1=dst[:], op0=ALU.mult,
                                               op1=ALU.add).then_inc(blk_done, 1)

        def reduce_part(pe, blocks, layer, col):
            pe.wait_ge(blk_done, blocks)
            dst = mod_acc1 if layer else mod_acc0
            for f in range(8):
                o = bank[7][:, col + f:col + f + 1] if isinstance(col, int) else bank[7][:, bass.ds(col + f, 1)]
                mm = nc.tensor.matmul(o, dst[:, f * P:(f + 1) * P], ones[:, 0:1], start=True, stop=True)
            mm.then_inc(part_done, 1)

        N_CTX = 20
        v_tile = [0, 1, 2, 3, 16, 17, 18, 19]

        def dve_read(eng, n):
            if 4 <= n < 12:
                eng.wait_ge(z_d, n - 3)
            elif n < N_CTX:
                eng.wait_ge(evac_dve, n + 1 if n < 4 else n - 7)

        UNITS = [(t, h) for t in range(NT) for h in range(NH)]
        KIND_MASK = [mask0, mask1, mask1, mask3]

        def window(t):
            lo = max(t - 1, 0)
            return lo, min(t + 2, NT) - lo

        NITEM = 8 * 8
        NSLOT = NITEM + 16

        def hg(s):
            u, e = divmod(s, 8)
            head, d = divmod(u, 2)
            return u, e, d, head, d * HH + head

        def halves(e):
            H = LEVELS[e - 1]
            return CH // (2 * H), H

        def prefix(i, d):
            return PRE[:, i, :, 1:CH + 1] if d == 0 else PRE[:, i, :, 0:CH]

        @block.sync
        def _(sp):
            sp.dma_start(cin[:], cvec).then_inc(const_in, 16)
            sp.dma_start(vec[:], vecs).then_inc(const_in, 16)
            def load_mod0(lo, hi):
                for q in range(lo, hi):
                    sp.dma_start(mod_w0[:, q], wmod0[q]).then_inc(mod0_in[q], 16)

            load_mod0(0, 6)
            sp.dma_start(xin[:], xT).then_inc(x_in, 16)
            sp.dma_start(cxin[:], ctxT).then_inc(x_in, 16)
            load_mod0(6, 14)
            for n in range(2):
                load_piece(sp, 0, n, w_in[n], KC * P, first=True)
            load_mod0(14, 16)
            sp.dma_start(ident[:], ident_d).then_inc(table_in, 16)
            sp.dma_start(lvl_f[:], lvl_d).then_inc(table_in, 16)
            for n in range(2, 32):
                load_piece(sp, n // 4, n % 4, w_in[n], KC * P, first=n < 4)
                b = n - 3
                if b == 0:
                    sp.wait_ge(mod0_done, KC)
                if b >= 0:
                    load_block(sp, b // 2, b % 2, 0, 2 + b // 8, b % 8, first=b < 2)
            for b in range(29, 32):
                load_block(sp, b // 2, b % 2, 0, 2 + b // 8, b % 8)
            for n in range(4):
                load_piece(sp, N_OUT // 4, n, w_out[n], KC * P)
            sp.wait_ge(part_done, 4)
            sp.dma_start(bias[:], bias_d).then_inc(bias_in, 16)
            sp.dma_start(mask0[:], mask_d[:, :, 0, 0:2 * TILE_W]).then_inc(bias_in, 16)
            sp.dma_start(mask1[:], mask_d[:, :, 1, :]).then_inc(bias_in, 16)
            sp.dma_start(mask3[:], mask_d[:, :, 2, 0:2 * TILE_W]).then_inc(bias_in, 16)
            sp.wait_ge(n_comb, len(UNITS))
            sp.dma_start(XA[:], xT).then_inc(xa_in, 16)
            for n in range(4, 8):
                load_piece(sp, N_OUT // 4 + 1, n % 4, w_out[n], KC * P)
            sp.wait_ge(oh_lo, 8)
            def up0():
                for j in range(4):
                    load_piece(sp, N_UP0 // 4, j, w_up[0, j], KC * P)
                with sp.Fori(0, 5) as it:
                    for j in range(8):
                        load_piece(sp, 2 * it + N_UP0 // 4 + 1 + j // 4, j % 4, w_up[0, 8 * it + 4 + j], KC * P)
                        load_block(sp, 4 * it + 16 + j // 2, j % 2, 1, it, j)

            def up1():
                with sp.Fori(0, 11) as it:
                    for j in range(4):
                        load_piece(sp, it + N_UP1 // 4, j, w_up[1, 4 * it + j], KC * P)

            def down(layer):
                with sp.Fori(0, 2) as it:
                    for j in range(12):
                        if layer == 0 and j % 3 == 0:
                            load_block(sp, 2 * it + 36 + j // 6, j // 3 % 2, 1, 5, 4 * it + j // 3)
                        k0 = sum(DN_KC[:j % 3]) * P
                        cols = DN_KC[j % 3] * P
                        load_piece(sp, 3 * it + (N_DN1 if layer else N_DN0) // 4 + j // 4, j % 4,
                                   w_dn[layer, 4 * it + j // 3, :, k0:k0 + cols], cols)

            up0()
            down(0)
            with sp.Fori(0, 4) as it:
                for j in range(4):
                    load_piece(sp, it + N_CV1 // 4, j, cv1[4 * it + j], KC * P)
            with sp.Fori(0, 2) as it:
                for j in range(4):
                    load_piece(sp, it + N_CV2 // 4, j, cv2[4 * it + j], KC * P)
            up1()
            down(1)
            for j in range(8):
                sp.wait_ge(ln_x, 24 + j + 1)
                sp.dma_start(out[j], XA[:, j]).then_inc(out_done, 16)
            sp.wait_ge(out_done, 16 * 8)

        @block.gpsimd
        def _(pool):
            nc.gpsimd.memset(ones[:], 1.0).then_inc(ones_set, 1)
            for n in range(2):
                split_lo(pool, 0, n)
            pool.wait_ge(table_in, 32)
            nc.gpsimd.tensor_copy(lvl[:], lvl_f[:]).then_inc(lvl_done, 1)
            for n in range(32):
                split_lo(pool, (n + 2) // 4, (n + 2) % 4)
            pool.wait_ge(gemm_done, 32)
            pool.wait_ge(bias_in, 64)
            for s in range(NSLOT):
                if s % 2 == 0 and s // 2 < len(UNITS):
                    w = s // 2
                    t, h = UNITS[w]
                    _, nl = window(t)
                    off = TILE_W if t == 0 else 0
                    if w >= 2:
                        pool.wait_ge(n_mx, w - 1)
                    dst = comb[:, w % 2, 0:ROWS * nl * TILE_W].rearrange("p (r c) -> p r c", r=ROWS)
                    nc.gpsimd.tensor_tensor(dst, bias[:, h, :, off:off + nl * TILE_W], KIND_MASK[t][:],
                                            ALU.add).then_inc(n_comb, 1)
                k = s - 2
                if 0 <= k < NITEM:
                    u, e, d, head, i = hg(k)
                    pool.wait_ge(g_exp, k + 1)
                    if e == 0:
                        b = EX[:, k % 4]
                        q_ = QBt[:, head].rearrange("p (c t) -> p c t", c=NCH)
                        k_ = KEY[:, i].rearrange("p (c t) -> p c t", c=NCH)
                        if u >= 1:
                            pool.wait_ge(g_ktr, u)
                        if d == 0:
                            nc.gpsimd.tensor_tensor(KD[:], b, k_, ALU.mult).then_inc(g_kd, 1)
                        else:
                            if head >= 1:
                                pool.wait_ge(g_o, head)
                            pool.wait_ge(g_e2, u + 1)
                            nc.gpsimd.tensor_tensor(QD[:, 1], b, q_, ALU.mult).then_inc(g_qd, 1)
                            nc.gpsimd.tensor_tensor(KD[:], KD[:], k_, ALU.mult).then_inc(g_kd, 1)
                    else:
                        nb, H = halves(e)
                        b = EX[:, k % 4].rearrange("p c t -> p (c t)").rearrange("p (b two h) -> p b two h", two=2, h=H)
                        q_ = QBt[:, head].rearrange("p (b two h) -> p b two h", two=2, h=H)
                        k_ = KEY[:, i].rearrange("p (b two h) -> p b two h", two=2, h=H)
                        first, second = (k_, q_) if d == 0 else (q_, k_)
                        nc.gpsimd.tensor_tensor(b[:, :, 0], b[:, :, 0], first[:, :, 0], ALU.mult)
                        nc.gpsimd.tensor_tensor(b[:, :, 1], b[:, :, 1], second[:, :, 1], ALU.mult).then_inc(g_x, 1)
                k = s - 6
                if 0 <= k < NITEM and k % 16 == 0:
                    u, e, d, head, i = hg(k)
                    pool.wait_ge(g_e2, u + 1)
                    q_ = QBt[:, head].rearrange("p (c t) -> p c t", c=NCH)
                    nc.gpsimd.tensor_tensor(QD[:, 0], QD[:, 0], q_, ALU.mult).then_inc(g_qd, 1)
                k = s - 8
                if k >= 0 and k % 16 == 15 and k < NITEM:
                    hd_ = k // 16
                    pool.wait_ge(g_mse, hd_ + 1)
                    nc.gpsimd.tensor_tensor(msq[:, 2], msq[:, 1], neg_half[:], ALU.pow).then_inc(g_pow, 1)

            pool.wait_ge(xa_in, 16)
            nc.gpsimd.tensor_scalar(XA[:], XA[:], ALPHA, None, ALU.mult).then_inc(xa_done, 1)

            def ln_shift(k, src):
                for j in range(8):
                    pool.wait_ge(ln_t1, 8 * k + j + 1)
                    nc.gpsimd.tensor_tensor(src[:, j], src[:, j], acc[:, 0], ALU.add).then_inc(ln_t2, 1)

            def sum_sq(k, count):
                pool.wait_ge(sq_done, count + 1)
                pool.wait_ge(qs_done, count)
                pool.wait_ge(acc_zero, k + 1)
                nc.gpsimd.tensor_tensor(acc[:, 1], acc[:, 1], tb[:, 0], ALU.add).then_inc(qs_done, 1)

            for n in range(8):
                split_lo(pool, N_OUT // 4 + n // 4, n % 4 + 2)
                sum_sq(0, n)
            ln_shift(0, XA)

            def up(layer):
                with pool.Fori(0, 11) as it:
                    for j in range(4):
                        split_lo(pool, it + (N_UP1 if layer else N_UP0) // 4, j + 2)

            def down_body(layer, it, last=False):
                for j in range(12):
                    if not (last and j >= 10):
                        split_lo(pool, 3 * it + (N_DN1 if layer else N_DN0) // 4 + j // 4, j % 4 + 2)
                    if j % 3 == 2:
                        sum_sq(4 if layer else 1, 4 * it + j // 3 + (32 if layer else 8))

            up(0)
            with pool.Fori(0, 2) as it:
                down_body(0, it)
            ln_shift(1, XA)

            def cv1_body(it):
                for b in range(2):
                    k = 2 * it + b
                    split_lo(pool, it + N_CV1 // 4, 2 * b + 2)
                    split_lo(pool, it + N_CV1 // 4, 2 * b + 3)
                    for a in range(TP - 1):
                        pool.wait_ge(cv_prod, TP * k + a + 2)
                        if a == 0:
                            if not isinstance(it, int):
                                pool.wait_ge(cv_join, 2 * k - 2)
                            ins = nc.gpsimd.tensor_tensor(pool_sum[:, b], prod[:, 0], prod[:, 1], ALU.add)
                        else:
                            pool.wait_ge(cv_sum, (TP - 1) * k + a)
                            ins = nc.gpsimd.tensor_tensor(pool_sum[:, b], pool_sum[:, b], prod[:, (a + 1) % 3], ALU.add)
                        ins.then_inc(cv_sum, 1)
                    if not (isinstance(k, int) and k == 0):
                        sum_sq(2, k + 15)

            cv1_body(0)
            with pool.Fori(1, 4) as it:
                cv1_body(it)
            sum_sq(2, 23)
            ln_shift(2, RC)
            with pool.Fori(0, 2) as it:
                for j in range(4):
                    split_lo(pool, it + N_CV2 // 4, j + 2)
                    sum_sq(3, 4 * it + j + 24)
            ln_shift(3, XA)
            up(1)
            down_body(1, 0)
            down_body(1, 1, last=True)
            ln_shift(4, XA)

        @block.tensor
        def _(pe):
            pe.wait_ge(cact_done, 1)
            pe.wait_ge(ones_set, 1)
            for q in range(16):
                pe.wait_ge(mod0_in[q], 16)
                for kc in range(KC):
                    mm = nc.tensor.matmul(bank[q // 2][:, q % 2 * 2:q % 2 * 2 + 2], mod_w0[:, q, kc * P:(kc + 1) * P],
                                          cact[:, kc, :], start=(kc == 0), stop=(kc == KC - 1))
                mm.then_inc(mod_done, 1)
            pe.wait_ge(table_in, 32)
            pe.wait_ge(hlo_done, 16)

            def v_transposes(v):
                pe.wait_ge(evac_act, v_tile[v] + 1)
                dve_read(pe, v_tile[v])
                if v >= 1:
                    pe.wait_ge(vx_done, v)
                    pe.wait_ge(vc_done, v)
                for c in range(4):
                    nc.tensor.transpose(bank[4][:, c * P:(c + 1) * P], VT[:, c * P:(c + 1) * P], ident[:])
                for c in range(2):
                    mm = nc.tensor.transpose(bank[5][:, c * P:(c + 1) * P], VT[:, T + c * P:T + (c + 1) * P], ident[:])
                mm.then_inc(vt_tr, 1)

            def z_tail(i):
                pe.wait_ge(z_kd, i + 1)
                if i >= 1:
                    pe.wait_ge(z_s0, i)
                for c in range(2):
                    mm = nc.tensor.transpose(bank[6][:, c * P:(c + 1) * P], Kdc[:, c * P:(c + 1) * P], ident[:])
                mm.then_inc(z_tr, 1)
                pe.wait_ge(z_kt, i + 1)
                pe.wait_ge(vc_done, 4)
                head = i % HH
                for c in range(2):
                    mm = nc.tensor.matmul(bank[6][:, 256:384], KcT[:, c], VIC[:, c, head * P:(head + 1) * P],
                                          start=(c == 0), stop=(c == 1))
                mm.then_inc(z_mm, 1)

            for n in range(32):
                kind = n // 4
                pe.wait_ge(lo_done, n + 1)
                if n >= 2:
                    pe.wait_ge(evac_act, n - 1)
                    dve_read(pe, n - 2)
                mm = gemm(bank[n % 2][:], n, h_hi, h_lo, T, range(KC))
                if kind <= VA:
                    mm = gemm(bank[2 + n % 2][:, 0:TC], n, hc_hi, hc_lo, TC, range(KC))
                mm.then_inc(gemm_done, 1)
                if n % 8 == 7:
                    reduce_part(pe, n + 1, 0, n + 1)
                if n - 1 in v_tile:
                    v_transposes(v_tile.index(n - 1))
                if 5 <= n <= 12:
                    z_tail(n - 5)

            pe.wait_ge(evac_act, 32)
            pe.wait_ge(vx_done, 8)
            pe.wait_ge(vc_done, 8)
            pe.wait_ge(z_s0, 8)
            pe.wait_ge(modv_done, 1)
            B_SL, B_SC, B_PL, B_PC, B_O, B_HA, B_HO, B_HT = bank
            for s in range(NSLOT):
                if s >= 21 and (s - 21) % 16 == 0 and (s - 21) // 16 < NT:
                    t = (s - 21) // 16
                    pe.wait_ge(n_osb, t + 1)
                    pe.wait_ge(n_ptl, min(8 * t + 9, len(UNITS)))
                    for g in range(4):
                        mm = nc.tensor.transpose(B_PL[:, g * P:(g + 1) * P],
                                                 Osb[:, 2 * g:2 * g + 2].rearrange("p a b -> p (a b)"), ident[:])
                    mm.then_inc(n_otr, 1)
                k = s - 5
                if 0 <= k < NITEM and k % 16 == 15:
                    hd_ = k // 16
                    pe.wait_ge(g_at, k + 1)
                    pe.wait_ge(g_st, 3 * 2 * (hd_ + 1))
                    pe.wait_ge(g_qd, 2 * (hd_ + 1))
                    if hd_ >= 1:
                        pe.wait_ge(g_on, hd_)
                    for c in range(NCH):
                        v_ = VI[:, c, hd_ * P:(hd_ + 1) * P]
                        dst = B_HO[:, c * P:(c + 1) * P]
                        nc.tensor.matmul(dst, AT[:, 0, c], v_, start=True, stop=False)
                        nc.tensor.matmul(dst, AT[:, 1, c], v_, start=False, stop=False)
                        sf = S0[:, hd_] if c == 0 else St[:, 0, c - 1]
                        sb_ = S0[:, HH + hd_] if c == 3 else St[:, 1, 2 - c]
                        nc.tensor.matmul(dst, QD[:, 0, c], sf, start=False, stop=False)
                        mm = nc.tensor.matmul(dst, QD[:, 1, c], sb_, start=False, stop=True)
                    mm.then_inc(g_o, 1)
                if s % 2 == 0 and s // 2 < len(UNITS):
                    w = s // 2
                    t, h = UNITS[w]
                    lo, nl = window(t)
                    part = slice(HD * (h % 2), HD * (h % 2) + HD)
                    if w >= 1:
                        pe.wait_ge(n_mx, w)
                        pe.wait_ge(n_exp, w)
                    q_ = Qt[part, h // 2, t * P:(t + 1) * P]
                    k_ = KT_[part, h // 2].rearrange("p (r c) -> p r c", r=ROWS)[:, :, lo * TILE_W:(lo + nl) * TILE_W]
                    nc.tensor.matmul(B_SL[:, 0:ROWS * nl * TILE_W].rearrange("p (r c) -> p r c", r=ROWS), q_, k_,
                                     start=True, stop=True)
                    nc.tensor.matmul(B_SC[:, 0:TC], q_, KTC[part, h // 2], start=True, stop=True).then_inc(n_s, 1)
                if (s - 3) % 2 == 0 and 0 <= (s - 3) // 2 < len(UNITS):
                    w = (s - 3) // 2
                    _, nl = window(UNITS[w][0])
                    pe.wait_ge(n_exp, w + 1)
                    if w >= 1:
                        pe.wait_ge(n_ptl, w)
                        pe.wait_ge(n_ptc, w)
                    if w >= 9:
                        pe.wait_ge(n_ot, (w - 1) // 8)
                    for c in range(nl):
                        nc.tensor.transpose(B_PL[:, c * P:(c + 1) * P], Pb[:, w % 2, c * P:(c + 1) * P], ident[:])
                    for c in range(2):
                        mm = nc.tensor.transpose(B_PC[:, c * P:(c + 1) * P],
                                                 Pb[:, w % 2, (3 + c) * P:(4 + c) * P], ident[:])
                    mm.then_inc(n_tr, 1)
                if (s - 5) % 2 == 0 and 0 <= (s - 5) // 2 < len(UNITS):
                    w = (s - 5) // 2
                    t, h = UNITS[w]
                    lo, nl = window(t)
                    pe.wait_ge(n_ptl, w + 1)
                    pe.wait_ge(n_ptc, w + 1)
                    if h == 0 and t >= 1:
                        pe.wait_ge(n_osb, t)
                    dst = B_O[:, h * HD:(h + 1) * HD]
                    for c in range(nl):
                        nc.tensor.matmul(dst, PTb[:, w % 2, c * P:(c + 1) * P], VAt[:, lo + c, h * HD:(h + 1) * HD],
                                         start=(c == 0), stop=False)
                    for c in range(2):
                        mm = nc.tensor.matmul(dst, PTb[:, w % 2, (3 + c) * P:(4 + c) * P],
                                              VAC[:, c, h * HD:(h + 1) * HD], start=False, stop=(c == 1))
                    mm.then_inc(n_pv, 1)
                k = s - 3
                if 0 <= k < NITEM:
                    u, e, d, head, i = hg(k)
                    if k >= 1:
                        pe.wait_ge(g_at, k)
                    if e == 0:
                        for c in range(NCH):
                            mm = nc.tensor.matmul(B_HA[:, c * P:(c + 1) * P], KEY[:, i, c * P:(c + 1) * P],
                                                  QBt[:, head, c * P:(c + 1) * P], start=True, stop=True)
                        mm.then_inc(g_mm, 1)
                        pe.wait_ge(g_kd, u + 1)
                        if u >= 1:
                            pe.wait_ge(g_st, 3 * u)
                        if u >= 3:
                            pe.wait_ge(g_ot, (u - 1) // 2)
                        for c in range(3):
                            cc = c if d == 0 else 3 - c
                            mm = nc.tensor.transpose(B_HT[:, c * P:(c + 1) * P], KD[:, cc], ident[:])
                        mm.then_inc(g_ktr, 1)
                    else:
                        pe.wait_ge(g_x, k - u)
                        for c in range(NCH):
                            x_ = EX[:, k % 4, c]
                            mm = nc.tensor.matmul(B_HA[:, c * P:(c + 1) * P], x_, x_, start=True, stop=True)
                        mm.then_inc(g_mm, 1)
                k = s - 5
                if 0 <= k < NITEM and k % 8 == 0:
                    u, e, d, head, i = hg(k)
                    pe.wait_ge(g_kdt, u + 1)
                    for c in range(3):
                        cc = c if d == 0 else 3 - c
                        mm = nc.tensor.matmul(B_HT[:, c * P:(c + 1) * P], KDT[:, c], VI[:, cc, head * P:(head + 1) * P],
                                              start=True, stop=True)
                    mm.then_inc(g_ds, 1)
                k = s - 10
                if 0 <= k < NITEM and k % 16 == 15:
                    hd_ = k // 16
                    pe.wait_ge(g_on, hd_ + 1)
                    u_now = min(2 * (hd_ + 1) + 1, 8)
                    pe.wait_ge(g_st, 3 * u_now)
                    for c in range(NCH):
                        mm = nc.tensor.transpose(B_HT[:, c * P:(c + 1) * P], ON[:, c], ident[:])
                    mm.then_inc(g_onr, 1)

            def res_bank(m):
                return bank[m % 2]

            pe.wait_ge(oh_lo, 8)
            for m in range(8):
                pe.wait_ge(lo_done, N_OUT + m + 1)
                if m >= 2:
                    pe.wait_ge(r_done, m - 1)
                gemm(res_bank(m)[:], m, h_hi, h_lo, T, range(KC)).then_inc(gemm_done, 1)

            def stats(k):
                pe.wait_ge(rs_done, 8 * (k + 1))
                pe.wait_ge(qs_done, 8 * (k + 1))
                nc.tensor.matmul(bank[5][:], ones[:], acc[:, 0], start=True, stop=True)
                nc.tensor.matmul(bank[6][:], ones[:], acc[:, 1], start=True, stop=True).then_inc(st_mm, 1)

            stats(0)

            def up(layer):
                pe.wait_ge(ln_lo, 32 if layer else 8)
                up_body(layer, 0)
                if layer == 0:
                    with pe.Fori(0, 5) as it:
                        up_body(layer, 2 * it + 1)
                        up_body(layer, 2 * it + 2)
                        reduce_part(pe, 8 * it + 40, 1, 8 * it + 64)
                else:
                    with pe.Fori(1, 11) as it:
                        up_body(layer, it)

            def up_body(layer, it):
                for j in range(4):
                    pe.wait_ge(lo_done, 4 * it + j + (N_UP1 if layer else N_UP0) + 1)
                    if not isinstance(it, int):
                        pe.wait_ge(up_a, 2 * it + j // 2 - 1 + 22 * layer)
                    gemm(bank[j][:], j, h_hi, h_lo, T, range(KC)).then_inc(gemm_done, 1)

            def down_body(layer, it):
                kc0 = (0, 8, 15)
                for j in range(12):
                    m = j // 3
                    if j % 3 == 0:
                        pe.wait_ge(r_done, 4 * it + m - 1 + (32 if layer else 8))
                    pe.wait_ge(lo_done, 12 * it + j + (N_DN1 if layer else N_DN0) + 1)
                    kcs = range(kc0[j % 3], kc0[j % 3] + DN_KC[j % 3])
                    gemm(res_bank(m)[:], j, A_hi, A_lo, T, kcs, first=j % 3 == 0, last=j % 3 == 2)\
                        .then_inc(gemm_done, 1)

            def down(layer):
                pe.wait_ge(up_lo, 22 * (layer + 1))
                with pe.Fori(0, 2) as it:
                    down_body(layer, it)

            up(0)
            down(0)
            reduce_part(pe, 80, 1, 104)
            stats(1)
            pe.wait_ge(ln_lo, 16)

            def conv_taps(k, b):
                pe.wait_ge(cv_u, k + 1)
                pe.wait_ge(cv_diag, k + 1)
                pe.wait_ge(r_done, k + 16)
                for a in range(TM):
                    mm = nc.tensor.matmul(bank[4][:], diag[:, b, a], U[:, b, TA + TB + a:TA + TB + a + T],
                                          start=(a == 0), stop=(a == TM - 1))
                mm.then_inc(cv_mm, 1)

            def cv1_body(it):
                for j in range(4):
                    pe.wait_ge(lo_done, 4 * it + j + N_CV1 + 1)
                    if not isinstance(it, int):
                        pe.wait_ge(cv_u, 2 * it + j // 2 - 1)
                    gemm(bank[j][:], j, h_hi, h_lo, T, range(KC)).then_inc(gemm_done, 1)
                    if j % 2 and not (isinstance(it, int) and j == 1):
                        conv_taps(2 * it + j // 2 - 1, (j // 2 + 1) % 2)

            cv1_body(0)
            with pe.Fori(1, 4) as it:
                cv1_body(it)
            conv_taps(7, 1)
            stats(2)
            pe.wait_ge(ln_lo, 24)
            with pe.Fori(0, 2) as it:
                for j in range(4):
                    pe.wait_ge(lo_done, 4 * it + j + N_CV2 + 1)
                    pe.wait_ge(r_done, 4 * it + j - 1 + 24)
                    gemm(res_bank(j)[:], j, h_hi, h_lo, T, range(KC)).then_inc(gemm_done, 1)
            stats(3)
            up(1)
            down(1)
            stats(4)

        @block.scalar
        def _(act):
            act.wait_ge(const_in, 32)
            nc.scalar.activation(cact[:], cin[:], ACT.Silu).then_inc(cact_done, 1)
            for n in range(2):
                split_hi(act, 0, n, first=True)
            act.wait_ge(ones_set, 1)
            act.wait_ge(x_in, 32)
            for j in range(KC):
                act.wait_ge(mod0_done, j + 1)
                for c, v in enumerate((xin, cxin)):
                    nc.scalar.activation(v[:, j], v[:, j], ACT.Identity, bias=mod0[:, j, 0, c:c + 1],
                                         scale=mod0p[:, j, c:c + 1]).then_inc(hx_done, 1)
                for c, (v, hi) in enumerate(((xin, h_hi), (cxin, hc_hi))):
                    act.wait_ge(hx_done, 2 * j + c + 1)
                    nc.scalar.activation(hi[:, j], v[:, j], ACT.Copy).then_inc(hhi_done, 1)

            def to_tiles(v):
                return v.rearrange("p (r t c) -> p t r c", r=ROWS, t=NT)

            def tiles(v):
                return v.rearrange("p (t r c) -> p t r c", r=ROWS, t=NT)

            for n in range(32):
                kind, f = divmod(n, 4)
                i, v = n - 4, -1
                if n in v_tile:
                    v = v_tile.index(n)
                if 5 <= n <= 12:
                    u = n - 5
                    act.wait_ge(z_pre, u + 1)
                    if u >= 1:
                        act.wait_ge(z_kd, u)
                    if u < HH:
                        nc.scalar.activation(Ec[:], prec[:, 1:TC + 1], ACT.Exp, bias=prec[:, TC:TC + 1],
                                             scale=-1.0).then_inc(z_ec, 1)
                    else:
                        nc.scalar.activation(Ec[:], prec[:, 0:TC], ACT.Exp).then_inc(z_ec, 1)
                split_hi(act, n // 4, n % 4 + 2)
                px, pc = bank[n % 2], bank[2 + n % 2][:, 0:TC]
                if kind == IB or kind == VA:
                    if v >= 1:
                        act.wait_ge(vt_tr, v)
                    if kind == IB:
                        nc.scalar.activation(VT[:, 0:T], px[:], ACT.Copy).then_inc(evac_act, 1)
                    else:
                        nc.scalar.activation(tiles(VT[:, 0:T]), to_tiles(px[:]), ACT.Copy).then_inc(evac_act, 1)
                elif kind == ZF or kind == ZB:
                    if i >= 1:
                        act.wait_ge(z_key, i)
                    nc.scalar.activation(ab[:, 0:T], px[:], ACT.Abs)
                    nc.scalar.activation(ab[:, T:T + TC], pc, ACT.Abs).then_inc(evac_act, 1)
                    act.wait_ge(evac_act, n + 1)
                    nc.scalar.activation(ab[:], ab[:], ACT.Exp, scale=-1.0).then_inc(z_exp, 1)
                    act.wait_ge(z_exp, i + 1)
                    nc.scalar.activation(lb_[:], ab[:], ACT.Ln, bias=ones[:, 0:1]).then_inc(z_ln, 1)
                elif kind == KA:
                    nc.scalar.activation(KT_[:, f], px[:], ACT.Copy).then_inc(evac_act, 1)
                elif kind == QB:
                    nc.scalar.activation(QBt[:, f], px[:], ACT.Copy).then_inc(evac_act, 1)
                elif kind == QA:
                    nc.scalar.activation(tiles(Qt[:, f]), to_tiles(px[:]), ACT.Copy,
                                         scale=HD ** -0.5).then_inc(evac_act, 1)
                else:
                    nc.scalar.activation(GBt[:, f], px[:], ACT.Silu).then_inc(evac_act, 1)
                if n - 1 in v_tile:
                    w = v_tile.index(n - 1)
                    act.wait_ge(vt_tr, w + 1)
                    dst = (VIC if w < 4 else VAC)[:, :, (w % 4) * P:(w % 4 + 1) * P]
                    nc.scalar.activation(dst, bank[5][:, 0:TC].rearrange("p (c d) -> p c d", c=2),
                                         ACT.Copy).then_inc(vc_done, 1)
                if 5 <= n <= 12:
                    u = n - 5
                    act.wait_ge(z_tr, u + 1)
                    if u >= 1:
                        act.wait_ge(z_mm, u)
                    nc.scalar.activation(KcT[:].rearrange("p c d -> p (c d)"), bank[6][:, 0:TC], ACT.Copy).then_inc(z_kt, 1)
                if kind == ZF or kind == ZB:
                    act.wait_ge(z_d, i + 1)
                    if i >= 1:
                        act.wait_ge(z_kd, i)
                    nc.scalar.activation(KEY[:, i], ab[:, 0:T], ACT.Exp)
                    nc.scalar.activation(keyc[:], ab[:, T:T + TC], ACT.Exp).then_inc(z_key, 1)

            act.wait_ge(gemm_done, 32)
            B_SL, B_SC, B_PL, B_PC, B_O, B_HA, B_HO, B_HT = bank
            for s in range(NSLOT):
                k = s - 1
                if 0 <= k < NITEM:
                    u, e, d, head, i = hg(k)
                    act.wait_ge(g_sub, k + 1)
                    b = EX[:, k % 4].rearrange("p c t -> p (c t)")
                    nc.scalar.activation(b, b, ACT.Exp).then_inc(g_exp, 1)
                    if e == 0:
                        if u >= 1:
                            act.wait_ge(g_st, 3 * u)
                        nc.scalar.activation(gam[:, d], PRE[:, i, :, CH], ACT.Exp).then_inc(g_gam, 1)
                        if d == 1:
                            act.wait_ge(g_ktr, u)
                            nc.scalar.activation(KD[:], prefix(i, d), ACT.Exp).then_inc(g_e2, 1)
                k = s - 5
                if 0 <= k < NITEM and k % 16 == 0:
                    u, e, d, head, i = hg(k)
                    if head >= 1:
                        act.wait_ge(g_o, head)
                    nc.scalar.activation(QD[:, 0], prefix(i, 0), ACT.Exp).then_inc(g_e2, 1)
                if s >= 2 and (s - 2) % 2 == 0 and (s - 2) // 2 < len(UNITS):
                    w = (s - 2) // 2
                    _, nl = window(UNITS[w][0])
                    act.wait_ge(n_neg, w + 1)
                    if w >= 2:
                        act.wait_ge(n_tr, w - 1)
                        act.wait_ge(n_sum, w - 1)
                    src = Ssb[:, w % 2, 0:nl * P].rearrange("p (r t c) -> p t r c", r=ROWS, t=nl)
                    dst = Pb[:, w % 2, 0:nl * P].rearrange("p (t r c) -> p t r c", r=ROWS, t=nl)
                    nc.scalar.activation(dst, src, ACT.Exp, bias=mxc[:, w % 2, 2:3], accum_out=sml[:, w % 2, 0:1])
                    nc.scalar.activation(Pb[:, w % 2, 3 * P:5 * P], B_SC[:, 0:TC], ACT.Exp, bias=mxc[:, w % 2, 2:3],
                                         accum_out=sml[:, w % 2, 1:2]).then_inc(n_exp, 1)
                if s >= 4 and (s - 4) % 2 == 0 and (s - 4) // 2 < len(UNITS):
                    w = (s - 4) // 2
                    act.wait_ge(n_tr, w + 1)
                    if w >= 2:
                        act.wait_ge(n_pv, w - 1)
                    nc.scalar.activation(PTb[:, w % 2, 3 * P:5 * P], B_PC[:, 0:TC], ACT.Copy).then_inc(n_ptc, 1)
                k = s - 4
                if 0 <= k < NITEM and k % 8 == 0:
                    u = k // 8
                    act.wait_ge(g_ktr, u + 1)
                    if u >= 1:
                        act.wait_ge(g_ds, u)
                    nc.scalar.activation(KDT[:].rearrange("p c d -> p (c d)"), B_HT[:, 0:3 * P], ACT.Copy).then_inc(g_kdt, 1)
                k = s - 6
                if 0 <= k < NITEM and k % 16 == 15:
                    hd_ = k // 16
                    act.wait_ge(g_o, hd_ + 1)
                    if hd_ >= 1:
                        act.wait_ge(g_onr, hd_)
                    nc.scalar.activation(ON[:].rearrange("p c d -> p (c d)"), B_HO[:], ACT.Square).then_inc(g_sq, 1)

            act.wait_ge(n_ot, NT)
            act.wait_ge(g_ot, HH)
            for j in range(8):
                nc.scalar.activation(h_hi[:, j], OT[:, j], ACT.Copy).then_inc(oh_hi, 1)

            def square(count, k, src):
                act.wait_ge(r_done, count + 1)
                if not (isinstance(count, int) and count == 0):
                    act.wait_ge(qs_done, count)
                nc.scalar.activation(tb[:, 0], src, ACT.Square).then_inc(sq_done, 1)

            def ln(k, src):
                act.wait_ge(ln_v, k + 1)
                nc.scalar.activation(tb[:, 3], tb[:, 3], ACT.Ln).then_inc(ln_l, 1)
                act.wait_ge(ln_l, k + 1)
                nc.scalar.activation(tb[:, 3], tb[:, 3], ACT.Exp, scale=-0.5).then_inc(ln_rstd, 1)
                nx = {0: 0, 1: 8, 3: 16, 4: 24}
                f = ACT.Silu if k == 2 else ACT.Identity
                for j in range(8):
                    act.wait_ge(ln_t2, 8 * k + j + 1)
                    if k == 4:
                        nc.scalar.activation(src[:, j], src[:, j], f, bias=norm[:, k, 3, j:j + 1],
                                             scale=norm[:, k, 2, j:j + 1]).then_inc(ln_x, 1)
                        continue
                    if j >= 2:
                        act.wait_ge(ln_lo, 8 * k + j - 1)
                    nc.scalar.activation(tb[:, j % 2], src[:, j], f, bias=norm[:, k, 1, j:j + 1],
                                         scale=norm[:, k, 0, j:j + 1]).then_inc(ln_h, 1)
                    act.wait_ge(ln_h, 8 * k + j + 1)
                    nc.scalar.activation(h_hi[:, j], tb[:, j % 2], ACT.Copy).then_inc(ln_hi, 1)
                if k in (0, 1, 3):
                    act.wait_ge(ln_hi, 24 + 8 if k == 3 else 8 * k + 8)
                    for j in range(8):
                        nc.scalar.activation(src[:, j], src[:, j], ACT.Identity, bias=norm[:, k, 3, j:j + 1],
                                             scale=norm[:, k, 2, j:j + 1]).then_inc(ln_x, 1)

            for n in range(8):
                split_hi(act, N_OUT // 4 + n // 4, n % 4 + 2)
                square(n, 0, XA[:, n])
            act.wait_ge(ln_vec, 1)
            ln(0, XA)

            def up(layer):
                n0 = (N_UP1 if layer else N_UP0) // 4
                with act.Fori(0, 11) as it:
                    for b in range(2):
                        k = 2 * it + b
                        split_hi(act, it + n0, 2 * b + 2)
                        nc.scalar.activation(tb[:, b], bank[2 * b][:], ACT.Silu).then_inc(up_s, 1)
                        split_hi(act, it + n0, 2 * b + 3)
                        act.wait_ge(up_a, k + 22 * layer + 1)
                        nc.scalar.activation(A_hi[:, k], tb[:, 2 + b], ACT.Copy).then_inc(up_hi, 1)

            def down_body(layer, it, last=False):
                for j in range(12):
                    if not (last and j >= 10):
                        split_hi(act, 3 * it + (N_DN1 if layer else N_DN0) // 4 + j // 4, j % 4 + 2)
                    if j % 3 == 2:
                        square(4 * it + j // 3 + (32 if layer else 8), 0, XA[:, 4 * it + j // 3])

            up(0)
            with act.Fori(0, 2) as it:
                down_body(0, it)
            act.wait_ge(ln_vec, 5)
            ln(1, XA)

            def cv1_body(it):
                for b in range(2):
                    k = 2 * it + b
                    split_hi(act, it + N_CV1 // 4, 2 * b + 2)
                    split_hi(act, it + N_CV1 // 4, 2 * b + 3)
                    nc.scalar.activation(tb[:, 2 + b], bank[2 * b + 1][:], ACT.Sigmoid,
                                         bias=vec[:, bass.ds(k + VEC["cv_b1"] + 8, 1)]).then_inc(cv_s, 1)
                    w0 = TAPS * k + VEC["cv_wdw"]
                    if not isinstance(it, int):
                        act.wait_ge(cv_mm, k - 1)
                    for a in range(TM):
                        ins = nc.scalar.activation(diag[:, b, a], ident[:], ACT.Copy,
                                                   scale=vec[:, bass.ds(w0 + TA + TB + a, 1)])
                    ins.then_inc(cv_diag, 1)
                    act.wait_ge(cv_u, k + 1)
                    for a in range(TP):
                        if a >= 3:
                            act.wait_ge(cv_sum, (TP - 1) * k + max(a - 4, 0) + 1)
                        elif not (isinstance(k, int) and k == 0):
                            act.wait_ge(cv_sum, (TP - 1) * (k - 1) + a + 3)
                        tap = TAPS - TP + a
                        nc.scalar.activation(prod[:, a % 3], U[:, b, tap:tap + T], ACT.Copy,
                                             scale=vec[:, bass.ds(w0 + tap, 1)]).then_inc(cv_prod, 1)
                    if not (isinstance(k, int) and k == 0):
                        square(k + 15, 2, RC[:, k - 1])

            cv1_body(0)
            with act.Fori(1, 4) as it:
                cv1_body(it)
            square(23, 2, RC[:, 7])
            ln(2, RC)
            with act.Fori(0, 2) as it:
                for j in range(4):
                    split_hi(act, it + N_CV2 // 4, j + 2)
                    square(4 * it + j + 24, 3, XA[:, 4 * it + j])
            ln(3, XA)
            up(1)
            down_body(1, 0)
            down_body(1, 1, last=True)
            ln(4, XA)

        @block.vector
        def _(dve):
            V = nc.vector
            steps = [0]

            def small(ins):
                steps[0] += 1
                ins.then_inc(mchain, 1)
                dve.wait_ge(mchain, steps[0])

            def mod_values(layer, lo, hi, parts):
                dve.wait_ge(part_done, parts)
                c0 = 64 + lo if layer else lo - 8
                b0 = VEC["b_mod"] + 48 * layer
                small(V.tensor_tensor(mod[:, layer, lo:hi], bank[7][:, c0:c0 + hi - lo], vec[:, b0 + lo:b0 + hi], ALU.add))
                V.tensor_scalar(modp[:, layer, lo:hi], mod[:, layer, lo:hi], 1.0, None, ALU.add).then_inc(modv_done, 1)

            def norm_vectors(k, g, b, sc=None, sh=None, layer=0, extra=None):
                dve.wait_ge(modv_done, 2 if k else 1)
                G, B, AG, AB = (norm[:, k, r] for r in range(4))
                if sc is not None:
                    small(V.tensor_tensor(G, g, modp[:, layer, sc * 8:sc * 8 + 8], ALU.mult))
                    small(V.tensor_tensor(B, b, modp[:, layer, sc * 8:sc * 8 + 8], ALU.mult))
                    small(V.tensor_tensor(B, B, mod[:, layer, sh * 8:sh * 8 + 8], ALU.add))
                elif k == 2:
                    small(V.tensor_copy(G, g))
                    V.tensor_copy(B, b).then_inc(ln_vec, 1)
                    return
                a = 1.0 if k == 4 else ALPHA
                small(V.tensor_scalar(AG, g, a, None, ALU.mult))
                if extra is None:
                    V.tensor_scalar(AB, b, a, None, ALU.mult).then_inc(ln_vec, 1)
                else:
                    small(V.tensor_scalar(AB, b, a, None, ALU.mult))
                    small(V.tensor_tensor(norm[:, k, 4], extra, mod[:, 1, G1 * 8:G1 * 8 + 8], ALU.mult))
                    V.tensor_tensor(AB, AB, norm[:, k, 4], ALU.add).then_inc(ln_vec, 1)

            def vcol(name, i=0):
                return vec[:, VEC[name] + 8 * i:VEC[name] + 8 * i + 8]

            dve.wait_ge(const_in, 32)
            for j in range(KC + 1):
                if j < KC:
                    dve.wait_ge(mod_done, 2 * j + 2)
                    b = vec[:, VEC["b_mod"] + j:VEC["b_mod"] + j + 9:8].unsqueeze(2).broadcast_to([P, 2, 2])
                    small(V.tensor_tensor(mod0[:, j], bank[j][:, 0:4].rearrange("p (s c) -> p s c", s=2), b, ALU.add))
                    V.tensor_scalar(mod0p[:, j], mod0[:, j, 1], 1.0, None, ALU.add).then_inc(mod0_done, 1)
                if j >= 1:
                    for c, (v, hi, lo) in enumerate(((xin, h_hi, h_lo), (cxin, hc_hi, hc_lo))):
                        dve.wait_ge(hhi_done, 2 * j - 1 + c)
                        V.tensor_tensor(lo[:, j - 1], v[:, j - 1], hi[:, j - 1].bitcast(fp32),
                                        ALU.subtract).then_inc(hlo_done, 1)
            V.memset(PRE[:, :, :, 0:1], 0.0)
            small(V.memset(prec[:, 0:1], 0.0))
            small(V.memset(neg_half[:], -0.5))

            dve.wait_ge(ones_set, 1)
            for n in range(32):
                kind, f = divmod(n, 4)
                i, v = n - 4, -1
                if n in v_tile:
                    v = v_tile.index(n)
                if 5 <= n <= 12:
                    u = n - 5
                    dve.wait_ge(z_ec, u + 1)
                    if u >= 1:
                        dve.wait_ge(z_tr, u)
                    V.tensor_tensor(Kdc[:], keyc[:], Ec[:], ALU.mult).then_inc(z_kd, 1)
                add_block(dve, n // 2, n % 2, 0, n % 8, part_no=n // 8 if n else None)
                px, pc = bank[n % 2], bank[2 + n % 2][:, 0:TC]
                dve.wait_ge(gemm_done, n + 1)
                if kind == IB or kind == VA:
                    if v >= 1:
                        dve.wait_ge(vt_tr, v)
                    V.tensor_copy(VT[:, T:T + TC], pc).then_inc(evac_dve, 1)
                elif kind == ZF or kind == ZB:
                    dve.wait_ge(z_ln, i + 1)
                    if i >= 1:
                        dve.wait_ge(z_pre, i)
                    V.scalar_tensor_tensor(out=ls[:, 0:T], in0=px[:], scalar=0.0, in1=lb_[:, 0:T], op0=ALU.min,
                                           op1=ALU.subtract)
                    V.scalar_tensor_tensor(out=ls[:, T:T + TC], in0=pc, scalar=0.0, in1=lb_[:, T:T + TC], op0=ALU.min,
                                           op1=ALU.subtract).then_inc(z_ls, 1)
                    dve.wait_ge(z_ls, i + 1)
                    V.tensor_tensor(ab[:, 0:T], ls[:, 0:T], px[:], ALU.subtract)
                    V.tensor_tensor(ab[:, T:T + TC], ls[:, T:T + TC], pc, ALU.subtract).then_inc(z_d, 1)
                    if i >= 1:
                        dve.wait_ge(z_ec, i)
                    one = ones[:, 0:1].broadcast_to([P, TC])
                    for c in range(NCH):
                        V.tensor_tensor_scan(out=PRE[:, i, c, 1:CH + 1], data0=ones[:], data1=ls[:, c * CH:(c + 1) * CH],
                                             initial=0.0, op0=ALU.mult, op1=ALU.add)
                    V.tensor_tensor_scan(out=prec[:, 1:TC + 1], data0=one, data1=ls[:, T:T + TC],
                                         initial=0.0, op0=ALU.mult, op1=ALU.add).then_inc(z_pre, 1)
                elif kind == KA:
                    V.tensor_copy(KTC[:, f], pc).then_inc(evac_dve, 1)
                if n - 1 in v_tile:
                    w = v_tile.index(n - 1)
                    dve.wait_ge(vt_tr, w + 1)
                    dst = (VI if w < 4 else VAt)[:, :, (w % 4) * P:(w % 4 + 1) * P]
                    V.tensor_copy(dst, bank[4][:].rearrange("p (c d) -> p c d", c=4)).then_inc(vx_done, 1)
                if 5 <= n <= 12:
                    u = n - 5
                    dve.wait_ge(z_mm, u + 1)
                    V.tensor_copy(S0[:, u], bank[6][:, 256:384]).then_inc(z_s0, 1)

            mod_values(0, 16, 48, 4)
            norm_vectors(0, vcol("ln1_g"), vcol("ln1_b"), SC2, SH2)

            B_SL, B_SC, B_PL, B_PC, B_O, B_HA, B_HO, B_HT = bank
            dve.wait_ge(z_key, 8)
            dve.wait_ge(evac_act, 32)
            dve.wait_ge(table_in, 32)
            dve.wait_ge(lvl_done, 1)
            for s in range(NSLOT):
                k = s - 4
                if 0 <= k < NITEM:
                    u, e, d, head, i = hg(k)
                    dve.wait_ge(g_mm, k + 1)
                    a_ = AT[:, d]
                    p_ = B_HA[:].rearrange("p (c t) -> p c t", c=NCH)
                    if e == 0:
                        if head >= 1:
                            dve.wait_ge(g_o, head)
                        V.tensor_tensor(a_, p_, ident[:].unsqueeze(1).broadcast_to([P, NCH, CH]),
                                        ALU.mult).then_inc(g_at, 1)
                    else:
                        dve.wait_ge(g_at, k)
                        m_ = lvl[:, d, e - 1].unsqueeze(1).broadcast_to([P, NCH, CH])
                        V.copy_predicated(a_, m_, p_).then_inc(g_at, 1)
                if s >= 21 and (s - 21) % 16 == 0 and (s - 21) // 16 < NT:
                    t = (s - 21) // 16
                    dve.wait_ge(n_otr, t + 1)
                    for g in range(4):
                        dst = OT[:, g].rearrange("p (r c) -> p r c", r=ROWS)[:, :, t * TILE_W:(t + 1) * TILE_W]
                        ins = V.tensor_copy(dst, B_PL[:, g * P:(g + 1) * P].rearrange("p (r c) -> p r c", r=ROWS))
                    ins.then_inc(n_ot, 1)
                if s >= 1 and (s - 1) % 2 == 0 and (s - 1) // 2 < len(UNITS):
                    w = (s - 1) // 2
                    _, nl = window(UNITS[w][0])
                    dve.wait_ge(n_s, w + 1)
                    dve.wait_ge(n_comb, w + 1)
                    if w >= 2:
                        dve.wait_ge(n_exp, w - 1)
                    V.reduce_max(mxc[:, w % 2, 0:1], B_SC[:, 0:TC], AX.X).then_inc(n_mc, 1)
                    dve.wait_ge(n_mc, w + 1)
                    V.tensor_tensor_reduce(out=Ssb[:, w % 2, 0:nl * P], in0=B_SL[:, 0:nl * P],
                                           in1=comb[:, w % 2, 0:nl * P], scale=1.0, scalar=mxc[:, w % 2, 0:1],
                                           op0=ALU.add, op1=ALU.max, accum_out=mxc[:, w % 2, 1:2]).then_inc(n_mx, 1)
                    dve.wait_ge(n_mx, w + 1)
                    V.tensor_scalar(mxc[:, w % 2, 2:3], mxc[:, w % 2, 1:2], -1.0, None, ALU.mult).then_inc(n_neg, 1)
                if s >= 3 and (s - 3) % 2 == 0 and (s - 3) // 2 < len(UNITS):
                    w = (s - 3) // 2
                    t, h = UNITS[w]
                    dve.wait_ge(n_exp, w + 1)
                    V.tensor_tensor(rsum[:, t % 2, h:h + 1], sml[:, w % 2, 0:1], sml[:, w % 2, 1:2],
                                    ALU.add).then_inc(n_sum, 1)
                if s >= 4 and (s - 4) % 2 == 0 and (s - 4) // 2 < len(UNITS):
                    w = (s - 4) // 2
                    _, nl = window(UNITS[w][0])
                    dve.wait_ge(n_tr, w + 1)
                    if w >= 2:
                        dve.wait_ge(n_pv, w - 1)
                    V.tensor_copy(PTb[:, w % 2, 0:nl * P], B_PL[:, 0:nl * P]).then_inc(n_ptl, 1)
                if s >= 20 and (s - 20) % 16 == 0 and (s - 20) // 16 < NT:
                    t = (s - 20) // 16
                    dve.wait_ge(n_sum, 8 * (t + 1))
                    V.reciprocal(rinv[:, t % 2], rsum[:, t % 2]).then_inc(n_inv, 1)
                    dve.wait_ge(n_inv, t + 1)
                    dve.wait_ge(n_pv, 8 * (t + 1))
                    if t >= 1:
                        dve.wait_ge(n_otr, t)
                    V.tensor_tensor(Osb[:], B_O[:].rearrange("p (h d) -> p h d", h=NH),
                                    rinv[:, t % 2].unsqueeze(2).broadcast_to([P, NH, HD]), ALU.mult).then_inc(n_osb, 1)
                k = s - 6
                if 0 <= k < NITEM and k % 8 == 0:
                    u, e, d, head, i = hg(k)
                    dve.wait_ge(g_ds, u + 1)
                    dve.wait_ge(g_gam, u + 1)
                    if head >= 1:
                        dve.wait_ge(g_o, head)
                    for c in range(3):
                        cc = c if d == 0 else 3 - c
                        prev = S0[:, i] if c == 0 else St[:, d, c - 1]
                        if c:
                            dve.wait_ge(g_st, 3 * u + c)
                        V.scalar_tensor_tensor(out=St[:, d, c], in0=prev, scalar=gam[:, d, cc:cc + 1],
                                               in1=B_HT[:, c * P:(c + 1) * P], op0=ALU.mult,
                                               op1=ALU.add).then_inc(g_st, 1)
                k = s - 7
                if 0 <= k < NITEM and k % 16 == 15:
                    hd_ = k // 16
                    dve.wait_ge(g_sq, hd_ + 1)
                    V.reduce_sum(msq[:, 0], ON[:], AX.X).then_inc(g_ms, 1)
                    dve.wait_ge(g_ms, hd_ + 1)
                    V.tensor_scalar(msq[:, 1], msq[:, 0], 1.0 / P, RMS_EPS, ALU.mult, ALU.add).then_inc(g_mse, 1)
                k = s - 9
                if 0 <= k < NITEM and k % 16 == 15:
                    hd_ = k // 16
                    dve.wait_ge(g_pow, hd_ + 1)
                    V.tensor_tensor(ON[:], B_HO[:].rearrange("p (c d) -> p c d", c=NCH),
                                    msq[:, 2].unsqueeze(2).broadcast_to([P, NCH, P]), ALU.mult).then_inc(g_on, 1)
                k = s - 11
                if 0 <= k < NITEM and k % 16 == 15:
                    hd_ = k // 16
                    dve.wait_ge(g_onr, hd_ + 1)
                    g0 = VEC["hg_norm_g"] + hd_
                    V.scalar_tensor_tensor(out=OT[:, 4 + hd_], in0=B_HT[:], scalar=vec[:, g0:g0 + 1], in1=GBt[:, hd_],
                                           op0=ALU.mult, op1=ALU.mult).then_inc(g_ot, 1)
                k = s
                if k < NITEM:
                    u, e, d, head, i = hg(k)
                    if k >= 4:
                        dve.wait_ge(g_mm, k - 3)
                        if (k - 4) % 8 == 0:
                            dve.wait_ge(g_kd, (k - 4) // 8 + 1)
                    b = EX[:, k % 4]
                    if e == 0:
                        tot = PRE[:, i, :, CH:CH + 1].broadcast_to([P, NCH, CH])
                        V.tensor_tensor(b, tot, prefix(i, d), ALU.subtract).then_inc(g_sub, 1)
                    else:
                        nb, H = halves(e)
                        b = b.rearrange("p c (b t) -> p c b t", b=nb)
                        v_ = prefix(i, d).rearrange("p c (b t) -> p c b t", b=nb)
                        r_ = PRE[:, i, :, 1:CH + 1].rearrange("p c (b t) -> p c b t", b=nb)[:, :, :, H - 1:H]
                        r_ = r_.broadcast_to([P, NCH, nb, H])
                        V.tensor_tensor(b[:, :, :, 0:H], r_, v_[:, :, :, 0:H], ALU.subtract)
                        V.tensor_tensor(b[:, :, :, H:2 * H], v_[:, :, :, H:2 * H], r_, ALU.subtract).then_inc(g_sub, 1)

            for j in range(8):
                dve.wait_ge(oh_hi, j + 1)
                V.tensor_tensor(h_lo[:, j], OT[:, j], h_hi[:, j].bitcast(fp32), ALU.subtract).then_inc(oh_lo, 1)

            def zero_acc():
                V.memset(acc[:], 0.0).then_inc(acc_zero, 1)

            def residual(count, k, ps, gain, xa):
                V.scalar_tensor_tensor(out=xa, in0=ps, scalar=gain, in1=xa, op0=ALU.mult, op1=ALU.add).then_inc(r_done, 1)
                add_up(count, k, xa)

            def add_up(count, k, src):
                dve.wait_ge(r_done, count + 1)
                dve.wait_ge(rs_done, count)
                dve.wait_ge(acc_zero, k + 1)
                V.tensor_tensor(acc[:, 0], acc[:, 0], src, ALU.add).then_inc(rs_done, 1)

            def ln(k, src):
                dve.wait_ge(st_mm, k + 1)
                V.tensor_scalar(tb[:, 2], bank[5][:], 1.0 / D, None, ALU.mult).then_inc(ln_mu, 1)
                dve.wait_ge(ln_mu, k + 1)
                V.tensor_tensor(acc[:, 1], tb[:, 2], tb[:, 2], ALU.mult).then_inc(ln_m2, 1)
                dve.wait_ge(ln_m2, k + 1)
                V.scalar_tensor_tensor(out=tb[:, 3], in0=bank[6][:], scalar=1.0 / D, in1=acc[:, 1], op0=ALU.mult,
                                       op1=ALU.subtract).then_inc(ln_var, 1)
                dve.wait_ge(ln_var, k + 1)
                V.tensor_scalar(tb[:, 3], tb[:, 3], 0.0, LN_EPS, ALU.max, ALU.add).then_inc(ln_v, 1)
                dve.wait_ge(ln_rstd, k + 1)
                V.scalar_tensor_tensor(out=acc[:, 0], in0=tb[:, 2], scalar=-1.0, in1=tb[:, 3], op0=ALU.mult,
                                       op1=ALU.mult).then_inc(ln_nmr, 1)
                dve.wait_ge(ln_nmr, k + 1)

                def lo(j):
                    dve.wait_ge(ln_hi, 8 * k + j + 1)
                    V.tensor_tensor(h_lo[:, j], tb[:, j % 2], h_hi[:, j].bitcast(fp32), ALU.subtract).then_inc(ln_lo, 1)

                for j in range(8):
                    V.tensor_tensor(src[:, j], src[:, j], tb[:, 3], ALU.mult).then_inc(ln_t1, 1)
                    if j >= 2 and k < 4:
                        lo(j - 2)
                if k < 4:
                    lo(6)
                    lo(7)
                    dve.wait_ge(ln_t2, 8 * k + 8)
                    zero_acc()

            zero_acc()
            dve.wait_ge(xa_done, 1)
            for m in range(8):
                dve.wait_ge(gemm_done, N_OUT + m + 1)
                residual(m, 0, bank[m % 2][:], mod[:, 0, G1 * 8 + m:G1 * 8 + m + 1], XA[:, m])
            ln(0, XA)

            def up(layer):
                n0 = N_UP1 if layer else N_UP0

                def body(it, part=None, half=0):
                    for b in range(2):
                        k = 2 * it + b
                        if part is not None:
                            for q in range(2):
                                kc = 4 * half + 2 * b + q
                                add_block(dve, 4 * part + 16 + kc // 2, q, 1, kc, part_no=part + 4)
                        dve.wait_ge(gemm_done, 4 * it + 2 * b + n0 + 2)
                        dve.wait_ge(up_s, k + 22 * layer + 1)
                        if not isinstance(it, int):
                            dve.wait_ge(up_lo, k + 22 * layer - 1)
                        V.tensor_tensor(tb[:, 2 + b], tb[:, b], bank[2 * b + 1][:], ALU.mult).then_inc(up_a, 1)
                        dve.wait_ge(up_hi, k + 22 * layer + 1)
                        V.tensor_tensor(A_lo[:, k], tb[:, 2 + b], A_hi[:, k].bitcast(fp32),
                                        ALU.subtract).then_inc(up_lo, 1)

                body(0)
                if layer == 0:
                    with dve.Fori(0, 5) as it:
                        for p in range(2):
                            body(2 * it + 1 + p, it, p)
                else:
                    with dve.Fori(1, 11) as it:
                        body(it)

            def down(layer):
                with dve.Fori(0, 2) as it:
                    for m in range(4):
                        if layer == 0:
                            add_block(dve, 2 * it + 36 + m // 2, m % 2, 1, 4 * it + m)
                        dve.wait_ge(gemm_done, 12 * it + 3 * m + (N_DN1 if layer else N_DN0) + 3)
                        if layer == 0:
                            dve.wait_ge(ln_x, 4 * it + m + 1)
                        residual(4 * it + m + (32 if layer else 8), 4 if layer else 1, bank[m % 2][:],
                                 mod[:, layer, bass.ds(4 * it + m + G2 * 8, 1)], XA[:, 4 * it + m])

            up(0)
            mod_values(1, 0, 40, 9)
            norm_vectors(1, vcol("ln2_g"), vcol("ln2_b"), SC1, SH1, 1, extra=vcol("cv_b2"))
            norm_vectors(2, vcol("cv_ln_g"), vcol("cv_ln_b"))
            norm_vectors(3, vcol("ln1_g", 1), vcol("ln1_b", 1), SC2, SH2, 1)
            norm_vectors(4, vcol("ln2_g", 1), vcol("ln2_b", 1))
            dve.wait_ge(part_done, 9)
            small(V.memset(mod_acc1[:], 0.0))
            down(0)
            V.memset(U[:, :, 0:PAD], 0.0)
            V.memset(U[:, :, PAD + T:], 0.0).then_inc(cv_pad, 1)
            ln(1, XA)
            mod_values(1, 40, 48, 10)

            def join(k, b, step):
                rc = RC[:, k]
                if step == 0:
                    dve.wait_ge(cv_a, TA * (k + 1))
                    dve.wait_ge(cv_b, TB * (k + 1))
                    V.tensor_tensor(rc, rc, chain_b[:, b], ALU.add).then_inc(cv_join, 1)
                elif step == 1:
                    dve.wait_ge(cv_join, 2 * k + 1)
                    dve.wait_ge(cv_sum, (TP - 1) * (k + 1))
                    V.tensor_tensor(rc, rc, pool_sum[:, b], ALU.add).then_inc(cv_join, 1)
                elif step == 2:
                    dve.wait_ge(cv_join, 2 * k + 2)
                    dve.wait_ge(cv_mm, k + 1)
                    V.tensor_tensor(rc, rc, bank[4][:], ALU.add).then_inc(r_done, 1)
                else:
                    add_up(k + 16, 2, rc)

            def conv_body(it):
                for b in range(2):
                    k = 2 * it + b
                    dve.wait_ge(cv_pad, 1)
                    dve.wait_ge(cv_s, k + 1)
                    dve.wait_ge(gemm_done, 4 * it + 2 * b + N_CV1 + 2)
                    if not isinstance(it, int):
                        dve.wait_ge(cv_mm, k - 1)
                        dve.wait_ge(cv_prod, TP * (k - 1))
                    V.scalar_tensor_tensor(out=U[:, b, PAD:PAD + T], in0=bank[2 * b][:],
                                           scalar=vec[:, bass.ds(k + VEC["cv_b1"], 1)], in1=tb[:, 2 + b], op0=ALU.add,
                                           op1=ALU.mult).then_inc(cv_u, 1)
                    dve.wait_ge(cv_u, k + 1)
                    for tap in range(TA + TB):
                        w_ = vec[:, bass.ds(TAPS * k + VEC["cv_wdw"] + tap, 1)]
                        u_ = U[:, b, tap:tap + T]
                        i, in_b = divmod(tap, 2)
                        dst, done, n = (chain_b[:, b], cv_b, TB) if in_b else (RC[:, k], cv_a, TA)
                        if tap == 0:
                            ins = V.tensor_scalar(dst, u_, w_, vec[:, bass.ds(k + VEC["cv_bdw"], 1)], ALU.mult, ALU.add)
                        elif tap == 1:
                            ins = V.tensor_scalar(dst, u_, w_, None, ALU.mult)
                        else:
                            dve.wait_ge(done, n * k + i)
                            ins = V.scalar_tensor_tensor(out=dst, in0=u_, scalar=w_, in1=dst, op0=ALU.mult, op1=ALU.add)
                        ins.then_inc(done, 1)
                        if tap in (2, 5, 8, 11) and not (isinstance(k, int) and k == 0):
                            join(k - 1, (b + 1) % 2, tap // 3)

            conv_body(0)
            with dve.Fori(1, 4) as it:
                conv_body(it)
            for step in range(4):
                join(7, 1, step)
            ln(2, RC)
            with dve.Fori(0, 2) as it:
                for m in range(4):
                    dve.wait_ge(gemm_done, 4 * it + m + N_CV2 + 1)
                    dve.wait_ge(ln_x, 4 * it + m + 9)
                    residual(4 * it + m + 24, 3, bank[m % 2][:], mod[:, 1, bass.ds(4 * it + m + G1 * 8, 1)],
                             XA[:, 4 * it + m])
            ln(3, XA)
            up(1)
            dve.wait_ge(ln_x, 24)
            down(1)
            ln(4, XA)


def kernel(x, c, ctx, c_ctx, w_mod, b_mod, ln1_g, ln1_b, ln2_g, ln2_b, w_in_even, w_out_even, na_rpb, hg_lb,
           hg_norm_g, cv_w1, cv_b1, cv_wdw, cv_bdw, cv_ln_g, cv_ln_b, cv_w2, cv_b2, ffn_w1, ffn_w3, ffn_w2):
    import numpy as np
    import concourse.bacc as bacc
    from concourse.bass_utils import run_bass_kernel_spmd

    def features(a, n):
        return np.ascontiguousarray(np.asarray(a).T.reshape(-1, P, n).transpose(1, 0, 2))

    def columns(a):
        return np.asarray(a).reshape(-1, P).T

    def pieces(w):
        w = np.asarray(w)
        k, n = w.shape
        return np.ascontiguousarray(w.reshape(k // P, P, n // P, P).transpose(2, 1, 0, 3)).reshape(n // P, P, k)

    def interleave(a, b):
        return np.ascontiguousarray(np.stack([a, b], 1)).reshape((-1,) + a.shape[1:])

    w_in_t = pieces(w_in_even[0]).reshape(8, 4, P, D)[list(IN_ORDER)].reshape(32, P, D)
    cv1 = pieces(cv_w1[0])
    up_ = np.stack([interleave(pieces(ffn_w1[l]), pieces(ffn_w3[l])) for l in range(2)])
    vectors = np.concatenate([columns(a) for a in (b_mod, ln1_g, ln1_b, ln2_g, ln2_b, hg_norm_g, cv_b1, cv_bdw,
                                                   cv_ln_g, cv_ln_b, cv_b2)]
                             + [np.asarray(cv_wdw[0]).reshape(TAPS, 8, P).transpose(2, 1, 0).reshape(P, 8 * TAPS)], 1)

    qr, qc = np.divmod(np.arange(P), TILE_W)
    dr = np.arange(ROWS)[None, :] - qr[:, None] + ROWS - 1
    dc = np.clip(np.arange(WIN)[None, :] - TILE_W - qc[:, None] + TILE_W - 1, 0, 2 * TILE_W - 2)
    bias_t = np.ascontiguousarray(np.asarray(na_rpb)[0][:, dr[:, :, None], dc[:, None, :]].transpose(1, 0, 2, 3))
    mask = np.zeros((P, ROWS, 3, WIN), np.float32)
    for kind, (t, lo) in enumerate(((0, 0), (1, 0), (3, 2))):
        col = t * TILE_W + qc
        start = np.clip(col - TILE_W // 2, 0, COLS - TILE_W)
        kcol = lo * TILE_W + np.arange(WIN)
        seen = (kcol[None, :] >= start[:, None]) & (kcol[None, :] < start[:, None] + TILE_W)
        mask[:, :, kind, :] = np.where(seen, 0.0, -1e30)[:, None, :]
    lvl_t = np.zeros((P, 2, 7, P), np.float32)
    a = np.arange(P)
    for e, H in enumerate(LEVELS):
        same = a[:, None] // (2 * H) == a[None, :] // (2 * H)
        first = a // H % 2 == 0
        lvl_t[:, 0, e] = same & first[:, None] & ~first[None, :]
        lvl_t[:, 1, e] = same & ~first[:, None] & first[None, :]

    arrays = {
        "xT": features(x[0], T), "ctxT": features(ctx[0], TC),
        "cvec": np.ascontiguousarray(np.stack([columns(c[0]), columns(c_ctx)], 2)),
        "vecs": np.ascontiguousarray(vectors), "ident_d": np.eye(P, dtype=np.float32), "lvl_d": lvl_t,
        "bias_d": bias_t, "mask_d": mask,
        "wmod0": interleave(*pieces(w_mod[0][:, :2 * D]).reshape(2, KC, P, D)),
        "wmod": np.ascontiguousarray(np.asarray(w_mod).reshape(2, KC, P, 6, D).transpose(0, 3, 1, 2, 4))
        .reshape(12, KC, P, D),
        "w_in": w_in_t, "w_out": pieces(w_out_even[0]), "w_up": up_,
        "w_dn": np.stack([pieces(ffn_w2[0]), pieces(ffn_w2[1])]),
        "cv1": interleave(cv1[:8], cv1[8:]), "cv2": pieces(cv_w2[0]),
    }
    nc = bacc.Bacc("TRN2", target_bir_lowering=False, num_devices=1)
    args = [nc.dram_tensor(f"in_{k}", v.shape, mybir.dt.from_np(v.dtype), kind="ExternalInput").ap()
            for k, v in arrays.items()]
    args.append(nc.dram_tensor("out_y", (8, P, T), mybir.dt.float32, kind="ExternalOutput").ap())
    build(nc, *args)
    r = run_bass_kernel_spmd(nc, [{f"in_{k}": v for k, v in arrays.items()}], core_ids=[0])
    y = r.results[0]["out_y"]
    return np.ascontiguousarray(np.asarray(y).reshape(D, T).T)[None]
```

```python
import concourse.bass as bass
from concourse import mybir
from contextlib import ExitStack

P = 128
D = 1024
KC = D // P
T = 512
TC = 256
ROWS, COLS = 8, 64
NH, HD = 8, 64
HH = 4
CH = 128
NCH = T // CH
TILE_W = 16
NT = COLS // TILE_W
WIN = 3 * TILE_W
DFF = 2816
FC = DFF // P
TAPS = 31
PAD = TAPS // 2
TA, TB, TM, TP = 9, 8, 6, 8
TA7, TB7, TM7, TP7 = 5, 5, 12, 9
assert TA + TB + TM + TP == TAPS and TA7 + TB7 + TM7 + TP7 == TAPS
ALPHA = (2 * 2) ** 0.25
LN_EPS, RMS_EPS = 1e-5, 1e-6
LEVELS = [64, 32, 16, 8, 4, 2, 1]

N_OUT, N_UP0, N_DN0, N_CV1, N_CV2, N_UP1, N_DN1 = 32, 40, 84, 108, 124, 132, 176
DN_KC = (8, 7, 7)
IB, ZF, ZB, KA, VA, QB, QA, GB = range(8)
IN_ORDER = (4, 5, 6, 1, 2, 3, 0, 7)
OUT_ORDER = (4, 5, 6, 0, 1, 2, 3, 7)

VEC = {}
_at = 0
for _name, _n in (("b_mod", 96), ("ln1_g", 16), ("ln1_b", 16), ("ln2_g", 16), ("ln2_b", 16), ("hg_norm_g", 4),
                  ("cv_b1", 16), ("cv_bdw", 8), ("cv_ln_g", 8), ("cv_ln_b", 8), ("cv_b2", 8), ("cv_wdw", 8 * TAPS)):
    VEC[_name] = _at
    _at += _n
NVEC = _at

SH1, SC1, G1, SH2, SC2, G2 = range(6)


def build(nc, xT, ctxT, cvec, vecs, ident_d, lvl_d, bias_d, mask_d, w_sc1, wmod, w_in, w_out, w_up, w_dn, cv1, cv2,
          out):
    fp32, f32r, u8 = mybir.dt.float32, mybir.dt.float32r, mybir.dt.uint8
    ACT, ALU, AX = mybir.ActivationFunctionType, mybir.AluOpType, mybir.AxisListType

    stack = ExitStack()
    with stack:
        BASE = 16512
        CONST, RING = BASE, BASE + 8192
        H0 = RING + 32768
        REST = H0 + 49152
        TMP = REST + 94336

        def at(name, shape, offset, dt=fp32):
            return nc.alloc_sbuf_tensor_at(name, [P] + shape, dt, offset=offset)

        const_at = [CONST]

        def const(name, shape, dt=fp32):
            size = 1
            for s in shape:
                size *= s
            t = at(name, shape, const_at[0], dt)
            const_at[0] += -(-size * (1 if dt == u8 else 4) // 32) * 32
            assert const_at[0] <= RING
            return t

        vec = const("vec", [NVEC])
        ident = const("ident", [P])
        ones = const("ones", [P])
        ones_d = const("ones_d", [P])
        lvl = const("lvl", [2, 7, P], u8)
        cin = const("cin", [KC, 2])
        cact = const("cact", [KC, 2])
        mod0 = const("mod0", [KC, 2, 2])
        mod0p = const("mod0p", [KC, 2])
        mod = const("mod", [2, 48])
        modp = const("modp", [2, 48])
        norm = const("norm", [5, 5, 8])
        neg_half = const("neg_half", [4])
        mxc = const("mxc", [2, 4])
        sml = const("sml", [2, 2])
        rsum = const("rsum", [2, 8])
        rinv = const("rinv", [2, 8])
        gam = const("gam", [2, 4])
        msq = const("msq", [3, 4])

        raw = at("raw", [4, KC * P], RING)
        whi = at("whi", [2, KC * P], RING + 16384, f32r)
        wlo = at("wlo", [2, KC * P], RING + 24576, f32r)
        h_hi = at("h_hi", [KC, T], H0, f32r)
        h_lo = at("h_lo", [KC, T], H0 + 16384, f32r)
        hc_hi = at("hc_hi", [KC, TC], H0 + 32768, f32r)
        hc_lo = at("hc_lo", [KC, TC], H0 + 40960, f32r)
        sc_w = at("sc_w", [KC, KC * P], REST)
        sh_w = at("sh_w", [KC, D], REST + 32768)
        sh_acc = at("sh_acc", [2, D], TMP)
        mod_blk0 = at("mod_blk0", [2, D], REST)
        mod_acc0 = at("mod_acc0", [D], REST + 8192)
        KEY = at("KEY", [8, T], REST + 16384)
        PRE = at("PRE", [8, NCH, CH + 1], REST + 32768)
        QBt = at("QBt", [HH, T], REST + 49280)
        VI = at("VI", [NCH, 512], REST + 57472)
        VIC = at("VIC", [2, 512], REST + 65664)
        VAt = at("VAt", [NT, 512], REST + 69760)
        VAC = at("VAC", [2, 512], REST + 77952)
        KT_ = at("KT_", [4, T], REST + 82048)
        KTC = at("KTC", [4, TC], REST + 90240)
        xin = at("xin", [KC, T], REST + 69760)
        cxin = at("cxin", [KC, TC], REST + 86144)
        Qt = at("Qt", [4, T], H0 + 32768)
        GBt = at("GBt", [4, T], H0 + 40960)
        S0 = at("S0", [8, P], TMP)
        t1_ = TMP + 4096
        lvl_f = at("lvl_f", [2, 7, P], t1_ + 4096)
        VT = at("VT", [T + TC], t1_)
        ab = at("ab", [T + TC], t1_ + 3072)
        soft = at("soft", [T + TC], t1_ + 6144)
        ls = at("ls", [T + TC], t1_ + 9216)
        keyc = at("keyc", [TC], t1_ + 12288)
        prec = at("prec", [TC + 1], t1_ + 13312)
        Ec = at("Ec", [TC], t1_ + 14368)
        Kdc = at("Kdc", [TC], t1_ + 15392)
        KcT = at("KcT", [2, P], t1_ + 16416)
        bias = at("bias", [NH, ROWS, WIN], REST)
        mask0 = at("mask0", [ROWS, 2 * TILE_W], REST + 12288)
        mask1 = at("mask1", [ROWS, WIN], REST + 13312)
        mask3 = at("mask3", [ROWS, 2 * TILE_W], REST + 14848)
        EX = at("EX", [4, NCH, CH], H0)
        QD = at("QD", [2, NCH, CH], H0 + 8192)
        AT = at("AT", [2, NCH, CH], H0 + 12288)
        OT = at("OT", [8, T], H0 + 16384)
        St = at("St", [2, 3, P], REST + 65664)
        comb = at("comb", [2, ROWS * WIN], t1_)
        Ssb = at("Ssb", [2, ROWS * WIN], t1_ + 3072)
        Pb = at("Pb", [2, 5 * P], t1_ + 6144)
        PTb = at("PTb", [2, 5 * P], t1_ + 11264)
        Osb = at("Osb", [NH, HD], t1_ + 16384)
        KD = at("KD", [NCH, CH], t1_ + 18432)
        KDT = at("KDT", [3, P], t1_ + 20480)
        ON = at("ON", [NCH, CH], t1_ + 22016)
        XA = at("XA", [8, T], REST)
        mod_blk1 = at("mod_blk1", [2, D], H0 + 32768)
        mod_acc1 = at("mod_acc1", [D], H0 + 40960)
        A_hi = at("A_hi", [FC, T], REST + 16384, f32r)
        A_lo = at("A_lo", [FC, T], REST + 16384 + 45056, f32r)
        U = at("U", [2, T + 2 * PAD], REST + 16384)
        RC = at("RC", [8, T], REST + 16384 + 8192)
        chain_b = at("chain_b", [2, T], REST + 40960)
        pool_sum = at("pool_sum", [2, T], REST + 45056)
        prod = at("prod", [TP7, T], REST + 49152)
        diag = at("diag", [2, TM, P], REST + 67584)
        diag7 = at("diag7", [TM7, P], REST + 73728)
        tb = at("tb", [4, T], REST + 106496)
        acc = at("acc", [2, T], REST + 114688)
        rstd_a = at("rstd_a", [T], REST + 118784)
        rstd_b = at("rstd_b", [T], REST + 83968)
        lt = at("lt", [2, T], H0 + 45056)

        bank = [stack.enter_context(nc.psum_tensor(f"bank{i}", [P, 512], fp32)) for i in range(8)]

        def sem(name):
            return stack.enter_context(nc.semaphore(name))

        table_in, lvl_done = sem("table_in"), sem("lvl_done")
        raw_in = [sem(f"raw_in{i}") for i in range(4)]
        sc_in = [sem(f"sc_in{i}") for i in range(KC)]
        mod_in = [sem(f"mod_in{i}") for i in range(2)]
        (mod0_done, blk_done, part_done, half_done, hi_first, lo_first, sh_done, sh_mm, hxc_done, hhic_done,
         hloc_done) = [sem(n) for n in ("mod0_done", "blk_done", "part_done", "half_done", "hi_first", "lo_first",
                                        "sh_done", "sh_mm", "hxc_done", "hhic_done", "hloc_done")]
        sh_in = [sem(f"sh_in{i}") for i in range(KC)]
        cx_in = sem("cx_in")
        (hi_done, lo_done, gemm_done, mod_done, const_in, x_in, bias_in, xa_in, out_done, ones_set, cact_done,
         modv_done, mchain, hx_done, hhi_done, hlo_done) = [sem(n) for n in (
             "hi_done", "lo_done", "gemm_done", "mod_done", "const_in", "x_in", "bias_in", "xa_in", "out_done",
             "ones_set", "cact_done", "modv_done", "mchain", "hx_done", "hhi_done", "hlo_done")]
        (evac_act, evac_dve, vt_tr, vx_done, vc_done, z_exp, z_ln, z_ls, z_d, z_key, z_pre, z_ec, z_kd,
         z_tr, z_kt, z_mm, z_s0) = [sem(n) for n in (
             "evac_act", "evac_dve", "vt_tr", "vx_done", "vc_done", "z_exp", "z_ln", "z_ls", "z_d",
             "z_key", "z_pre", "z_ec", "z_kd", "z_tr", "z_kt", "z_mm", "z_s0")]
        (n_comb, n_s, n_mc, n_mx, n_neg, n_exp, n_sum, n_tr, n_ptl, n_ptc, n_pv, n_inv, n_osb, n_otr, n_ot) = [
            sem(n) for n in ("n_comb", "n_s", "n_mc", "n_mx", "n_neg", "n_exp", "n_sum", "n_tr", "n_ptl", "n_ptc",
                             "n_pv", "n_inv", "n_osb", "n_otr", "n_ot")]
        (g_sub, g_exp, g_x, g_mm, g_at, g_e2, g_kd, g_ktr, g_kdt, g_ds, g_st, g_o, g_qd, g_gam, g_sq, g_ms, g_mse,
         g_pow, g_on,
         g_onr, g_ot) = [sem(n) for n in ("g_sub", "g_exp", "g_x", "g_mm", "g_at", "g_e2", "g_kd", "g_ktr",
                                          "g_kdt", "g_ds", "g_st", "g_o", "g_qd", "g_gam", "g_sq", "g_ms", "g_mse", "g_pow", "g_on",
                                          "g_onr", "g_ot")]
        (xa_done, oh_hi, oh_lo) = [sem(n) for n in ("xa_done", "oh_hi", "oh_lo")]
        (r_done, sq_done, rs_done, qs_done, acc_zero, st_mean, st_sq, ln_vec, ln_mu, ln_m2, ln_var, ln_v, ln_l,
         ln_rstd, ln_d, ln_t, ln_h, ln_hi, ln_lo, ln_ax, ln_x) = [sem(n) for n in (
             "r_done", "sq_done", "rs_done", "qs_done", "acc_zero", "st_mean", "st_sq", "ln_vec", "ln_mu", "ln_m2",
             "ln_var", "ln_v", "ln_l", "ln_rstd", "ln_d", "ln_t", "ln_h", "ln_hi", "ln_lo", "ln_ax", "ln_x")]
        ln_d_pool, ln_t0, ln_h0 = sem("ln_d_pool"), sem("ln_t0"), sem("ln_h0")
        (up_s, up_a, up_hi, up_lo, cv_s, cv_u, cv_pad, cv_a, cv_b, cv_diag, cv_mm, cv_prod, cv_sum, cv_join) = [
            sem(n) for n in ("up_s", "up_a", "up_hi", "up_lo", "cv_s", "cv_u", "cv_pad", "cv_a", "cv_b", "cv_diag",
                             "cv_mm", "cv_prod", "cv_sum", "cv_join")]

        HALF = (slice(0, T // 2), slice(T // 2, T))

        def rstd_of(k):
            return rstd_b if k == 1 else rstd_a

        def taps_of(k):
            return (TA7, TB7, TM7, TP7) if isinstance(k, int) and k == 7 else (TA, TB, TM, TP)

        def norm_buf(j):
            return (tb[:, 0], tb[:, 1], lt[:, 0], lt[:, 1])[j % 4]

        block = stack.enter_context(nc.Block())

        def load_piece(eng, g, j, src, cols, first=False):
            if not first:
                eng.wait_ge(lo_done, 4 * g + j - 3)
            eng.dma_start(raw[:, j, 0:cols], src).then_inc(raw_in[j], 16)

        def split_hi(eng, g, j, first=False):
            if j >= 4:
                g, j = g + 1, j - 4
            eng.wait_ge(raw_in[j], 16 * (g + 1))
            if not first:
                eng.wait_ge(gemm_done, 4 * g + j - 1)
            nc.scalar.activation(whi[:, j % 2], raw[:, j], ACT.Copy).then_inc(hi_done, 1)

        def split_lo(eng, g, j):
            if j >= 4:
                g, j = g + 1, j - 4
            eng.wait_ge(hi_done, 4 * g + j + 1)
            nc.gpsimd.tensor_tensor(wlo[:, j % 2], raw[:, j], whi[:, j % 2].bitcast(fp32),
                                    ALU.subtract).then_inc(lo_done, 1)

        def half(n, h):
            w = slice(h * KC // 2 * P, (h + 1) * KC // 2 * P)
            return whi[:, n % 2, w], wlo[:, n % 2, w], raw[:, n % 4, w]

        def split_hi_halves(eng, n0, pair):
            for h in range(2):
                for n in (n0 + 2, n0 + 3):
                    hi, _, src = half(n, h)
                    if h == 0:
                        eng.wait_ge(raw_in[n % 4], 16 * (n // 4 + 1))
                        eng.wait_ge(half_done, pair + 1)
                    else:
                        eng.wait_ge(gemm_done, n - 1)
                    nc.scalar.activation(hi, src, ACT.Copy).then_inc(hi_done if h else hi_first, 1)

        def split_lo_halves(eng, n0, pair):
            for h in range(2):
                for n in (n0 + 2, n0 + 3):
                    hi, lo, src = half(n, h)
                    if h == 0:
                        eng.wait_ge(hi_first, 2 * pair + n - n0 - 1)
                    else:
                        eng.wait_ge(hi_done, n + 1)
                    nc.gpsimd.tensor_tensor(lo, src, hi.bitcast(fp32), ALU.subtract).then_inc(
                        lo_done if h else lo_first, 1)

        def gemm(dst, j, rhs_hi, rhs_lo, cols, kcs, first=True, last=True):
            n = len(kcs)
            for i, kc in enumerate(kcs):
                w_h, w_l = (w[:, j % 2, i * P:(i + 1) * P] for w in (whi, wlo))
                nc.tensor.matmul(dst, w_h, rhs_hi[:, kc, 0:cols], start=(first and i == 0), stop=False)
                nc.tensor.matmul(dst, w_h, rhs_lo[:, kc, 0:cols], start=False, stop=False)
                mm = nc.tensor.matmul(dst, w_l, rhs_hi[:, kc, 0:cols], start=False, stop=(last and i == n - 1))
            return mm

        def load_block(sp, half, j, layer, part, kc, first=False):
            if not first:
                sp.wait_ge(blk_done, 2 * half + j - 1)
            sp.dma_start((mod_blk1 if layer else mod_blk0)[:, j], wmod[6 * layer + part, kc]).then_inc(mod_in[j], 16)

        def blocks_at(n):
            return [n] if n < 16 else [2 * n - 16, 2 * n - 15] if n < 24 else []

        def add_block(eng, half, j, layer, kc, part_no=None, start=True):
            blk, dst = (mod_blk1, mod_acc1) if layer else (mod_blk0, mod_acc0)
            eng.wait_ge(mod_in[j], 16 * (half + 1))
            if start and isinstance(kc, int) and kc == 0:
                if part_no is not None:
                    eng.wait_ge(part_done, part_no)
                nc.vector.tensor_scalar(dst[:], blk[:, j], cact[:, 0, 0:1], None, ALU.mult).then_inc(blk_done, 1)
            else:
                eng.wait_ge(blk_done, 2 * half + j)
                c_ = cact[:, kc, 0:1] if isinstance(kc, int) else cact[:, bass.ds(kc, 1), 0]
                nc.vector.scalar_tensor_tensor(out=dst[:], in0=blk[:, j], scalar=c_, in1=dst[:], op0=ALU.mult,
                                               op1=ALU.add).then_inc(blk_done, 1)

        def reduce_part(pe, blocks, layer, col):
            pe.wait_ge(blk_done, blocks)
            dst = mod_acc1 if layer else mod_acc0
            for f in range(8):
                o = bank[7][:, col + f:col + f + 1] if isinstance(col, int) else bank[7][:, bass.ds(col + f, 1)]
                mm = nc.tensor.matmul(o, dst[:, f * P:(f + 1) * P], ones[:, 0:1], start=True, stop=True)
            mm.then_inc(part_done, 1)

        N_CTX = 20
        v_tile = [0, 1, 2, 3, 16, 17, 18, 19]

        def dve_read(eng, n):
            if 4 <= n < 12:
                eng.wait_ge(z_d, n - 3)
            elif n < N_CTX:
                eng.wait_ge(evac_dve, n + 1 if n < 4 else n - 7)

        UNITS = [(t, h) for t in range(NT) for h in range(NH)]
        KIND_MASK = [mask0, mask1, mask1, mask3]

        def window(t):
            lo = max(t - 1, 0)
            return lo, min(t + 2, NT) - lo

        NITEM = 8 * 8
        NSLOT = NITEM + 16

        def hg(s):
            u, e = divmod(s, 8)
            head, d = divmod(u, 2)
            return u, e, d, head, d * HH + head

        def product_bank(k):
            return 6 if k % 2 and not (k >= 16 and k % 16 <= 5) else 5

        def halves(e):
            H = LEVELS[e - 1]
            return CH // (2 * H), H

        def prefix(i, d):
            return PRE[:, i, :, 1:CH + 1] if d == 0 else PRE[:, i, :, 0:CH]

        @block.sync
        def _(sp):
            sp.dma_start(cin[:], cvec).then_inc(const_in, 16)
            sp.dma_start(vec[:], vecs).then_inc(const_in, 16)
            def load_sc(lo, hi):
                for q in range(lo, hi):
                    sp.dma_start(sc_w[:, q], w_sc1[q]).then_inc(sc_in[q], 16)

            def load_sh(lo, hi):
                for q in range(lo, hi):
                    sp.dma_start(sh_w[:, q], wmod[SH1, q]).then_inc(sh_in[q], 16)

            def load_bias():
                sp.wait_ge(part_done, 4)
                sp.dma_start(bias[:], bias_d).then_inc(bias_in, 16)
                sp.dma_start(mask0[:], mask_d[:, :, 0, 0:2 * TILE_W]).then_inc(bias_in, 16)
                sp.dma_start(mask1[:], mask_d[:, :, 1, :]).then_inc(bias_in, 16)
                sp.dma_start(mask3[:], mask_d[:, :, 2, 0:2 * TILE_W]).then_inc(bias_in, 16)

            load_sc(0, 2)
            load_sh(0, 2)
            load_sc(2, 4)
            load_sh(2, 6)
            load_sc(4, 6)
            load_sh(6, 8)
            load_sc(6, 8)
            sp.dma_start(xin[:], xT).then_inc(x_in, 16)
            for n in range(2):
                load_piece(sp, 0, n, w_in[n], KC * P, first=True)
            sp.dma_start(cxin[:], ctxT).then_inc(cx_in, 16)
            sp.dma_start(ident[:], ident_d).then_inc(table_in, 16)
            sp.dma_start(lvl_f[:], lvl_d).then_inc(table_in, 16)
            for n in range(2, 32):
                load_piece(sp, n // 4, n % 4, w_in[n], KC * P, first=n < 4)
                if n == 3:
                    sp.wait_ge(mod0_done, KC)
                for q in blocks_at(n - 3) if n >= 3 else ():
                    load_block(sp, q // 2, q % 2, 0, 2 + q // 8, q % 8, first=q < 2)
                if n == 30:
                    load_bias()
            for n in range(4):
                load_piece(sp, N_OUT // 4, n, w_out[n], KC * P)
            sp.wait_ge(n_comb, len(UNITS))
            sp.dma_start(XA[:], xT).then_inc(xa_in, 16)
            for n in range(4, 8):
                load_piece(sp, N_OUT // 4 + 1, n % 4, w_out[n], KC * P)
            sp.wait_ge(oh_lo, 8)
            def up0():
                for j in range(4):
                    load_piece(sp, N_UP0 // 4, j, w_up[0, j], KC * P)
                with sp.Fori(0, 5) as it:
                    for j in range(8):
                        load_piece(sp, 2 * it + N_UP0 // 4 + 1 + j // 4, j % 4, w_up[0, 8 * it + 4 + j], KC * P)
                        load_block(sp, 4 * it + 16 + j // 2, j % 2, 1, it, j)

            def up1():
                with sp.Fori(0, 11) as it:
                    for j in range(4):
                        load_piece(sp, it + N_UP1 // 4, j, w_up[1, 4 * it + j], KC * P)

            def down(layer):
                with sp.Fori(0, 2) as it:
                    for j in range(12):
                        if layer == 0 and j % 3 == 0:
                            load_block(sp, 2 * it + 36 + j // 6, j // 3 % 2, 1, 5, 4 * it + j // 3)
                        k0 = sum(DN_KC[:j % 3]) * P
                        cols = DN_KC[j % 3] * P
                        load_piece(sp, 3 * it + (N_DN1 if layer else N_DN0) // 4 + j // 4, j % 4,
                                   w_dn[layer, 4 * it + j // 3, :, k0:k0 + cols], cols)

            up0()
            down(0)
            with sp.Fori(0, 4) as it:
                for j in range(4):
                    load_piece(sp, it + N_CV1 // 4, j, cv1[4 * it + j], KC * P)
            with sp.Fori(0, 2) as it:
                for j in range(4):
                    load_piece(sp, it + N_CV2 // 4, j, cv2[4 * it + j], KC * P)
            up1()
            down(1)
            for j in range(8):
                sp.wait_ge(ln_x, 24 + j + 1)
                sp.dma_start(out[j], XA[:, j]).then_inc(out_done, 16)
            sp.wait_ge(out_done, 16 * 8)

        @block.gpsimd
        def _(pool):
            nc.gpsimd.memset(ones_d[:], 1.0 / D)
            nc.gpsimd.memset(ones[:], 1.0).then_inc(ones_set, 1)
            for n in range(2):
                split_lo(pool, 0, n)
            pool.wait_ge(table_in, 32)
            nc.gpsimd.tensor_copy(lvl[:], lvl_f[:]).then_inc(lvl_done, 1)
            for n in range(32):
                split_lo(pool, (n + 2) // 4, (n + 2) % 4)
            pool.wait_ge(gemm_done, 32)
            pool.wait_ge(bias_in, 64)
            for s in range(NSLOT):
                if s % 2 == 0 and s // 2 < len(UNITS):
                    w = s // 2
                    t, h = UNITS[w]
                    _, nl = window(t)
                    off = TILE_W if t == 0 else 0
                    if w >= 2:
                        pool.wait_ge(n_mx, w - 1)
                    dst = comb[:, w % 2, 0:ROWS * nl * TILE_W].rearrange("p (r c) -> p r c", r=ROWS)
                    nc.gpsimd.tensor_tensor(dst, bias[:, h, :, off:off + nl * TILE_W], KIND_MASK[t][:],
                                            ALU.add).then_inc(n_comb, 1)
                k = s - 2
                if 0 <= k < NITEM:
                    u, e, d, head, i = hg(k)
                    pool.wait_ge(g_exp, k + 1)
                    if e == 0:
                        b = EX[:, k % 4]
                        q_ = QBt[:, head].rearrange("p (c t) -> p c t", c=NCH)
                        k_ = KEY[:, i].rearrange("p (c t) -> p c t", c=NCH)
                        if u >= 1:
                            pool.wait_ge(g_ktr, u)
                        if d == 0:
                            nc.gpsimd.tensor_tensor(KD[:], b, k_, ALU.mult).then_inc(g_kd, 1)
                        else:
                            if head >= 1:
                                pool.wait_ge(g_o, head)
                            pool.wait_ge(g_e2, u + 1)
                            nc.gpsimd.tensor_tensor(QD[:, 1], b, q_, ALU.mult).then_inc(g_qd, 1)
                            nc.gpsimd.tensor_tensor(KD[:], KD[:], k_, ALU.mult).then_inc(g_kd, 1)
                    else:
                        nb, H = halves(e)
                        b = EX[:, k % 4].rearrange("p c t -> p (c t)").rearrange("p (b two h) -> p b two h", two=2, h=H)
                        q_ = QBt[:, head].rearrange("p (b two h) -> p b two h", two=2, h=H)
                        k_ = KEY[:, i].rearrange("p (b two h) -> p b two h", two=2, h=H)
                        first, second = (k_, q_) if d == 0 else (q_, k_)
                        nc.gpsimd.tensor_tensor(b[:, :, 0], b[:, :, 0], first[:, :, 0], ALU.mult)
                        nc.gpsimd.tensor_tensor(b[:, :, 1], b[:, :, 1], second[:, :, 1], ALU.mult).then_inc(g_x, 1)
                k = s - 6
                if 0 <= k < NITEM and k % 16 == 0:
                    u, e, d, head, i = hg(k)
                    pool.wait_ge(g_e2, u + 1)
                    q_ = QBt[:, head].rearrange("p (c t) -> p c t", c=NCH)
                    nc.gpsimd.tensor_tensor(QD[:, 0], QD[:, 0], q_, ALU.mult).then_inc(g_qd, 1)
                k = s - 8
                if k >= 0 and k % 16 == 15 and k < NITEM:
                    hd_ = k // 16
                    pool.wait_ge(g_mse, hd_ + 1)
                    nc.gpsimd.tensor_tensor(msq[:, 2], msq[:, 1], neg_half[:], ALU.pow).then_inc(g_pow, 1)

            def ln(k):
                for j in range(8):
                    pool.wait_ge(ln_hi, 8 * k + j + 1)
                    nc.gpsimd.tensor_tensor(h_lo[:, j], norm_buf(j), h_hi[:, j].bitcast(fp32),
                                            ALU.subtract).then_inc(ln_lo, 1)
                split_lo_halves(pool, (N_UP0, N_CV1, N_CV2, N_UP1)[k], k + 1)

            def sum_sq(k, count):
                pool.wait_ge(sq_done, count + 1)
                pool.wait_ge(qs_done, count - k)
                pool.wait_ge(acc_zero, k + 1)
                nc.gpsimd.tensor_tensor(acc[:, 1], acc[:, 1], tb[:, 0], ALU.add).then_inc(qs_done, 1)

            split_lo_halves(pool, N_OUT, 0)
            for n in range(2, 8):
                split_lo(pool, N_OUT // 4 + n // 4, n % 4 + 2)
            ln(0)

            def up(layer):
                for j in range(2, 4):
                    split_lo(pool, (N_UP1 if layer else N_UP0) // 4, j + 2)
                with pool.Fori(1, 11) as it:
                    for j in range(4):
                        split_lo(pool, it + (N_UP1 if layer else N_UP0) // 4, j + 2)

            def down_body(layer, it, last=False):
                for j in range(12):
                    if not (last and j >= 10):
                        split_lo(pool, 3 * it + (N_DN1 if layer else N_DN0) // 4 + j // 4, j % 4 + 2)

            up(0)
            with pool.Fori(0, 2) as it:
                down_body(0, it)
            ln(1)

            def cv1_body(it):
                for b in range(2):
                    k = 2 * it + b
                    if not (isinstance(k, int) and k == 0):
                        split_lo(pool, it + N_CV1 // 4, 2 * b + 2)
                        split_lo(pool, it + N_CV1 // 4, 2 * b + 3)
                    for a in range(taps_of(k)[3] - 1):
                        pool.wait_ge(cv_prod, TP * k + a + 2)
                        if a == 0:
                            if not (isinstance(k, int) and k < 2):
                                pool.wait_ge(cv_join, 2 * k - 2)
                            ins = nc.gpsimd.tensor_tensor(pool_sum[:, b], prod[:, 0], prod[:, 1], ALU.add)
                        else:
                            pool.wait_ge(cv_sum, (TP - 1) * k + a)
                            ins = nc.gpsimd.tensor_tensor(pool_sum[:, b], pool_sum[:, b], prod[:, a + 1], ALU.add)
                        ins.then_inc(cv_sum, 1)
                    if not (isinstance(k, int) and k == 0):
                        sum_sq(2, k + 15)

            cv1_body(0)
            with pool.Fori(1, 3) as it:
                cv1_body(it)
            cv1_body(3)
            ln(2)
            for n in range(2, 8):
                split_lo(pool, N_CV2 // 4 + n // 4, n % 4 + 2)
            ln(3)
            up(1)
            down_body(1, 0)
            down_body(1, 1, last=True)
            pool.wait_ge(ln_mu, 5)
            pool.wait_ge(st_sq, 5)
            for j in range(3, 8):
                nc.gpsimd.tensor_tensor(XA[:, j], XA[:, j], tb[:, 2], ALU.subtract).then_inc(ln_d_pool, 1)

        @block.tensor
        def _(pe):
            pe.wait_ge(cact_done, 1)
            pe.wait_ge(ones_set, 1)

            def sc_tiles(lo, hi):
                for q in range(lo, hi):
                    pe.wait_ge(sc_in[q], 16)
                    for kc in range(KC):
                        mm = nc.tensor.matmul(bank[q][:, 2:4], sc_w[:, q, kc * P:(kc + 1) * P], cact[:, kc, :],
                                              start=(kc == 0), stop=(kc == KC - 1))
                    mm.then_inc(mod_done, 1)

            sc_tiles(0, 6)
            pe.wait_ge(sh_done, 2 * KC)
            for q in range(KC):
                for c in range(2):
                    mm = nc.tensor.matmul(bank[q][:, c:c + 1], sh_acc[:, c, q * P:(q + 1) * P], ones[:, 0:1],
                                          start=True, stop=True)
            mm.then_inc(sh_mm, 1)
            sc_tiles(6, 8)
            pe.wait_ge(table_in, 32)

            def v_transposes(v):
                pe.wait_ge(evac_act, v_tile[v] + 1)
                dve_read(pe, v_tile[v])
                if v == 4:
                    pe.wait_ge(z_s0, 8)
                if v >= 1:
                    pe.wait_ge(vx_done, v)
                    pe.wait_ge(vc_done, v)
                for c in range(4):
                    nc.tensor.transpose(bank[4][:, c * P:(c + 1) * P], VT[:, c * P:(c + 1) * P], ident[:])
                for c in range(2):
                    mm = nc.tensor.transpose(bank[5][:, c * P:(c + 1) * P], VT[:, T + c * P:T + (c + 1) * P], ident[:])
                mm.then_inc(vt_tr, 1)

            def z_transpose(i):
                pe.wait_ge(z_kd, i + 1)
                if i >= 1:
                    pe.wait_ge(z_kt, i)
                for c in range(2):
                    mm = nc.tensor.transpose(bank[6][:, c * P:(c + 1) * P], Kdc[:, c * P:(c + 1) * P], ident[:])
                mm.then_inc(z_tr, 1)

            def z_state(i):
                pe.wait_ge(z_kt, i + 1)
                pe.wait_ge(vx_done, 4)
                pe.wait_ge(vc_done, 4)
                if i >= 1:
                    pe.wait_ge(z_s0, i)
                head = i % HH
                for c in range(2):
                    mm = nc.tensor.matmul(bank[4][:, 0:P], KcT[:, c], VIC[:, c, head * P:(head + 1) * P],
                                          start=(c == 0), stop=(c == 1))
                mm.then_inc(z_mm, 1)

            for n in range(32):
                kind = n // 4
                pe.wait_ge(lo_done, n + 1)
                if n >= 2:
                    pe.wait_ge(evac_act, n - 1)
                    dve_read(pe, n - 2)
                if n == 0:
                    for kc in range(KC):
                        pe.wait_ge(hlo_done, kc + 1)
                        w = slice(kc * P, (kc + 1) * P)
                        nc.tensor.matmul(bank[0][:], whi[:, 0, w], h_hi[:, kc], start=(kc == 0), stop=False)
                        nc.tensor.matmul(bank[0][:], whi[:, 0, w], h_lo[:, kc], start=False, stop=False)
                        nc.tensor.matmul(bank[0][:], wlo[:, 0, w], h_hi[:, kc], start=False, stop=(kc == KC - 1))
                    pe.wait_ge(hloc_done, KC)
                else:
                    mm = gemm(bank[n % 2][:], n, h_hi, h_lo, T, range(KC))
                if kind <= VA:
                    mm = gemm(bank[2 + n % 2][:, 0:TC], n, hc_hi, hc_lo, TC, range(KC))
                mm.then_inc(gemm_done, 1)
                for q in blocks_at(n):
                    if q % 8 == 7:
                        reduce_part(pe, q + 1, 0, q + 1)
                if n - 1 in v_tile:
                    v_transposes(v_tile.index(n - 1))
                if 6 <= n <= 13:
                    z_state(n - 6)
                if 5 <= n <= 12:
                    z_transpose(n - 5)

            def first_pair(n0, hi_ready, lo_ready, count, order=range(KC), i0=0, i1=KC):
                pe.wait_ge(lo_done, n0 + 2)
                for i in range(i0, i1):
                    kc = order[i]
                    w = slice(i * P, (i + 1) * P)
                    pe.wait_ge(hi_ready, count + i + 1)
                    for b in range(2):
                        nc.tensor.matmul(bank[b][:], whi[:, b, w], h_hi[:, kc], start=(i == 0), stop=False)
                        nc.tensor.matmul(bank[b][:], wlo[:, b, w], h_hi[:, kc], start=False, stop=False)
                    pe.wait_ge(lo_ready, count + i + 1)
                    for b in range(2):
                        mm = nc.tensor.matmul(bank[b][:], whi[:, b, w], h_lo[:, kc], start=False, stop=(i == KC - 1))
                        if i == KC - 1:
                            mm.then_inc(gemm_done, 1)
                    if i == KC // 2 - 1:
                        mm.then_inc(half_done, 1)

            pe.wait_ge(evac_act, 32)
            pe.wait_ge(vx_done, 8)
            pe.wait_ge(vc_done, 8)
            pe.wait_ge(z_s0, 8)
            pe.wait_ge(modv_done, 1)
            B_SL, B_SC, B_PL, B_PC, B_O, B_HA, B_HO, B_HT = bank
            for s in range(NSLOT):
                k = s - 5
                if 0 <= k < NITEM and k % 16 == 15:
                    hd_ = k // 16
                    pe.wait_ge(g_at, k + 1)
                    if hd_ >= 1:
                        pe.wait_ge(g_on, hd_)
                    pe.wait_ge(g_st, 3 * 2 * (hd_ + 1))
                    pe.wait_ge(g_qd, 2 * (hd_ + 1))
                    for c in range(NCH):
                        v_ = VI[:, c, hd_ * P:(hd_ + 1) * P]
                        dst = B_HO[:, c * P:(c + 1) * P]
                        nc.tensor.matmul(dst, AT[:, 0, c], v_, start=True, stop=False)
                        nc.tensor.matmul(dst, AT[:, 1, c], v_, start=False, stop=False)
                        sf = S0[:, hd_] if c == 0 else St[:, 0, c - 1]
                        sb_ = S0[:, HH + hd_] if c == 3 else St[:, 1, 2 - c]
                        nc.tensor.matmul(dst, QD[:, 0, c], sf, start=False, stop=False)
                        mm = nc.tensor.matmul(dst, QD[:, 1, c], sb_, start=False, stop=True)
                    mm.then_inc(g_o, 1)
                k = s - 3
                if 0 <= k < NITEM:
                    u, e, d, head, i = hg(k)
                    b_ = bank[product_bank(k)]
                    before = [q for q in range(k) if product_bank(q) == product_bank(k)]
                    if before:
                        pe.wait_ge(g_at, before[-1] + 1)
                    if k >= 16 and product_bank(k) == 6:
                        pe.wait_ge(g_on, (k - 6) // 16)
                    if e == 0:
                        for c in range(NCH):
                            mm = nc.tensor.matmul(b_[:, c * P:(c + 1) * P], KEY[:, i, c * P:(c + 1) * P],
                                                  QBt[:, head, c * P:(c + 1) * P], start=True, stop=True)
                        mm.then_inc(g_mm, 1)
                    else:
                        pe.wait_ge(g_x, k - u)
                        for c in range(NCH):
                            x_ = EX[:, k % 4, c]
                            mm = nc.tensor.matmul(b_[:, c * P:(c + 1) * P], x_, x_, start=True, stop=True)
                        mm.then_inc(g_mm, 1)
                if s >= 21 and (s - 21) % 16 == 0 and (s - 21) // 16 < NT:
                    t = (s - 21) // 16
                    pe.wait_ge(n_osb, t + 1)
                    pe.wait_ge(n_ptl, min(8 * t + 9, len(UNITS)))
                    for g in range(4):
                        mm = nc.tensor.transpose(B_PL[:, g * P:(g + 1) * P],
                                                 Osb[:, 2 * g:2 * g + 2].rearrange("p a b -> p (a b)"), ident[:])
                    mm.then_inc(n_otr, 1)
                if s % 2 == 0 and s // 2 < len(UNITS):
                    w = s // 2
                    t, h = UNITS[w]
                    lo, nl = window(t)
                    part = slice(HD * (h % 2), HD * (h % 2) + HD)
                    if w >= 1:
                        pe.wait_ge(n_mx, w)
                        pe.wait_ge(n_exp, w)
                    q_ = Qt[part, h // 2, t * P:(t + 1) * P]
                    k_ = KT_[part, h // 2].rearrange("p (r c) -> p r c", r=ROWS)[:, :, lo * TILE_W:(lo + nl) * TILE_W]
                    nc.tensor.matmul(B_SL[:, 0:ROWS * nl * TILE_W].rearrange("p (r c) -> p r c", r=ROWS), q_, k_,
                                     start=True, stop=True)
                    nc.tensor.matmul(B_SC[:, 0:TC], q_, KTC[part, h // 2], start=True, stop=True).then_inc(n_s, 1)
                if (s - 3) % 2 == 0 and 0 <= (s - 3) // 2 < len(UNITS):
                    w = (s - 3) // 2
                    _, nl = window(UNITS[w][0])
                    pe.wait_ge(n_exp, w + 1)
                    if w >= 1:
                        pe.wait_ge(n_ptl, w)
                        pe.wait_ge(n_ptc, w)
                    if w >= 9:
                        pe.wait_ge(n_ot, (w - 1) // 8)
                    for c in range(nl):
                        nc.tensor.transpose(B_PL[:, c * P:(c + 1) * P], Pb[:, w % 2, c * P:(c + 1) * P], ident[:])
                    for c in range(2):
                        mm = nc.tensor.transpose(B_PC[:, c * P:(c + 1) * P],
                                                 Pb[:, w % 2, (3 + c) * P:(4 + c) * P], ident[:])
                    mm.then_inc(n_tr, 1)
                if (s - 5) % 2 == 0 and 0 <= (s - 5) // 2 < len(UNITS):
                    w = (s - 5) // 2
                    t, h = UNITS[w]
                    lo, nl = window(t)
                    pe.wait_ge(n_ptl, w + 1)
                    pe.wait_ge(n_ptc, w + 1)
                    if h == 0 and t >= 1:
                        pe.wait_ge(n_osb, t)
                    dst = B_O[:, h * HD:(h + 1) * HD]
                    for c in range(nl):
                        nc.tensor.matmul(dst, PTb[:, w % 2, c * P:(c + 1) * P], VAt[:, lo + c, h * HD:(h + 1) * HD],
                                         start=(c == 0), stop=False)
                    for c in range(2):
                        mm = nc.tensor.matmul(dst, PTb[:, w % 2, (3 + c) * P:(4 + c) * P],
                                              VAC[:, c, h * HD:(h + 1) * HD], start=False, stop=(c == 1))
                    mm.then_inc(n_pv, 1)
                k = s - 3
                if 0 <= k < NITEM and k % 8 == 0:
                    u, e, d, head, i = hg(k)
                    pe.wait_ge(g_kd, u + 1)
                    if u >= 1:
                        pe.wait_ge(g_st, 3 * u)
                    if u >= 3:
                        pe.wait_ge(g_ot, (u - 1) // 2)
                    for c in range(3):
                        cc = c if d == 0 else 3 - c
                        mm = nc.tensor.transpose(B_HT[:, c * P:(c + 1) * P], KD[:, cc], ident[:])
                    mm.then_inc(g_ktr, 1)
                k = s - 5
                if 0 <= k < NITEM and k % 8 == 0:
                    u, e, d, head, i = hg(k)
                    pe.wait_ge(g_kdt, u + 1)
                    for c in range(3):
                        cc = c if d == 0 else 3 - c
                        mm = nc.tensor.matmul(B_HT[:, c * P:(c + 1) * P], KDT[:, c], VI[:, cc, head * P:(head + 1) * P],
                                              start=True, stop=True)
                    mm.then_inc(g_ds, 1)
                k = s - 10
                if k == NITEM - 1:
                    first_pair(N_OUT, oh_hi, oh_lo, 0, OUT_ORDER, 0, 3)
                if 0 <= k < NITEM and k % 16 == 15:
                    hd_ = k // 16
                    pe.wait_ge(g_on, hd_ + 1)
                    u_now = min(2 * (hd_ + 1) + 1, 8)
                    pe.wait_ge(g_st, 3 * u_now)
                    for c in range(NCH):
                        mm = nc.tensor.transpose(B_HT[:, c * P:(c + 1) * P], ON[:, c], ident[:])
                    mm.then_inc(g_onr, 1)

            def res_bank(m):
                return bank[m % 4]

            def by_halves(dst, n, first, order=range(KC)):
                for h in range(2):
                    if h == 0:
                        pe.wait_ge(lo_first, first)
                    else:
                        pe.wait_ge(lo_done, n + 1)
                    for i in range(h * KC // 2, (h + 1) * KC // 2):
                        w, kc = slice(i * P, (i + 1) * P), order[i]
                        nc.tensor.matmul(dst, whi[:, n % 2, w], h_hi[:, kc], start=(i == 0), stop=False)
                        nc.tensor.matmul(dst, whi[:, n % 2, w], h_lo[:, kc], start=False, stop=False)
                        mm = nc.tensor.matmul(dst, wlo[:, n % 2, w], h_hi[:, kc], start=False, stop=(i == KC - 1))
                mm.then_inc(gemm_done, 1)

            def second_pair(n0, pair):
                for q in range(2):
                    by_halves(bank[2 + q][:], n0 + 2 + q, 2 * pair + q + 1)

            first_pair(N_OUT, oh_hi, oh_lo, 0, OUT_ORDER, 3, KC)
            for m in range(2, 8):
                if m >= 4:
                    pe.wait_ge(r_done, m - 3)
                if m < 4:
                    by_halves(res_bank(m)[:], N_OUT + m, m - 1, OUT_ORDER)
                    continue
                pe.wait_ge(lo_done, N_OUT + m + 1)
                gemm(res_bank(m)[:], m, h_hi, h_lo, T, OUT_ORDER).then_inc(gemm_done, 1)

            def stats(k, src):
                pe.wait_ge(rs_done, 7 * (k + 1))
                nc.tensor.matmul(bank[5][:], ones_d[:], acc[:, 0], start=True, stop=False)
                pe.wait_ge(qs_done, 7 * (k + 1))
                nc.tensor.matmul(bank[6][:], ones_d[:], acc[:, 1], start=True, stop=False)
                pe.wait_ge(r_done, 8 * (k + 1))
                nc.tensor.matmul(bank[5][:], ones_d[:], src[:, 7], start=False, stop=True).then_inc(st_mean, 1)
                pe.wait_ge(sq_done, 8 * (k + 1))
                nc.tensor.matmul(bank[6][:], ones_d[:], tb[:, 0], start=False, stop=True).then_inc(st_sq, 1)

            stats(0, XA)

            def up(layer):
                first_pair(N_UP1 if layer else N_UP0, ln_hi, ln_lo, 24 if layer else 0)
                second_pair(N_UP1 if layer else N_UP0, 4 if layer else 1)
                if layer == 0:
                    with pe.Fori(0, 5) as it:
                        up_body(layer, 2 * it + 1)
                        up_body(layer, 2 * it + 2)
                        reduce_part(pe, 8 * it + 40, 1, 8 * it + 64)
                else:
                    with pe.Fori(1, 11) as it:
                        up_body(layer, it)

            def up_body(layer, it):
                for j in range(4):
                    pe.wait_ge(lo_done, 4 * it + j + (N_UP1 if layer else N_UP0) + 1)
                    pe.wait_ge(up_a, 2 * it + j // 2 - 1 + 22 * layer)
                    gemm(bank[j][:], j, h_hi, h_lo, T, range(KC)).then_inc(gemm_done, 1)

            def down_body(layer, it):
                kc0 = (0, 8, 15)
                for j in range(12):
                    m = j // 3
                    if j % 3 == 0:
                        pe.wait_ge(r_done, 4 * it + m - 3 + (32 if layer else 8))
                    pe.wait_ge(up_lo, (8, 15, 22)[j % 3] + 22 * layer)
                    pe.wait_ge(lo_done, 12 * it + j + (N_DN1 if layer else N_DN0) + 1)
                    kcs = range(kc0[j % 3], kc0[j % 3] + DN_KC[j % 3])
                    gemm(res_bank(m)[:], j, A_hi, A_lo, T, kcs, first=j % 3 == 0, last=j % 3 == 2)\
                        .then_inc(gemm_done, 1)

            def down(layer):
                with pe.Fori(0, 2) as it:
                    down_body(layer, it)

            up(0)
            down(0)
            reduce_part(pe, 80, 1, 104)
            stats(1, XA)
            first_pair(N_CV1, ln_hi, ln_lo, 8)

            def conv_taps(k, b):
                pe.wait_ge(cv_u, k + 1)
                pe.wait_ge(cv_diag, k + 1)
                pe.wait_ge(r_done, k + 16)
                ta, tb_, tm, _ = taps_of(k)
                for a in range(tm):
                    m_ = diag7[:, a] if tm == TM7 else diag[:, b, a]
                    mm = nc.tensor.matmul(bank[4][:], m_, U[:, b, ta + tb_ + a:ta + tb_ + a + T],
                                          start=(a == 0), stop=(a == tm - 1))
                mm.then_inc(cv_mm, 1)

            def cv1_body(it):
                for j in range(4):
                    pe.wait_ge(lo_done, 4 * it + j + N_CV1 + 1)
                    pe.wait_ge(cv_u, 2 * it + j // 2 - 1)
                    gemm(bank[j][:], j, h_hi, h_lo, T, range(KC)).then_inc(gemm_done, 1)
                    if j % 2:
                        conv_taps(2 * it + j // 2 - 1, (j // 2 + 1) % 2)

            second_pair(N_CV1, 2)
            conv_taps(0, 0)
            with pe.Fori(1, 4) as it:
                cv1_body(it)
            conv_taps(7, 1)
            stats(2, RC)
            first_pair(N_CV2, ln_hi, ln_lo, 16)
            for m in range(2, 8):
                if m >= 4:
                    pe.wait_ge(r_done, m - 3 + 24)
                if m < 4:
                    by_halves(res_bank(m)[:], N_CV2 + m, 6 + m - 1)
                    continue
                pe.wait_ge(lo_done, m + N_CV2 + 1)
                gemm(res_bank(m)[:], m, h_hi, h_lo, T, range(KC)).then_inc(gemm_done, 1)
            stats(3, XA)
            up(1)
            down(1)
            stats(4, XA)

        @block.scalar
        def _(act):
            act.wait_ge(const_in, 32)
            nc.scalar.activation(cact[:], cin[:], ACT.Silu).then_inc(cact_done, 1)
            for n in range(2):
                split_hi(act, 0, n, first=True)
            act.wait_ge(ones_set, 1)
            act.wait_ge(x_in, 16)
            for j in range(KC):
                act.wait_ge(mod0_done, j + 1)
                nc.scalar.activation(xin[:, j], xin[:, j], ACT.Identity, bias=mod0[:, j, 0, 0:1],
                                     scale=mod0p[:, j, 0:1]).then_inc(hx_done, 1)
                act.wait_ge(hx_done, j + 1)
                nc.scalar.activation(h_hi[:, j], xin[:, j], ACT.Copy).then_inc(hhi_done, 1)

            def to_tiles(v):
                return v.rearrange("p (r t c) -> p t r c", r=ROWS, t=NT)

            def tiles(v):
                return v.rearrange("p (t r c) -> p t r c", r=ROWS, t=NT)

            for n in range(32):
                kind, f = divmod(n, 4)
                if n == 4:
                    nc.scalar.preload_act_table_set("natural_log_exp_and_others")
                i, v = n - 4, -1
                if n in v_tile:
                    v = v_tile.index(n)
                if 5 <= n <= 12:
                    u = n - 5
                    act.wait_ge(z_pre, u + 1)
                    if u >= 1:
                        act.wait_ge(z_kd, u)
                    if u < HH:
                        nc.scalar.activation(Ec[:], prec[:, 1:TC + 1], ACT.Exp, bias=prec[:, TC:TC + 1],
                                             scale=-1.0).then_inc(z_ec, 1)
                    else:
                        nc.scalar.activation(Ec[:], prec[:, 0:TC], ACT.Exp).then_inc(z_ec, 1)
                split_hi(act, n // 4, n % 4 + 2)
                px, pc = bank[n % 2], bank[2 + n % 2][:, 0:TC]
                if kind == IB or kind == VA:
                    if v >= 1:
                        act.wait_ge(vt_tr, v)
                    if kind == IB:
                        nc.scalar.activation(VT[:, 0:T], px[:], ACT.Copy).then_inc(evac_act, 1)
                    else:
                        nc.scalar.activation(tiles(VT[:, 0:T]), to_tiles(px[:]), ACT.Copy).then_inc(evac_act, 1)
                elif kind == ZF or kind == ZB:
                    if i >= 1:
                        act.wait_ge(z_key, i)
                    nc.scalar.activation(ab[:, 0:T], px[:], ACT.Abs)
                    nc.scalar.activation(ab[:, T:T + TC], pc, ACT.Abs).then_inc(evac_act, 1)
                    act.wait_ge(evac_act, n + 1)
                    nc.scalar.activation(ab[:], ab[:], ACT.Exp, scale=-1.0).then_inc(z_exp, 1)
                    act.wait_ge(z_exp, i + 1)
                    nc.scalar.activation(soft[:], ab[:], ACT.Ln, bias=ones[:, 0:1]).then_inc(z_ln, 1)
                elif kind == KA:
                    nc.scalar.activation(KT_[:, f], px[:], ACT.Copy).then_inc(evac_act, 1)
                elif kind == QB:
                    nc.scalar.activation(QBt[:, f], px[:], ACT.Copy).then_inc(evac_act, 1)
                elif kind == QA:
                    nc.scalar.activation(tiles(Qt[:, f]), to_tiles(px[:]), ACT.Copy,
                                         scale=HD ** -0.5).then_inc(evac_act, 1)
                else:
                    nc.scalar.activation(GBt[:, f], px[:], ACT.Silu).then_inc(evac_act, 1)
                if n - 1 in v_tile:
                    w = v_tile.index(n - 1)
                    act.wait_ge(vt_tr, w + 1)
                    dst = (VIC if w < 4 else VAC)[:, :, (w % 4) * P:(w % 4 + 1) * P]
                    nc.scalar.activation(dst, bank[5][:, 0:TC].rearrange("p (c d) -> p c d", c=2),
                                         ACT.Copy).then_inc(vc_done, 1)
                if 5 <= n <= 12:
                    u = n - 5
                    act.wait_ge(z_tr, u + 1)
                    if u >= 1:
                        act.wait_ge(z_mm, u)
                    nc.scalar.activation(KcT[:].rearrange("p c d -> p (c d)"), bank[6][:, 0:TC], ACT.Copy).then_inc(z_kt, 1)
                if kind == ZF or kind == ZB:
                    act.wait_ge(z_d, i + 1)
                    if i >= 1:
                        act.wait_ge(z_kd, i)
                    nc.scalar.activation(KEY[:, i], ab[:, 0:T], ACT.Exp)
                    nc.scalar.activation(keyc[:], ab[:, T:T + TC], ACT.Exp).then_inc(z_key, 1)

            act.wait_ge(gemm_done, 32)
            B_SL, B_SC, B_PL, B_PC, B_O, B_HA, B_HO, B_HT = bank
            for s in range(NSLOT):
                if s >= 2 and (s - 2) % 2 == 0 and (s - 2) // 2 < len(UNITS):
                    w = (s - 2) // 2
                    _, nl = window(UNITS[w][0])
                    act.wait_ge(n_neg, w + 1)
                    if w >= 2:
                        act.wait_ge(n_tr, w - 1)
                        act.wait_ge(n_sum, w - 1)
                    src = Ssb[:, w % 2, 0:nl * P].rearrange("p (r t c) -> p t r c", r=ROWS, t=nl)
                    dst = Pb[:, w % 2, 0:nl * P].rearrange("p (t r c) -> p t r c", r=ROWS, t=nl)
                    nc.scalar.activation(dst, src, ACT.Exp, bias=mxc[:, w % 2, 2:3], accum_out=sml[:, w % 2, 0:1])
                    nc.scalar.activation(Pb[:, w % 2, 3 * P:5 * P], B_SC[:, 0:TC], ACT.Exp, bias=mxc[:, w % 2, 2:3],
                                         accum_out=sml[:, w % 2, 1:2]).then_inc(n_exp, 1)
                if s >= 4 and (s - 4) % 2 == 0 and (s - 4) // 2 < len(UNITS):
                    w = (s - 4) // 2
                    act.wait_ge(n_tr, w + 1)
                    if w >= 2:
                        act.wait_ge(n_pv, w - 1)
                    nl = window(UNITS[w][0])[1]
                    nc.scalar.activation(PTb[:, w % 2, 0:nl * P], B_PL[:, 0:nl * P], ACT.Copy).then_inc(n_ptl, 1)
                    nc.scalar.activation(PTb[:, w % 2, 3 * P:5 * P], B_PC[:, 0:TC], ACT.Copy).then_inc(n_ptc, 1)
                k = s - 1
                if 0 <= k < NITEM:
                    u, e, d, head, i = hg(k)
                    act.wait_ge(g_sub, k + 1)
                    b = EX[:, k % 4].rearrange("p c t -> p (c t)")
                    nc.scalar.activation(b, b, ACT.Exp).then_inc(g_exp, 1)
                    if e == 0:
                        if u >= 1:
                            act.wait_ge(g_st, 3 * u)
                        nc.scalar.activation(gam[:, d], PRE[:, i, :, CH], ACT.Exp).then_inc(g_gam, 1)
                        if d == 1:
                            act.wait_ge(g_ktr, u)
                            nc.scalar.activation(KD[:], prefix(i, d), ACT.Exp).then_inc(g_e2, 1)
                k = s - 5
                if 0 <= k < NITEM and k % 16 == 0:
                    u, e, d, head, i = hg(k)
                    if head >= 1:
                        act.wait_ge(g_o, head)
                    nc.scalar.activation(QD[:, 0], prefix(i, 0), ACT.Exp).then_inc(g_e2, 1)
                k = s - 4
                if 0 <= k < NITEM and k % 8 == 0:
                    u = k // 8
                    act.wait_ge(g_ktr, u + 1)
                    if u >= 1:
                        act.wait_ge(g_ds, u)
                    nc.scalar.activation(KDT[:].rearrange("p c d -> p (c d)"), B_HT[:, 0:3 * P], ACT.Copy).then_inc(g_kdt, 1)
                k = s - 6
                if 0 <= k < NITEM and k % 16 == 15:
                    hd_ = k // 16
                    act.wait_ge(g_o, hd_ + 1)
                    if hd_ >= 1:
                        act.wait_ge(g_onr, hd_)
                    nc.scalar.activation(ON[:].rearrange("p c d -> p (c d)"), B_HO[:], ACT.Square).then_inc(g_sq, 1)

            act.wait_ge(g_o, HH)
            act.wait_ge(g_ot, HH - 1)
            for i, j in enumerate(OUT_ORDER):
                if i == 3:
                    act.wait_ge(g_mm, NITEM)
                    act.wait_ge(n_ot, NT)
                if i == 7:
                    act.wait_ge(g_ot, HH)
                nc.scalar.activation(h_hi[:, j], OT[:, j], ACT.Copy).then_inc(oh_hi, 1)

            def square(count, k, src):
                act.wait_ge(r_done, count + 1)
                if not (isinstance(count, int) and count == 0):
                    act.wait_ge(qs_done, count - k)
                if k:
                    act.wait_ge(st_sq, k)
                nc.scalar.activation(tb[:, 0], src, ACT.Square).then_inc(sq_done, 1)

            def ln(k, src):
                nc.scalar.preload_act_table_set("natural_log_exp_and_others")
                rstd = rstd_of(k)
                act.wait_ge(st_mean, k + 1)
                nc.scalar.activation(tb[:, 3], bank[5][:], ACT.Square).then_inc(ln_m2, 1)
                for q in range(2):
                    act.wait_ge(ln_v, 2 * k + q + 1)
                    nc.scalar.activation(rstd[:, HALF[q]], rstd[:, HALF[q]], ACT.Ln).then_inc(ln_l, 1)
                for q in range(2):
                    act.wait_ge(ln_l, 2 * k + q + 1)
                    nc.scalar.activation(rstd[:, HALF[q]], rstd[:, HALF[q]], ACT.Exp, scale=-0.5).then_inc(ln_rstd, 1)
                if k < 4:
                    f, t_ = ACT.Silu if k == 2 else ACT.Identity, norm_buf(0)
                    for q in range(2):
                        act.wait_ge(*((ln_t0, k + 1) if q == 0 else (ln_t, 8 * k + 1)))
                        nc.scalar.activation(t_[:, HALF[q]], t_[:, HALF[q]], f,
                                             bias=norm[:, k, 1, 0:1]).then_inc(ln_h if q else ln_h0, 1)
                    for q in range(2):
                        act.wait_ge(*((ln_h0, k + 1) if q == 0 else (ln_h, 8 * k + 1)))
                        ins = nc.scalar.activation(h_hi[:, 0, HALF[q]], t_[:, HALF[q]], ACT.Copy)
                    ins.then_inc(ln_hi, 1)
                    for j in range(1, 8):
                        act.wait_ge(ln_t, 8 * k + j + 1)
                        t_ = norm_buf(j)
                        nc.scalar.activation(t_, t_, ACT.Silu if k == 2 else ACT.Identity,
                                             bias=norm[:, k, 1, j:j + 1]).then_inc(ln_h, 1)
                        act.wait_ge(ln_h, 8 * k + j + 1)
                        nc.scalar.activation(h_hi[:, j], t_, ACT.Copy).then_inc(ln_hi, 1)
                    split_hi_halves(act, (N_UP0, N_CV1, N_CV2, N_UP1)[k], k + 1)
                if k == 4:
                    for j in range(8):
                        act.wait_ge(ln_ax, 24 + j + 1)
                        nc.scalar.activation(src[:, j], src[:, j], ACT.Identity,
                                             bias=norm[:, k, 3, j:j + 1]).then_inc(ln_x, 1)

            split_hi_halves(act, N_OUT, 0)
            for n in range(8):
                if n >= 2:
                    split_hi(act, N_OUT // 4 + n // 4, n % 4 + 2)
                square(n, 0, XA[:, n])
            act.wait_ge(ln_vec, 1)
            ln(0, XA)

            def up(layer):
                n0 = (N_UP1 if layer else N_UP0) // 4

                def body(it):
                    for b in range(2):
                        k = 2 * it + b
                        with_norm = isinstance(k, int) and k == 0
                        if not with_norm:
                            split_hi(act, it + n0, 2 * b + 2)
                        nc.scalar.activation(tb[:, b], bank[2 * b][:], ACT.Silu).then_inc(up_s, 1)
                        if not with_norm:
                            split_hi(act, it + n0, 2 * b + 3)
                        act.wait_ge(up_a, k + 22 * layer + 1)
                        nc.scalar.activation(A_hi[:, k], tb[:, 2 + b], ACT.Copy).then_inc(up_hi, 1)

                body(0)
                with act.Fori(1, 11) as it:
                    body(it)

            def down_body(layer, it, last=False):
                for j in range(12):
                    if not (last and j >= 10):
                        split_hi(act, 3 * it + (N_DN1 if layer else N_DN0) // 4 + j // 4, j % 4 + 2)
                    if j % 3 == 2:
                        square(4 * it + j // 3 + (32 if layer else 8), 4 if layer else 1, XA[:, 4 * it + j // 3])

            up(0)
            with act.Fori(0, 2) as it:
                down_body(0, it)
            act.wait_ge(ln_vec, 5)
            ln(1, XA)

            def cv1_body(it):
                for b in range(2):
                    k = 2 * it + b
                    if not (isinstance(k, int) and k == 0):
                        split_hi(act, it + N_CV1 // 4, 2 * b + 2)
                        split_hi(act, it + N_CV1 // 4, 2 * b + 3)
                    nc.scalar.activation(tb[:, 2 + b], bank[2 * b + 1][:], ACT.Sigmoid,
                                         bias=vec[:, bass.ds(k + VEC["cv_b1"] + 8, 1)]).then_inc(cv_s, 1)
                    w0 = TAPS * k + VEC["cv_wdw"]
                    ta, tb_, tm, tp = taps_of(k)
                    if not (isinstance(k, int) and k < 2):
                        act.wait_ge(cv_mm, k - 1)
                    for a in range(tm):
                        m_ = diag7[:, a] if tm == TM7 else diag[:, b, a]
                        ins = nc.scalar.activation(m_, ident[:], ACT.Copy, scale=vec[:, bass.ds(w0 + ta + tb_ + a, 1)])
                    ins.then_inc(cv_diag, 1)
                    act.wait_ge(cv_u, k + 1)
                    for a in range(tp):
                        if not (isinstance(k, int) and k == 0):
                            act.wait_ge(cv_sum, (TP - 1) * (k - 1) + min(max(a, 1), TP - 1))
                        tap = TAPS - tp + a
                        nc.scalar.activation(prod[:, a], U[:, b, tap:tap + T], ACT.Copy,
                                             scale=vec[:, bass.ds(w0 + tap, 1)]).then_inc(cv_prod, 1)
                    if not (isinstance(k, int) and k == 0):
                        square(k + 15, 2, RC[:, k - 1])

            cv1_body(0)
            with act.Fori(1, 3) as it:
                cv1_body(it)
            cv1_body(3)
            square(23, 2, RC[:, 7])
            ln(2, RC)
            for n in range(8):
                if n >= 2:
                    split_hi(act, N_CV2 // 4 + n // 4, n % 4 + 2)
                square(n + 24, 3, XA[:, n])
            ln(3, XA)
            up(1)
            down_body(1, 0)
            down_body(1, 1, last=True)
            ln(4, XA)

        @block.vector
        def _(dve):
            V = nc.vector
            steps = [0]

            def small(ins):
                steps[0] += 1
                ins.then_inc(mchain, 1)
                dve.wait_ge(mchain, steps[0])

            def mod_values(layer, lo, hi, parts):
                dve.wait_ge(part_done, parts)
                c0 = 64 + lo if layer else lo - 8
                b0 = VEC["b_mod"] + 48 * layer
                small(V.tensor_tensor(mod[:, layer, lo:hi], bank[7][:, c0:c0 + hi - lo], vec[:, b0 + lo:b0 + hi], ALU.add))
                V.tensor_scalar(modp[:, layer, lo:hi], mod[:, layer, lo:hi], 1.0, None, ALU.add).then_inc(modv_done, 1)

            def norm_vectors(k, g, b, sc=None, sh=None, layer=0, extra=None):
                dve.wait_ge(modv_done, 2 if k else 1)
                G, B, AG, AB = (norm[:, k, r] for r in range(4))
                if sc is not None:
                    small(V.tensor_tensor(G, g, modp[:, layer, sc * 8:sc * 8 + 8], ALU.mult))
                    small(V.tensor_tensor(B, b, modp[:, layer, sc * 8:sc * 8 + 8], ALU.mult))
                    small(V.tensor_tensor(B, B, mod[:, layer, sh * 8:sh * 8 + 8], ALU.add))
                elif k == 2:
                    small(V.tensor_copy(G, g))
                    V.tensor_copy(B, b).then_inc(ln_vec, 1)
                    return
                a = 1.0 if k == 4 else ALPHA
                small(V.tensor_scalar(AG, g, a, None, ALU.mult))
                if extra is None:
                    V.tensor_scalar(AB, b, a, None, ALU.mult).then_inc(ln_vec, 1)
                else:
                    small(V.tensor_scalar(AB, b, a, None, ALU.mult))
                    small(V.tensor_tensor(norm[:, k, 4], extra, mod[:, 1, G1 * 8:G1 * 8 + 8], ALU.mult))
                    V.tensor_tensor(AB, AB, norm[:, k, 4], ALU.add).then_inc(ln_vec, 1)

            def vcol(name, i=0):
                return vec[:, VEC[name] + 8 * i:VEC[name] + 8 * i + 8]

            dve.wait_ge(const_in, 32)
            dve.wait_ge(cact_done, 1)
            for kc in range(KC):
                dve.wait_ge(sh_in[kc], 16)
                for c in range(2):
                    a_, b_ = sh_acc[:, c], sh_w[:, kc]
                    if kc == 0:
                        ins = V.tensor_scalar(a_, b_, cact[:, 0, c:c + 1], None, ALU.mult)
                    else:
                        dve.wait_ge(sh_done, 2 * kc + c - 1)
                        ins = V.scalar_tensor_tensor(out=a_, in0=b_, scalar=cact[:, kc, c:c + 1], in1=a_,
                                                     op0=ALU.mult, op1=ALU.add)
                    ins.then_inc(sh_done, 1)
            dve.wait_ge(sh_mm, 1)
            for j in range(KC + 1):
                if j < KC:
                    dve.wait_ge(mod_done, j + 1)
                    b = vec[:, VEC["b_mod"] + j:VEC["b_mod"] + j + 9:8].unsqueeze(2).broadcast_to([P, 2, 2])
                    small(V.tensor_tensor(mod0[:, j], bank[j][:, 0:4].rearrange("p (s c) -> p s c", s=2), b, ALU.add))
                    V.tensor_scalar(mod0p[:, j], mod0[:, j, 1], 1.0, None, ALU.add).then_inc(mod0_done, 1)
                    if j == 0:
                        dve.wait_ge(cx_in, 16)
                    dve.wait_ge(mod0_done, j + 1)
                    V.tensor_scalar(cxin[:, j], cxin[:, j], mod0p[:, j, 1:2], mod0[:, j, 0, 1:2], ALU.mult,
                                    ALU.add).then_inc(hxc_done, 1)
                if j >= 1:
                    dve.wait_ge(hhi_done, j)
                    V.tensor_tensor(h_lo[:, j - 1], xin[:, j - 1], h_hi[:, j - 1].bitcast(fp32),
                                    ALU.subtract).then_inc(hlo_done, 1)
                if j < KC:
                    dve.wait_ge(hxc_done, j + 1)
                    V.tensor_copy(hc_hi[:, j], cxin[:, j]).then_inc(hhic_done, 1)
                if j >= 1:
                    dve.wait_ge(hhic_done, j)
                    V.tensor_tensor(hc_lo[:, j - 1], cxin[:, j - 1], hc_hi[:, j - 1].bitcast(fp32),
                                    ALU.subtract).then_inc(hloc_done, 1)
            V.memset(PRE[:, :, :, 0:1], 0.0)
            small(V.memset(prec[:, 0:1], 0.0))
            small(V.memset(neg_half[:], -0.5))

            dve.wait_ge(ones_set, 1)
            for n in range(32):
                kind, f = divmod(n, 4)
                i, v = n - 4, -1
                if n in v_tile:
                    v = v_tile.index(n)
                if 5 <= n <= 12:
                    u = n - 5
                    dve.wait_ge(z_ec, u + 1)
                    if u >= 1:
                        dve.wait_ge(z_tr, u)
                    V.tensor_tensor(Kdc[:], keyc[:], Ec[:], ALU.mult).then_inc(z_kd, 1)
                for q in blocks_at(n):
                    add_block(dve, q // 2, q % 2, 0, q % 8, part_no=q // 8 if q else None)
                px, pc = bank[n % 2], bank[2 + n % 2][:, 0:TC]
                dve.wait_ge(gemm_done, n + 1)
                if kind == IB or kind == VA:
                    if v >= 1:
                        dve.wait_ge(vt_tr, v)
                    V.tensor_copy(VT[:, T:T + TC], pc).then_inc(evac_dve, 1)
                elif kind == ZF or kind == ZB:
                    dve.wait_ge(z_ln, i + 1)
                    if i >= 1:
                        dve.wait_ge(z_pre, i)
                    V.scalar_tensor_tensor(out=ls[:, 0:T], in0=px[:], scalar=0.0, in1=soft[:, 0:T], op0=ALU.min,
                                           op1=ALU.subtract)
                    V.scalar_tensor_tensor(out=ls[:, T:T + TC], in0=pc, scalar=0.0, in1=soft[:, T:T + TC], op0=ALU.min,
                                           op1=ALU.subtract).then_inc(z_ls, 1)
                    dve.wait_ge(z_ls, i + 1)
                    V.tensor_tensor(ab[:, 0:T], ls[:, 0:T], px[:], ALU.subtract)
                    V.tensor_tensor(ab[:, T:T + TC], ls[:, T:T + TC], pc, ALU.subtract).then_inc(z_d, 1)
                    if i >= 1:
                        dve.wait_ge(z_ec, i)
                    one = ones[:, 0:1].broadcast_to([P, TC])
                    for c in range(NCH):
                        V.tensor_tensor_scan(out=PRE[:, i, c, 1:CH + 1], data0=ones[:], data1=ls[:, c * CH:(c + 1) * CH],
                                             initial=0.0, op0=ALU.mult, op1=ALU.add)
                    V.tensor_tensor_scan(out=prec[:, 1:TC + 1], data0=one, data1=ls[:, T:T + TC],
                                         initial=0.0, op0=ALU.mult, op1=ALU.add).then_inc(z_pre, 1)
                elif kind == KA:
                    V.tensor_copy(KTC[:, f], pc).then_inc(evac_dve, 1)
                if n - 1 in v_tile:
                    w = v_tile.index(n - 1)
                    dve.wait_ge(vt_tr, w + 1)
                    dst = (VI if w < 4 else VAt)[:, :, (w % 4) * P:(w % 4 + 1) * P]
                    V.tensor_copy(dst, bank[4][:].rearrange("p (c d) -> p c d", c=4)).then_inc(vx_done, 1)
                if 6 <= n <= 13:
                    u = n - 6
                    dve.wait_ge(z_mm, u + 1)
                    V.tensor_copy(S0[:, u], bank[4][:, 0:P]).then_inc(z_s0, 1)

            mod_values(0, 16, 48, 4)
            norm_vectors(0, vcol("ln1_g"), vcol("ln1_b"), SC2, SH2)

            B_SL, B_SC, B_PL, B_PC, B_O, B_HA, B_HO, B_HT = bank
            dve.wait_ge(z_key, 8)
            dve.wait_ge(evac_act, 32)
            dve.wait_ge(table_in, 32)
            dve.wait_ge(lvl_done, 1)
            def out_lo(i0, i1):
                for i in range(i0, i1):
                    j = OUT_ORDER[i]
                    dve.wait_ge(oh_hi, i + 1)
                    V.tensor_tensor(h_lo[:, j], OT[:, j], h_hi[:, j].bitcast(fp32), ALU.subtract).then_inc(oh_lo, 1)

            for s in range(NSLOT):
                if s == NITEM + 8:
                    out_lo(0, 3)
                if s == NITEM + 10:
                    out_lo(3, 7)
                k = s - 4
                if 0 <= k < NITEM:
                    u, e, d, head, i = hg(k)
                    dve.wait_ge(g_mm, k + 1)
                    a_ = AT[:, d]
                    p_ = bank[product_bank(k)][:].rearrange("p (c t) -> p c t", c=NCH)
                    if e == 0:
                        if head >= 1:
                            dve.wait_ge(g_o, head)
                        V.tensor_tensor(a_, p_, ident[:].unsqueeze(1).broadcast_to([P, NCH, CH]),
                                        ALU.mult).then_inc(g_at, 1)
                    else:
                        dve.wait_ge(g_at, k)
                        m_ = lvl[:, d, e - 1].unsqueeze(1).broadcast_to([P, NCH, CH])
                        V.copy_predicated(a_, m_, p_).then_inc(g_at, 1)
                if s >= 21 and (s - 21) % 16 == 0 and (s - 21) // 16 < NT:
                    t = (s - 21) // 16
                    dve.wait_ge(n_otr, t + 1)
                    for g in range(4):
                        dst = OT[:, g].rearrange("p (r c) -> p r c", r=ROWS)[:, :, t * TILE_W:(t + 1) * TILE_W]
                        ins = V.tensor_copy(dst, B_PL[:, g * P:(g + 1) * P].rearrange("p (r c) -> p r c", r=ROWS))
                    ins.then_inc(n_ot, 1)
                if s >= 1 and (s - 1) % 2 == 0 and (s - 1) // 2 < len(UNITS):
                    w = (s - 1) // 2
                    _, nl = window(UNITS[w][0])
                    dve.wait_ge(n_s, w + 1)
                    dve.wait_ge(n_comb, w + 1)
                    if w >= 2:
                        dve.wait_ge(n_exp, w - 1)
                    V.reduce_max(mxc[:, w % 2, 0:1], B_SC[:, 0:TC], AX.X).then_inc(n_mc, 1)
                    dve.wait_ge(n_mc, w + 1)
                    V.tensor_tensor_reduce(out=Ssb[:, w % 2, 0:nl * P], in0=B_SL[:, 0:nl * P],
                                           in1=comb[:, w % 2, 0:nl * P], scale=1.0, scalar=mxc[:, w % 2, 0:1],
                                           op0=ALU.add, op1=ALU.max, accum_out=mxc[:, w % 2, 1:2]).then_inc(n_mx, 1)
                    dve.wait_ge(n_mx, w + 1)
                    V.tensor_scalar(mxc[:, w % 2, 2:3], mxc[:, w % 2, 1:2], -1.0, None, ALU.mult).then_inc(n_neg, 1)
                if s >= 3 and (s - 3) % 2 == 0 and (s - 3) // 2 < len(UNITS):
                    w = (s - 3) // 2
                    t, h = UNITS[w]
                    dve.wait_ge(n_exp, w + 1)
                    V.tensor_tensor(rsum[:, t % 2, h:h + 1], sml[:, w % 2, 0:1], sml[:, w % 2, 1:2],
                                    ALU.add).then_inc(n_sum, 1)
                if s >= 20 and (s - 20) % 16 == 0 and (s - 20) // 16 < NT:
                    t = (s - 20) // 16
                    dve.wait_ge(n_sum, 8 * (t + 1))
                    V.reciprocal(rinv[:, t % 2], rsum[:, t % 2]).then_inc(n_inv, 1)
                    dve.wait_ge(n_inv, t + 1)
                    dve.wait_ge(n_pv, 8 * (t + 1))
                    if t >= 1:
                        dve.wait_ge(n_otr, t)
                    V.tensor_tensor(Osb[:], B_O[:].rearrange("p (h d) -> p h d", h=NH),
                                    rinv[:, t % 2].unsqueeze(2).broadcast_to([P, NH, HD]), ALU.mult).then_inc(n_osb, 1)
                k = s - 6
                if 0 <= k < NITEM and k % 8 == 0:
                    u, e, d, head, i = hg(k)
                    dve.wait_ge(g_ds, u + 1)
                    dve.wait_ge(g_gam, u + 1)
                    if head >= 1:
                        dve.wait_ge(g_o, head)
                    for c in range(3):
                        cc = c if d == 0 else 3 - c
                        prev = S0[:, i] if c == 0 else St[:, d, c - 1]
                        if c:
                            dve.wait_ge(g_st, 3 * u + c)
                        V.scalar_tensor_tensor(out=St[:, d, c], in0=prev, scalar=gam[:, d, cc:cc + 1],
                                               in1=B_HT[:, c * P:(c + 1) * P], op0=ALU.mult,
                                               op1=ALU.add).then_inc(g_st, 1)
                k = s - 7
                if 0 <= k < NITEM and k % 16 == 15:
                    hd_ = k // 16
                    dve.wait_ge(g_sq, hd_ + 1)
                    V.reduce_sum(msq[:, 0], ON[:], AX.X).then_inc(g_ms, 1)
                    dve.wait_ge(g_ms, hd_ + 1)
                    V.tensor_scalar(msq[:, 1], msq[:, 0], 1.0 / P, RMS_EPS, ALU.mult, ALU.add).then_inc(g_mse, 1)
                k = s - 9
                if 0 <= k < NITEM and k % 16 == 15:
                    hd_ = k // 16
                    dve.wait_ge(g_pow, hd_ + 1)
                    V.tensor_tensor(ON[:], B_HO[:].rearrange("p (c d) -> p c d", c=NCH),
                                    msq[:, 2].unsqueeze(2).broadcast_to([P, NCH, P]), ALU.mult).then_inc(g_on, 1)
                k = s - 11
                if 0 <= k < NITEM and k % 16 == 15:
                    hd_ = k // 16
                    dve.wait_ge(g_onr, hd_ + 1)
                    g0 = VEC["hg_norm_g"] + hd_
                    V.scalar_tensor_tensor(out=OT[:, 4 + hd_], in0=B_HT[:], scalar=vec[:, g0:g0 + 1], in1=GBt[:, hd_],
                                           op0=ALU.mult, op1=ALU.mult).then_inc(g_ot, 1)
                k = s
                if k < NITEM:
                    u, e, d, head, i = hg(k)
                    if k >= 4:
                        dve.wait_ge(g_mm, k - 3)
                        if (k - 4) % 8 == 0:
                            dve.wait_ge(g_kd, (k - 4) // 8 + 1)
                    b = EX[:, k % 4]
                    if e == 0:
                        tot = PRE[:, i, :, CH:CH + 1].broadcast_to([P, NCH, CH])
                        V.tensor_tensor(b, tot, prefix(i, d), ALU.subtract).then_inc(g_sub, 1)
                    else:
                        nb, H = halves(e)
                        b = b.rearrange("p c (b t) -> p c b t", b=nb)
                        v_ = prefix(i, d).rearrange("p c (b t) -> p c b t", b=nb)
                        r_ = PRE[:, i, :, 1:CH + 1].rearrange("p c (b t) -> p c b t", b=nb)[:, :, :, H - 1:H]
                        r_ = r_.broadcast_to([P, NCH, nb, H])
                        V.tensor_tensor(b[:, :, :, 0:H], r_, v_[:, :, :, 0:H], ALU.subtract)
                        V.tensor_tensor(b[:, :, :, H:2 * H], v_[:, :, :, H:2 * H], r_, ALU.subtract).then_inc(g_sub, 1)

            out_lo(7, 8)
            dve.wait_ge(xa_in, 16)
            V.tensor_scalar(XA[:], XA[:], ALPHA, None, ALU.mult).then_inc(xa_done, 1)

            def zero_acc():
                V.memset(acc[:], 0.0).then_inc(acc_zero, 1)

            def residual(count, k, ps, gain, xa):
                V.scalar_tensor_tensor(out=xa, in0=ps, scalar=gain, in1=xa, op0=ALU.mult, op1=ALU.add).then_inc(r_done, 1)
                if count % 8 < 7:
                    add_up(count, k, xa)
                    sum_sq(count, k)

            def sum_sq(count, k):
                dve.wait_ge(sq_done, count + 1)
                dve.wait_ge(qs_done, count - k)
                V.tensor_tensor(acc[:, 1], acc[:, 1], tb[:, 0], ALU.add).then_inc(qs_done, 1)

            def add_up(count, k, src):
                dve.wait_ge(r_done, count + 1)
                dve.wait_ge(rs_done, count - k)
                dve.wait_ge(acc_zero, k + 1)
                V.tensor_tensor(acc[:, 0], acc[:, 0], src, ALU.add).then_inc(rs_done, 1)

            def scaled(k, dst, src, j, row, done):
                V.scalar_tensor_tensor(out=dst, in0=src, scalar=norm[:, k, row, j:j + 1], in1=rstd_of(k)[:],
                                       op0=ALU.mult, op1=ALU.mult).then_inc(done, 1)

            def ln(k, src):
                rstd = rstd_of(k)
                dve.wait_ge(ln_m2, k + 1)
                dve.wait_ge(st_sq, k + 1)
                for q in range(2):
                    r_ = rstd[:, HALF[q]]
                    V.scalar_tensor_tensor(out=r_, in0=bank[6][:, HALF[q]], scalar=LN_EPS, in1=tb[:, 3, HALF[q]],
                                           op0=ALU.add, op1=ALU.subtract).then_inc(ln_var, 1)
                    dve.wait_ge(ln_var, 2 * k + q + 1)
                    V.tensor_scalar(r_, r_, LN_EPS, None, ALU.max).then_inc(ln_v, 1)

                V.tensor_copy(tb[:, 2], bank[5][:]).then_inc(ln_mu, 1)
                dve.wait_ge(ln_mu, k + 1)
                n = 8 if k < 4 else 3

                def centre(j):
                    V.tensor_tensor(src[:, j], src[:, j], tb[:, 2], ALU.subtract).then_inc(ln_d, 1)

                centre(0)
                if k < 4:
                    dve.wait_ge(ln_rstd, 2 * k + 1)
                    dve.wait_ge(ln_d, 8 * k + 1)
                    for q in range(2):
                        dve.wait_ge(ln_rstd, 2 * k + q + 1)
                        V.scalar_tensor_tensor(out=norm_buf(0)[:, HALF[q]], in0=src[:, 0, HALF[q]],
                                               scalar=norm[:, k, 0, 0:1], in1=rstd[:, HALF[q]], op0=ALU.mult,
                                               op1=ALU.mult).then_inc(ln_t if q else ln_t0, 1)
                centre(1)
                centre(2)
                dve.wait_ge(ln_rstd, 2 * k + 2)
                for j in range(1 if k < 4 else 0, 8):
                    if j < n:
                        dve.wait_ge(ln_d, 8 * k + j + 1)
                    else:
                        dve.wait_ge(ln_d_pool, j - n + 1)
                    if k < 4:
                        if j >= 4:
                            dve.wait_ge(ln_lo, 8 * k + j - 3)
                        scaled(k, norm_buf(j), src[:, j], j, 0, ln_t)
                    else:
                        scaled(k, src[:, j], src[:, j], j, 2, ln_ax)
                    if 3 <= j + 2 < n:
                        centre(j + 2)
                if k < 4:
                    zero_acc()

            def keep(k, j0=0, j1=8):
                c0 = 8 * (0, 1, 1, 2)[k]
                dve.wait_ge(ln_t, 8 * k + 8)
                for j in range(j0, j1 + 1):
                    if j < j1:
                        scaled(k, XA[:, j], XA[:, j], j, 2, ln_ax)
                    if j > j0:
                        dve.wait_ge(ln_ax, c0 + j)
                        V.tensor_scalar(XA[:, j - 1], XA[:, j - 1], norm[:, k, 3, j - 1:j], None,
                                        ALU.add).then_inc(ln_x, 1)

            zero_acc()
            dve.wait_ge(xa_done, 1)
            for m in range(8):
                dve.wait_ge(gemm_done, N_OUT + m + 1)
                residual(m, 0, bank[m % 4][:], mod[:, 0, G1 * 8 + m:G1 * 8 + m + 1], XA[:, m])
            ln(0, XA)

            def up(layer):
                n0 = N_UP1 if layer else N_UP0

                def body(it, part=None, half=0):
                    for b in range(2):
                        k = 2 * it + b
                        if part is not None:
                            for q in range(2):
                                kc = 4 * half + 2 * b + q
                                add_block(dve, 4 * part + 16 + kc // 2, q, 1, kc, part_no=part + 4)
                        dve.wait_ge(gemm_done, 4 * it + 2 * b + n0 + 2)
                        dve.wait_ge(up_s, k + 22 * layer + 1)
                        if not isinstance(it, int):
                            dve.wait_ge(up_lo, k + 22 * layer - 1)
                        V.tensor_tensor(tb[:, 2 + b], tb[:, b], bank[2 * b + 1][:], ALU.mult).then_inc(up_a, 1)
                        dve.wait_ge(up_hi, k + 22 * layer + 1)
                        V.tensor_tensor(A_lo[:, k], tb[:, 2 + b], A_hi[:, k].bitcast(fp32),
                                        ALU.subtract).then_inc(up_lo, 1)
                        if isinstance(it, int):
                            keep(3 if layer else 0, (0, 3)[b], (3, 5)[b])

                body(0)
                keep(3 if layer else 0, 5, 8)
                if layer == 0:
                    with dve.Fori(0, 5) as it:
                        for p in range(2):
                            body(2 * it + 1 + p, it, p)
                else:
                    with dve.Fori(1, 11) as it:
                        body(it)

            def down(layer):
                k = 4 if layer else 1
                for m in range(8):
                    if layer == 0:
                        add_block(dve, 36 + m // 2, m % 2, 1, m, part_no=9)
                    dve.wait_ge(gemm_done, 3 * m + (N_DN1 if layer else N_DN0) + 3)
                    if layer == 0:
                        dve.wait_ge(ln_x, m + 1)
                    g0 = G2 * 8 + m
                    residual(8 * k + m, k, bank[m % 4][:], mod[:, layer, g0:g0 + 1], XA[:, m])

            up(0)
            mod_values(1, 0, 40, 9)
            norm_vectors(1, vcol("ln2_g"), vcol("ln2_b"), SC1, SH1, 1, extra=vcol("cv_b2"))
            norm_vectors(2, vcol("cv_ln_g"), vcol("cv_ln_b"))
            norm_vectors(3, vcol("ln1_g", 1), vcol("ln1_b", 1), SC2, SH2, 1)
            norm_vectors(4, vcol("ln2_g", 1), vcol("ln2_b", 1))
            down(0)
            V.memset(U[:, :, 0:PAD], 0.0)
            V.memset(U[:, :, PAD + T:], 0.0).then_inc(cv_pad, 1)
            ln(1, XA)
            mod_values(1, 40, 48, 10)

            def join(k, b, step):
                rc = RC[:, k]
                if step == 0:
                    ta, tb_, _, tp = taps_of(k)
                    dve.wait_ge(cv_a, TA * k + ta)
                    dve.wait_ge(cv_b, TB * k + tb_)
                    V.tensor_tensor(rc, rc, chain_b[:, b], ALU.add).then_inc(cv_join, 1)
                elif step == 1:
                    dve.wait_ge(cv_join, 2 * k + 1)
                    dve.wait_ge(cv_sum, (TP - 1) * k + taps_of(k)[3] - 1)
                    V.tensor_tensor(rc, rc, pool_sum[:, b], ALU.add).then_inc(cv_join, 1)
                elif step == 2:
                    dve.wait_ge(cv_join, 2 * k + 2)
                    dve.wait_ge(cv_mm, k + 1)
                    V.tensor_tensor(rc, rc, bank[4][:], ALU.add).then_inc(r_done, 1)
                else:
                    add_up(k + 16, 2, rc)

            def conv_body(it):
                for b in range(2):
                    k = 2 * it + b
                    dve.wait_ge(cv_pad, 1)
                    dve.wait_ge(cv_s, k + 1)
                    dve.wait_ge(gemm_done, 4 * it + 2 * b + N_CV1 + 2)
                    if not (isinstance(k, int) and k < 2):
                        dve.wait_ge(cv_mm, k - 1)
                        dve.wait_ge(cv_prod, TP * (k - 1))
                    V.scalar_tensor_tensor(out=U[:, b, PAD:PAD + T], in0=bank[2 * b][:],
                                           scalar=vec[:, bass.ds(k + VEC["cv_b1"], 1)], in1=tb[:, 2 + b], op0=ALU.add,
                                           op1=ALU.mult).then_inc(cv_u, 1)
                    dve.wait_ge(cv_u, k + 1)
                    for tap in range(sum(taps_of(k)[:2])):
                        w_ = vec[:, bass.ds(TAPS * k + VEC["cv_wdw"] + tap, 1)]
                        u_ = U[:, b, tap:tap + T]
                        i, in_b = divmod(tap, 2)
                        dst, done, n = (chain_b[:, b], cv_b, TB) if in_b else (RC[:, k], cv_a, TA)
                        if tap == 0:
                            ins = V.tensor_scalar(dst, u_, w_, vec[:, bass.ds(k + VEC["cv_bdw"], 1)], ALU.mult, ALU.add)
                        elif tap == 1:
                            ins = V.tensor_scalar(dst, u_, w_, None, ALU.mult)
                        else:
                            dve.wait_ge(done, n * k + i)
                            ins = V.scalar_tensor_tensor(out=dst, in0=u_, scalar=w_, in1=dst, op0=ALU.mult, op1=ALU.add)
                        ins.then_inc(done, 1)
                        at_ = (1, 3, 6, 8) if isinstance(k, int) and k == 7 else (2, 5, 8, 11)
                        if tap in at_ and not (isinstance(k, int) and k == 0):
                            join(k - 1, (b + 1) % 2, at_.index(tap))

            conv_body(0)
            with dve.Fori(1, 3) as it:
                conv_body(it)
            conv_body(3)
            for step in range(3):
                join(7, 1, step)
            ln(2, RC)
            keep(1)
            for m in range(8):
                dve.wait_ge(gemm_done, m + N_CV2 + 1)
                dve.wait_ge(ln_x, m + 9)
                residual(m + 24, 3, bank[m % 4][:], mod[:, 1, G1 * 8 + m:G1 * 8 + m + 1], XA[:, m])
            ln(3, XA)
            up(1)
            dve.wait_ge(ln_x, 24)
            down(1)
            ln(4, XA)


def kernel(x, c, ctx, c_ctx, w_mod, b_mod, ln1_g, ln1_b, ln2_g, ln2_b, w_in_even, w_out_even, na_rpb, hg_lb,
           hg_norm_g, cv_w1, cv_b1, cv_wdw, cv_bdw, cv_ln_g, cv_ln_b, cv_w2, cv_b2, ffn_w1, ffn_w3, ffn_w2):
    import numpy as np
    import concourse.bacc as bacc
    from concourse.bass_utils import run_bass_kernel_spmd

    def features(a, n):
        return np.ascontiguousarray(np.asarray(a).T.reshape(-1, P, n).transpose(1, 0, 2))

    def columns(a):
        return np.asarray(a).reshape(-1, P).T

    def pieces(w):
        w = np.asarray(w)
        k, n = w.shape
        return np.ascontiguousarray(w.reshape(k // P, P, n // P, P).transpose(2, 1, 0, 3)).reshape(n // P, P, k)

    def interleave(a, b):
        return np.ascontiguousarray(np.stack([a, b], 1)).reshape((-1,) + a.shape[1:])

    w_in_t = pieces(w_in_even[0]).reshape(8, 4, P, D)[list(IN_ORDER)].reshape(32, P, D)
    cv1 = pieces(cv_w1[0])
    up_ = np.stack([interleave(pieces(ffn_w1[l]), pieces(ffn_w3[l])) for l in range(2)])
    vectors = np.concatenate([columns(a) for a in (b_mod, ln1_g, ln1_b, ln2_g, ln2_b, hg_norm_g, cv_b1, cv_bdw,
                                                   cv_ln_g, cv_ln_b, cv_b2)]
                             + [np.asarray(cv_wdw[0]).reshape(TAPS, 8, P).transpose(2, 1, 0).reshape(P, 8 * TAPS)], 1)

    qr, qc = np.divmod(np.arange(P), TILE_W)
    dr = np.arange(ROWS)[None, :] - qr[:, None] + ROWS - 1
    dc = np.clip(np.arange(WIN)[None, :] - TILE_W - qc[:, None] + TILE_W - 1, 0, 2 * TILE_W - 2)
    bias_t = np.ascontiguousarray(np.asarray(na_rpb)[0][:, dr[:, :, None], dc[:, None, :]].transpose(1, 0, 2, 3))
    mask = np.zeros((P, ROWS, 3, WIN), np.float32)
    for kind, (t, lo) in enumerate(((0, 0), (1, 0), (3, 2))):
        col = t * TILE_W + qc
        start = np.clip(col - TILE_W // 2, 0, COLS - TILE_W)
        kcol = lo * TILE_W + np.arange(WIN)
        seen = (kcol[None, :] >= start[:, None]) & (kcol[None, :] < start[:, None] + TILE_W)
        mask[:, :, kind, :] = np.where(seen, 0.0, -1e30)[:, None, :]
    lvl_t = np.zeros((P, 2, 7, P), np.float32)
    a = np.arange(P)
    for e, H in enumerate(LEVELS):
        same = a[:, None] // (2 * H) == a[None, :] // (2 * H)
        first = a // H % 2 == 0
        lvl_t[:, 0, e] = same & first[:, None] & ~first[None, :]
        lvl_t[:, 1, e] = same & ~first[:, None] & first[None, :]

    arrays = {
        "xT": features(x[0], T), "ctxT": features(ctx[0], TC),
        "cvec": np.ascontiguousarray(np.stack([columns(c[0]), columns(c_ctx)], 2)),
        "vecs": np.ascontiguousarray(vectors), "ident_d": np.eye(P, dtype=np.float32), "lvl_d": lvl_t,
        "bias_d": bias_t, "mask_d": mask,
        "w_sc1": pieces(w_mod[0][:, SC1 * D:(SC1 + 1) * D]),
        "wmod": np.ascontiguousarray(np.asarray(w_mod).reshape(2, KC, P, 6, D).transpose(0, 3, 1, 2, 4))
        .reshape(12, KC, P, D),
        "w_in": w_in_t, "w_out": pieces(np.asarray(w_out_even[0]).reshape(KC, P, D)[list(OUT_ORDER)].reshape(D, D)), "w_up": up_,
        "w_dn": np.stack([pieces(ffn_w2[0]), pieces(ffn_w2[1])]),
        "cv1": interleave(cv1[:8], cv1[8:]), "cv2": pieces(cv_w2[0]),
    }
    nc = bacc.Bacc("TRN2", target_bir_lowering=False, num_devices=1)
    args = [nc.dram_tensor(f"in_{k}", v.shape, mybir.dt.from_np(v.dtype), kind="ExternalInput").ap()
            for k, v in arrays.items()]
    args.append(nc.dram_tensor("out_y", (8, P, T), mybir.dt.float32, kind="ExternalOutput").ap())
    build(nc, *args)
    r = run_bass_kernel_spmd(nc, [{f"in_{k}": v for k, v in arrays.items()}], core_ids=[0])
    y = r.results[0]["out_y"]
    return np.ascontiguousarray(np.asarray(y).reshape(D, T).T)[None]
```
